# Optimizing a Trainium2 kernel written in Bass

```python
import jax
import jax.numpy as jnp
from jax import lax
import numpy as np

D_MODEL = 1024
BATCH = 1
SEQ = 1024
DEPTH = 2

CHUNK = 64
HEAD_DIM = 64
ROT_DIM = HEAD_DIM // 4
ROPE_THETA = 500000.0
NORM_EPS = 1e-5
A_HEADS = (D_MODEL // 2) // HEAD_DIM
A_KV_HEADS = max(1, A_HEADS // 4)
WINDOW = 128
WINDOW_CHUNKS = WINDOW // CHUNK
B_HEADS = 4
B_DV = (D_MODEL // 2) // B_HEADS
B_DQK = B_DV // 2
CONV_K = 4
C_HEADS = D_MODEL // HEAD_DIM
C_KV_HEADS = max(1, C_HEADS // 4)
IDX_HEADS = 8
IDX_DIM = 64
TOPK_MAX = 256
QBLOCK = 128
D_FF = 4 * D_MODEL
N_EVEN = (DEPTH + 1) // 2
N_ODD = DEPTH // 2
EVEN_SPLITS = (A_HEADS * HEAD_DIM, A_KV_HEADS * HEAD_DIM, A_KV_HEADS * HEAD_DIM,
               2 * B_HEADS * B_DQK, B_HEADS * B_DV, B_HEADS * B_DV, B_HEADS, B_HEADS)
EVEN_IN = sum(EVEN_SPLITS)
EVEN_OUT = A_HEADS * HEAD_DIM + B_HEADS * B_DV
ODD_SPLITS = (C_HEADS * HEAD_DIM, C_KV_HEADS * HEAD_DIM, C_KV_HEADS * HEAD_DIM,
              IDX_HEADS * IDX_DIM, IDX_DIM, IDX_HEADS)
ODD_IN = sum(ODD_SPLITS)
ODD_OUT = C_HEADS * HEAD_DIM

kernel_name = "hybrid_swa_mlstm_dsa_trunk"

def rms_norm(x, g):
    xf = x.astype(jnp.float32)
    y = xf * lax.rsqrt(jnp.mean(xf * xf, axis=-1, keepdims=True) + NORM_EPS)
    return (y * g.astype(jnp.float32)).astype(x.dtype)

def split_cols(z, sizes):
    offs = [int(o) for o in np.cumsum(sizes)[:-1]]
    return jnp.split(z, offs, axis=-1)

def rope_angles(positions):
    inv_freq = ROPE_THETA ** (-jnp.arange(0, ROT_DIM, 2, dtype=jnp.float32) / ROT_DIM)
    ang = positions.astype(jnp.float32)[..., None] * inv_freq
    return jnp.cos(ang), jnp.sin(ang)

def partial_rope(t, cos, sin):
    half = ROT_DIM // 2
    c = cos[:, :, None, :]
    s = sin[:, :, None, :]
    t1 = t[..., :half].astype(jnp.float32)
    t2 = t[..., half:ROT_DIM].astype(jnp.float32)
    rot = jnp.concatenate([t1 * c - t2 * s, t2 * c + t1 * s], axis=-1).astype(t.dtype)
    return jnp.concatenate([rot, t[..., ROT_DIM:]], axis=-1)

def shift_chunks(a, lag):
    if lag == 0:
        return a
    pad = jnp.zeros_like(a[:, :lag])
    return jnp.concatenate([pad, a[:, :-lag]], axis=1)

def sliding_window_sink_attention(q, k, v, sinks):
    B, S, H, D = q.shape
    Hk = k.shape[2]
    G = H // Hk
    nC = S // CHUNK
    qb = q.reshape(B, nC, CHUNK, Hk, G, D)
    kb = k.reshape(B, nC, CHUNK, Hk, D)
    vb = v.reshape(B, nC, CHUNK, Hk, D)
    lags = list(range(WINDOW_CHUNKS - 1, -1, -1))
    kw = jnp.concatenate([shift_chunks(kb, l) for l in lags], axis=2)
    vw = jnp.concatenate([shift_chunks(vb, l) for l in lags], axis=2)
    cidx = jnp.arange(nC)
    valid = jnp.concatenate(
        [jnp.broadcast_to((cidx >= l)[:, None], (nC, CHUNK)) for l in lags], axis=1)
    logits = jnp.einsum('bcqhgd,bckhd->bchgqk', qb, kw).astype(jnp.float32) * (D ** -0.5)
    logits = jnp.where(valid[None, :, None, None, None, :], logits, -jnp.inf)
    sink = jnp.broadcast_to(sinks.astype(jnp.float32).reshape(1, 1, Hk, G, 1, 1),
                            logits.shape[:-1] + (1,))
    p = jax.nn.softmax(jnp.concatenate([logits, sink], axis=-1), axis=-1)[..., :-1]
    o = jnp.einsum('bchgqk,bckhd->bcqhgd', p.astype(v.dtype), vw)
    return o.reshape(B, S, H * D)

def causal_depthwise_conv(u, w, b):
    C = u.shape[-1]
    y = lax.conv_general_dilated(u, w[:, None, :].astype(u.dtype), window_strides=(1,),
                                 padding=[(CONV_K - 1, 0)],
                                 dimension_numbers=('NWC', 'WIO', 'NWC'),
                                 feature_group_count=C)
    return y + b

def mlstm_chunkwise(q, k, v, i_pre, f_pre):
    B, S, H, Dk = q.shape
    Dv = v.shape[-1]
    nC = S // CHUNK
    L = CHUNK
    f32 = jnp.float32

    def to_chunks(a):
        return a.astype(f32).reshape(B, nC, L, H, -1).transpose(1, 0, 3, 2, 4)

    qc = to_chunks(q)
    kc = to_chunks(k * (Dk ** -0.5))
    vc = to_chunks(v)
    log_f = jax.nn.log_sigmoid(f_pre.astype(f32)).reshape(B, nC, L, H).transpose(1, 0, 3, 2)
    log_i = i_pre.astype(f32).reshape(B, nC, L, H).transpose(1, 0, 3, 2)
    bcum = jnp.cumsum(log_f, axis=-1)
    causal = jnp.tril(jnp.ones((L, L), dtype=bool))

    def step(carry, xs):
        Cs, ns, ms = carry
        qj, kj, vj, bj, lij = xs
        dmat = bj[..., :, None] - bj[..., None, :] + lij[..., None, :]
        dmat = jnp.where(causal, dmat, -jnp.inf)
        inter = bj + ms[..., None]
        m_t = jnp.maximum(inter, jnp.max(dmat, axis=-1))
        wmat = jnp.einsum('bhld,bhsd->bhls', qj, kj) * jnp.exp(dmat - m_t[..., None])
        inter_scale = jnp.exp(inter - m_t)
        num = (jnp.einsum('bhls,bhsv->bhlv', wmat, vj)
               + inter_scale[..., None] * jnp.einsum('bhvd,bhld->bhlv', Cs, qj))
        den = jnp.sum(wmat, axis=-1) + inter_scale * jnp.einsum('bhd,bhld->bhl', ns, qj)
        h = num / jnp.maximum(jnp.abs(den), jnp.exp(-m_t))[..., None]
        b_last = bj[..., -1]
        decay = b_last[..., None] - bj + lij
        m_new = jnp.maximum(b_last + ms, jnp.max(decay, axis=-1))
        wts = jnp.exp(decay - m_new[..., None])
        sc = jnp.exp(b_last + ms - m_new)
        C_new = sc[..., None, None] * Cs + jnp.einsum('bhs,bhsv,bhsd->bhvd', wts, vj, kj)
        n_new = sc[..., None] * ns + jnp.einsum('bhs,bhsd->bhd', wts, kj)
        return (C_new, n_new, m_new), h

    init = (jnp.zeros((B, H, Dv, Dk), f32), jnp.zeros((B, H, Dk), f32), jnp.zeros((B, H), f32))
    _, hs = lax.scan(step, init, (qc, kc, vc, bcum, log_i))
    return hs.transpose(1, 0, 3, 2, 4).reshape(B, S, H * Dv).astype(v.dtype)

def dsa_attention(q, k, v, q_idx, k_idx, w_idx):
    B, S, H, D = q.shape
    Hk = k.shape[2]
    G = H // Hk
    nQ = S // QBLOCK
    top = min(TOPK_MAX, S // 4)
    key_chunk = jnp.arange(S) // CHUNK
    f32 = jnp.float32

    def blockify(a):
        return a.reshape((B, nQ, QBLOCK) + a.shape[2:]).swapaxes(0, 1)

    def one_block(args):
        qb, qib, wb, j = args
        qpos = j * QBLOCK + jnp.arange(QBLOCK)
        admissible = key_chunk[None, :] <= (qpos // CHUNK)[:, None]
        rel = jax.nn.relu(jnp.einsum('bqhd,bsd->bqhs', qib.astype(f32), k_idx.astype(f32)))
        score = jnp.einsum('bqh,bqhs->bqs', wb.astype(f32), rel)
        score = jnp.where(admissible[None], score, -jnp.inf)
        sel_score, sel = lax.top_k(score, top)
        valid = jnp.isfinite(sel_score)
        kg = jax.vmap(lambda kk, ii: kk[ii])(k, sel)
        vg = jax.vmap(lambda vv, ii: vv[ii])(v, sel)
        qg = qb.reshape(B, QBLOCK, Hk, G, D)
        logits = jnp.einsum('bqhgd,bqkhd->bqhgk', qg, kg).astype(f32) * (D ** -0.5)
        logits = jnp.where(valid[:, :, None, None, :], logits, -jnp.inf)
        p = jax.nn.softmax(logits, axis=-1).astype(v.dtype)
        o = jnp.einsum('bqhgk,bqkhd->bqhgd', p, vg)
        return o.reshape(B, QBLOCK, H * D)

    out = lax.map(one_block, (blockify(q), blockify(q_idx), blockify(w_idx), jnp.arange(nQ)))
    return out.swapaxes(0, 1).reshape(B, S, H * D)

def even_mixer(h, cos, sin, w_in, sinks, conv_w, conv_b, bias_i, bias_f, w_out):
    B, S, _ = h.shape
    z = h @ w_in
    a_q, a_k, a_v, b_qk, b_v, b_o, b_i, b_f = split_cols(z, EVEN_SPLITS)
    a_q = partial_rope(a_q.reshape(B, S, A_HEADS, HEAD_DIM), cos, sin)
    a_k = partial_rope(a_k.reshape(B, S, A_KV_HEADS, HEAD_DIM), cos, sin)
    a_v = a_v.reshape(B, S, A_KV_HEADS, HEAD_DIM)
    y_a = sliding_window_sink_attention(a_q, a_k, a_v, sinks)
    b_qk = jax.nn.silu(causal_depthwise_conv(b_qk, conv_w, conv_b))
    b_q, b_k = jnp.split(b_qk, 2, axis=-1)
    h_b = mlstm_chunkwise(b_q.reshape(B, S, B_HEADS, B_DQK), b_k.reshape(B, S, B_HEADS, B_DQK),
                          b_v.reshape(B, S, B_HEADS, B_DV), b_i + bias_i, b_f + bias_f)
    y_b = jax.nn.sigmoid(b_o) * h_b
    return jnp.concatenate([y_a, y_b], axis=-1) @ w_out

def odd_mixer(h, cos, sin, w_in, idx_k_norm, w_out):
    B, S, _ = h.shape
    z = h @ w_in
    c_q, c_k, c_v, i_q, i_k, i_w = split_cols(z, ODD_SPLITS)
    q = partial_rope(c_q.reshape(B, S, C_HEADS, HEAD_DIM), cos, sin)
    k = partial_rope(c_k.reshape(B, S, C_KV_HEADS, HEAD_DIM), cos, sin)
    v = c_v.reshape(B, S, C_KV_HEADS, HEAD_DIM)
    iq = partial_rope(i_q.reshape(B, S, IDX_HEADS, IDX_DIM), cos, sin) * (IDX_DIM ** -0.5)
    ik = partial_rope(rms_norm(i_k, idx_k_norm)[:, :, None, :], cos, sin)[:, :, 0, :]
    iw = i_w * (IDX_HEADS ** -0.5)
    return dsa_attention(q, k, v, iq, ik, iw) @ w_out

def squared_relu_mlp(h, w_up, w_down):
    return jnp.square(jax.nn.relu(h @ w_up)) @ w_down

def setup_inputs(seed: int = 0) -> dict:
    key = jax.random.key(seed)
    ks = jax.random.split(key, 20)

    def nrm(k, shape, scale):
        return jax.random.normal(k, shape, jnp.float32) * scale

    x = nrm(ks[0], (BATCH, SEQ, D_MODEL), 1.0)
    pos0 = jax.random.randint(ks[1], (BATCH, 1), 0, 64, dtype=jnp.int32) * CHUNK
    positions = (pos0 + jnp.arange(SEQ, dtype=jnp.int32)[None, :]).astype(jnp.int32)
    norm_mix = 1.0 + nrm(ks[2], (DEPTH, D_MODEL), 0.05)
    even_w_in = nrm(ks[3], (N_EVEN, D_MODEL, EVEN_IN), D_MODEL ** -0.5)
    even_sinks = nrm(ks[4], (N_EVEN, A_HEADS), 0.5)
    even_conv_w = nrm(ks[5], (N_EVEN, CONV_K, 2 * B_HEADS * B_DQK), CONV_K ** -0.5)
    even_conv_b = nrm(ks[6], (N_EVEN, 2 * B_HEADS * B_DQK), 0.02)
    even_bias_i = nrm(ks[7], (N_EVEN, B_HEADS), 0.1)
    even_bias_f = (jnp.broadcast_to(jnp.linspace(3.0, 6.0, B_HEADS, dtype=jnp.float32), (N_EVEN, B_HEADS))
                   + nrm(ks[8], (N_EVEN, B_HEADS), 0.1))
    even_w_out = nrm(ks[9], (N_EVEN, EVEN_OUT, D_MODEL), EVEN_OUT ** -0.5)
    odd_w_in = nrm(ks[10], (N_ODD, D_MODEL, ODD_IN), D_MODEL ** -0.5)
    odd_idx_k_norm = 1.0 + nrm(ks[11], (N_ODD, IDX_DIM), 0.05)
    odd_w_out = nrm(ks[12], (N_ODD, ODD_OUT, D_MODEL), ODD_OUT ** -0.5)
    norm_mlp = 1.0 + nrm(ks[13], (DEPTH, D_MODEL), 0.05)
    w_up = nrm(ks[14], (DEPTH, D_MODEL, D_FF), D_MODEL ** -0.5)
    w_down = nrm(ks[15], (DEPTH, D_FF, D_MODEL), D_FF ** -0.5)
    final_norm = 1.0 + nrm(ks[16], (D_MODEL,), 0.05)
    return {"x": x, "positions": positions, "norm_mix": norm_mix,
            "even_w_in": even_w_in, "even_sinks": even_sinks, "even_conv_w": even_conv_w,
            "even_conv_b": even_conv_b, "even_bias_i": even_bias_i, "even_bias_f": even_bias_f,
            "even_w_out": even_w_out, "odd_w_in": odd_w_in, "odd_idx_k_norm": odd_idx_k_norm,
            "odd_w_out": odd_w_out, "norm_mlp": norm_mlp, "w_up": w_up, "w_down": w_down,
            "final_norm": final_norm}

def reference(x, positions, norm_mix, even_w_in, even_sinks, even_conv_w, even_conv_b,
              even_bias_i, even_bias_f, even_w_out, odd_w_in, odd_idx_k_norm, odd_w_out,
              norm_mlp, w_up, w_down, final_norm):
    cos, sin = rope_angles(positions)
    for layer in range(DEPTH):
        j = layer // 2
        h = rms_norm(x, norm_mix[layer])
        if layer % 2 == 0:
            x = x + even_mixer(h, cos, sin, even_w_in[j], even_sinks[j], even_conv_w[j],
                               even_conv_b[j], even_bias_i[j], even_bias_f[j], even_w_out[j])
        else:
            x = x + odd_mixer(h, cos, sin, odd_w_in[j], odd_idx_k_norm[j], odd_w_out[j])
        x = x + squared_relu_mlp(rms_norm(x, norm_mlp[layer]), w_up[layer], w_down[layer])
    return rms_norm(x, final_norm)


_drawn_inputs = setup_inputs


def setup_inputs(seed=0):
    import zlib

    import numpy as np

    out = dict(_drawn_inputs(seed))
    spreads = {}
    factors = {'even_sinks': 8.0, 'even_bias_i': 8.0, 'odd_idx_k_norm': 35.907, 'even_conv_b': 3.637}
    for name, (base, spread) in spreads.items():
        noise = np.random.default_rng([zlib.crc32(name.encode()), seed]).standard_normal(out[name].shape)
        drawn = base * np.exp(spread * noise) if base else spread * noise
        out[name] = jnp.asarray(drawn.astype(out[name].dtype))
    for name, factor in factors.items():
        out[name] = (out[name] * factor).astype(out[name].dtype)
    return out
```

```python
from contextlib import ExitStack

import numpy as np

import concourse.bass as bass
from concourse import mybir

F32 = mybir.dt.float32
F32R = mybir.dt.float32r
BF16 = mybir.dt.bfloat16
I32 = mybir.dt.int32
ALU = mybir.AluOpType
ACT = mybir.ActivationFunctionType
AX = mybir.AxisListType

P = 128
D = 1024
SEQ = 1024
KC = D // P
RT = SEQ // P
CHUNK = 64
HD = 64
ROT = HD // 4
NF = ROT // 2
THETA = 500000.0
EPS = 1e-5
A_HEADS, A_KV = 8, 2
B_HEADS, B_DV, B_DK, CONV = 4, 128, 64, 4
C_HEADS, C_KV = 16, 4
IH = 8
TOPK = 256
D_FF = 4096
FC = D_FF // P
NB = 512
EVEN_IN, ODD_IN = 2312, 2120
ZW = EVEN_IN
EQ, EK, EV, EBQK, EBV, EBO, EBI, EBF = 0, 512, 640, 768, 1280, 1792, 2304, 2308
OQ, OK_, OV, OIQ, OIK, OIW = 0, 1024, 1280, 1536, 2048, 2112

KB = 1024
BASE = 16 * KB + 128


class Map:
    X = 0
    Z = 32 * KB
    T = Z + RT * ZW * 4
    W = T + 64 * KB
    SMALL = W + 36 * KB


class Mem:

    def __init__(self, nc, start, end):
        self.nc, self.at, self.end = nc, BASE + start, BASE + end

    def take(self, name, shape, dt):
        size = int(np.prod(shape[1:])) * (2 if dt == BF16 else 4)
        assert self.at + size <= self.end, (name, self.at + size - self.end)
        t = self.nc.alloc_sbuf_tensor_at(name, shape, dt, offset=self.at)
        self.at += (size + 31) // 32 * 32
        return t


def new_sem(nc, env, name):
    s = nc.alloc_semaphore(name)
    env["sems"].append(s)
    return s


def reset_semaphores(nc, env):
    nc.clear_and_free_semaphores(env["sems"])
    nc.all_engine_barrier()
    env["sems"] = []


def f32(ap):
    return ap.bitcast(F32)


def newton_rstd(nc, dve, st, ss, scale, sums, summed, var, root, rstd):
    dve.wait_ge(sums, summed)
    nc.vector.tensor_scalar(st[:, 0, :], ss, scale, EPS, ALU.mult, ALU.add).then_inc(var, 1)
    dve.wait_ge(root, 1)
    nc.vector.reciprocal(st[:, 2, :], st[:, 1, :]).then_inc(rstd, 1)
    dve.wait_ge(rstd, 1)
    nc.vector.tensor_tensor(st[:, 3, :], st[:, 2, :], st[:, 2, :], ALU.mult).then_inc(rstd, 1)
    dve.wait_ge(rstd, 2)
    nc.vector.tensor_tensor(st[:, 1, :], st[:, 3, :], st[:, 0, :], ALU.mult).then_inc(rstd, 1)
    dve.wait_ge(rstd, 3)
    nc.vector.tensor_scalar(st[:, 3, :], st[:, 1, :], -0.5, 1.5, ALU.mult, ALU.add).then_inc(rstd, 1)
    dve.wait_ge(rstd, 4)
    nc.vector.tensor_tensor(st[:, 2, :], st[:, 2, :], st[:, 3, :], ALU.mult).then_inc(rstd, 1)
    dve.wait_ge(rstd, 5)


def norm_transpose(nc, env, tag, g_dram, load_x=None, src=None):
    X, Thi, Tlo, ident = env["X"], env["Thi"], env["Tlo"], env["ident"]
    with ExitStack() as ctx:
        def sem(n):
            return new_sem(nc, env, f"{tag}_{n}")

        if src is None:
            mem = Mem(nc, Map.Z, Map.T)
            xn = mem.take(f"{tag}_xn", [P, 4, D], F32)
            junk = mem.take(f"{tag}_junk", [P, RT, D], F32)
            g = mem.take(f"{tag}_g", [P, KC], F32)
            ss = mem.take(f"{tag}_ss", [P, RT], F32)
            st = mem.take(f"{tag}_st", [P, 4, RT], F32)
        ps = [ctx.enter_context(nc.psum_tensor(f"{tag}_ps{i}", [P, NB], F32)) for i in range(4)]
        x_in, g_in, sums, var, root, rstd, xn_ready = map(sem, ("x_in", "g_in", "sums", "var", "root", "rstd", "xn_ready"))
        turned, hi_done, lo_done = map(sem, ("turned", "hi_done", "lo_done"))
        banks = [(half, k) for half in range(2) for k in range(KC)]
        block = ctx.enter_context(nc.Block())

        @block.sync
        def _(sp):
            if src is None:
                if load_x is not None:
                    for r in range(RT):
                        sp.dma_start(X[:, r, :], load_x[r * P:(r + 1) * P, :]).then_inc(x_in, 16)
                sp.dma_start(g[:, :], g_dram.rearrange("(k p) -> p k", p=P), allow_slow_non_contiguous=True).then_inc(g_in, 16)

        @block.vector
        def _(dve):
            if src is None:
                for r in range(1, RT, 2):
                    if load_x is not None:
                        dve.wait_ge(x_in, 16 * RT)
                    nc.vector.tensor_tensor_reduce(junk[:, r, :], X[:, r, :], X[:, r, :], 1.0, 0.0, ALU.mult,
                                                   ALU.add, ss[:, r:r + 1]).then_inc(sums, 1)
                newton_rstd(nc, dve, st, ss[:, :], 1.0 / D, sums, RT, var, root, rstd)
                dve.wait_ge(g_in, 16)
            for n, (half, k) in enumerate(banks):
                if src is None and k == 0:
                    if half:
                        dve.wait_ge(turned, KC)
                    for r in range(4):
                        nc.vector.tensor_scalar(xn[:, r, :], X[:, 4 * half + r, :], st[:, 2, 4 * half + r:4 * half + r + 1],
                                                None, ALU.mult).then_inc(xn_ready, 1)
                dve.wait_ge(hi_done, n + 1)
                lo, hi = Tlo[:, k, half * NB:(half + 1) * NB], f32(Thi[:, k, half * NB:(half + 1) * NB])
                if src is None:
                    nc.vector.scalar_tensor_tensor(lo, ps[n % 4][:, :], g[:, k:k + 1], hi, ALU.mult,
                                                   ALU.subtract).then_inc(lo_done, 1)
                else:
                    nc.vector.tensor_tensor(lo, ps[n % 4][:, :], hi, ALU.subtract).then_inc(lo_done, 1)

        @block.scalar
        def _(act):
            if src is None:
                for r in range(0, RT, 2):
                    if load_x is not None:
                        act.wait_ge(x_in, 16 * RT)
                    nc.scalar.activation(junk[:, r, :], X[:, r, :], ACT.Square, accum_out=ss[:, r:r + 1]).then_inc(sums, 1)
                act.wait_ge(var, 1)
                nc.scalar.activation(st[:, 1, :], st[:, 0, :], ACT.Sqrt).then_inc(root, 1)
                act.wait_ge(g_in, 16)
            for n, (half, k) in enumerate(banks):
                act.wait_ge(turned, n + 1)
                hi = Thi[:, k, half * NB:(half + 1) * NB]
                if src is None:
                    nc.scalar.activation(hi, ps[n % 4][:, :], ACT.Copy, scale=g[:, k:k + 1]).then_inc(hi_done, 1)
                else:
                    nc.scalar.activation(hi, ps[n % 4][:, :], ACT.Copy).then_inc(hi_done, 1)

        @block.tensor
        def _(pe):
            for n, (half, k) in enumerate(banks):
                if src is None and k == 0:
                    pe.wait_ge(xn_ready, 4 * half + 4)
                if n >= 4:
                    pe.wait_ge(lo_done, n - 3)
                for r in range(4):
                    rows = xn[:, r, k * P:(k + 1) * P] if src is None else src(4 * half + r, k)
                    last = nc.tensor.transpose(ps[n % 4][:, r * P:(r + 1) * P], rows, ident[:, :])
                last.then_inc(turned, 1)


def constants(nc, env):
    with ExitStack() as ctx:
        made = new_sem(nc, env, "const_made")
        ident = env["ident"]
        block = ctx.enter_context(nc.Block())

        @block.gpsimd
        def _(pool):
            nc.gpsimd.memset(ident[:, :], 0.0).then_inc(made, 1)
            pool.wait_ge(made, 1)
            nc.gpsimd.affine_select(out=ident[:, :], in_=ident[:, :], compare_op=ALU.not_equal, fill=1.0, base=0,
                                    pattern=[[-1, P]], channel_multiplier=1).then_inc(made, 1)
            pool.wait_ge(made, 2)
            nc.gpsimd.tensor_copy(env["identb"][:, :], ident[:, :]).then_inc(made, 1)


def project(nc, env, tag, w, width, dest, add=False):
    Thi, Tlo = env["Thi"], env["Tlo"]
    full, tail = divmod(width, NB)
    RAW, RING, LEAD = 4, 4, 3
    with ExitStack() as ctx:
        def sem(n):
            return new_sem(nc, env, f"{tag}_{n}")

        mem = Mem(nc, Map.W, Map.SMALL)
        raw = mem.take(f"{tag}_raw", [P, RAW, NB], F32)
        whi = mem.take(f"{tag}_whi", [P, RING, NB], F32R)
        wlo = mem.take(f"{tag}_wlo", [P, RING, NB], F32R)
        ps = [ctx.enter_context(nc.psum_tensor(f"{tag}_ps{i}", [P, NB], F32)) for i in range(RT)]
        w_in = [sem(f"w_in{i}") for i in range(RAW)]
        hi_done, lo_done, used, summed, out_act, out_dve = map(
            sem, ("hi_done", "lo_done", "used", "summed", "out_act", "out_dve"))
        block = ctx.enter_context(nc.Block())

        widths = [NB] * full + ([tail] if tail else [])

        def blocks(eng, step):
            step(0, widths[0], widths[1])
            if full > 3:
                with eng.Fori(1, full - 1) as b:
                    step(b, NB, NB)
                rest = range(full - 1, len(widths))
            else:
                rest = range(1, len(widths))
            for b in rest:
                step(b, widths[b], widths[b + 1] if b + 1 < len(widths) else 0)

        def chunks(split, b, n, after):
            if isinstance(b, int) and b == 0:
                for k in range(LEAD):
                    split(b, k, n)
            for k in range(LEAD, KC):
                split(b, k, n)
            if after:
                for k in range(LEAD):
                    split(b + 1, k, after)

        @block.sync
        def _(sp):
            def step(b, n, after):
                for k in range(KC):
                    if not (isinstance(b, int) and b == 0 and k < RAW):
                        sp.wait_ge(lo_done, KC * b + k - RAW + 1)
                    sp.dma_start(raw[:, k % RAW, 0:n], w[k * P:(k + 1) * P, bass.ds(b * NB, n)]).then_inc(w_in[k % RAW], 16)
            blocks(sp, step)

        @block.scalar
        def _(act):
            def split(b, k, n):
                act.wait_ge(w_in[k % RAW], (b * (KC // RAW) + k // RAW + 1) * 16)
                if k >= RING:
                    act.wait_ge(used, (KC - 1) * b + k - RING + 1)
                elif not (isinstance(b, int) and b == 0):
                    if k < RING - 1:
                        act.wait_ge(used, (KC - 1) * (b - 1) + KC + k - RING + 1)
                    else:
                        act.wait_ge(summed, RT * b)
                nc.scalar.activation(whi[:, k % RING, 0:n], raw[:, k % RAW, 0:n], ACT.Copy).then_inc(hi_done, 1)

            def step(b, n, after):
                chunks(split, b, n, after)
                if add:
                    return
                for r in range(0, RT, 2):
                    act.wait_ge(summed, RT * b + r + 1)
                    nc.scalar.activation(dest[:, r, bass.ds(b * NB, n)], ps[r][:, 0:n], ACT.Copy).then_inc(out_act, 1)
            blocks(act, step)

        @block.vector
        def _(dve):
            def split(b, k, n):
                dve.wait_ge(hi_done, KC * b + k + 1)
                nc.vector.tensor_tensor(wlo[:, k % RING, 0:n], raw[:, k % RAW, 0:n], f32(whi[:, k % RING, 0:n]),
                                        ALU.subtract).then_inc(lo_done, 1)

            def step(b, n, after):
                chunks(split, b, n, after)
                for r in range(0 if add else 1, RT, 1 if add else 2):
                    dve.wait_ge(summed, RT * b + r + 1)
                    to = dest[:, r, bass.ds(b * NB, n)]
                    if add:
                        nc.vector.tensor_tensor(to, ps[r][:, 0:n], to, ALU.add).then_inc(out_dve, 1)
                    else:
                        nc.vector.tensor_copy(to, ps[r][:, 0:n]).then_inc(out_dve, 1)
            blocks(dve, step)

        @block.tensor
        def _(pe):
            def step(b, n, after):
                for k in range(KC):
                    pe.wait_ge(lo_done, KC * b + k + 1)
                    hi, lo = whi[:, k % RING, 0:n], wlo[:, k % RING, 0:n]
                    for r in range(RT):
                        if k == 0 and not (isinstance(b, int) and b == 0):
                            if add:
                                pe.wait_ge(out_dve, RT * (b - 1) + r + 1)
                            else:
                                pe.wait_ge(out_dve if r % 2 else out_act, RT // 2 * (b - 1) + r // 2 + 1)
                        rows = slice(r * P, (r + 1) * P)
                        nc.tensor.matmul(ps[r][:, 0:n], Thi[:, k, rows], hi, start=(k == 0), stop=False)
                        nc.tensor.matmul(ps[r][:, 0:n], Thi[:, k, rows], lo, start=False, stop=False)
                        last = nc.tensor.matmul(ps[r][:, 0:n], Tlo[:, k, rows], hi, start=False, stop=(k == KC - 1))
                        if k == KC - 1:
                            last.then_inc(summed, 1)
                        elif r == RT - 1:
                            last.then_inc(used, 1)
            blocks(pe, step)


def mlp(nc, env, tag, w_up, w_down):
    X, Thi, Tlo = env["X"], env["Thi"], env["Tlo"]
    NBLK = FC // 2
    HEAD, BODY = 3, 6
    with ExitStack() as ctx:
        def sem(n):
            return new_sem(nc, env, f"{tag}_{n}")

        mem = Mem(nc, Map.Z, Map.T)
        uhi = mem.take(f"{tag}_uhi", [P, 4, SEQ], F32R)
        ulo = mem.take(f"{tag}_ulo", [P, 4, SEQ], F32R)
        dhi = mem.take(f"{tag}_dhi", [P, 4, D], F32R)
        dlo = mem.take(f"{tag}_dlo", [P, 4, D], F32R)
        relu = mem.take(f"{tag}_relu", [P, 4, NB], F32)
        mem = Mem(nc, Map.W, Map.SMALL)
        raw = mem.take(f"{tag}_raw", [P, 4, D], F32)
        phi = mem.take(f"{tag}_phi", [P, 2, D], F32R)
        plo = mem.take(f"{tag}_plo", [P, 2, D], F32R)
        psu = [ctx.enter_context(nc.psum_tensor(f"{tag}_psu{i}", [P, NB], F32)) for i in range(4)]
        psd = [ctx.enter_context(nc.psum_tensor(f"{tag}_psd{i}", [P, NB], F32)) for i in range(4)]
        up_in = [sem(f"up_in{i}") for i in range(2)]
        down_in = [sem(f"down_in{i}") for i in range(2)]
        up_hi, up_lo, down_hi, down_lo = map(sem, ("up_hi", "up_lo", "down_hi", "down_lo"))
        up_sum, relu_done, square, u_hi, u_lo, down_sum, added = map(
            sem, ("up_sum", "relu_done", "square", "u_hi", "u_lo", "down_sum", "added"))
        block = ctx.enter_context(nc.Block())
        up_v = w_up.rearrange("(k p) f -> p k f", p=P)

        def first(b, count=1):
            return isinstance(b, int) and b < count

        def blocks(eng, step):
            for b in range(HEAD):
                step(b, b % 2)
            with eng.Fori(0, BODY) as j:
                step(2 * j + HEAD, HEAD % 2)
                step(2 * j + HEAD + 1, (HEAD + 1) % 2)
            for b in range(HEAD + 2 * BODY, NBLK):
                step(b, b % 2)

        @block.sync
        def _(sp):
            def step(b, s):
                for c in range(2):
                    if not first(b):
                        sp.wait_ge(up_lo, 2 * b - 1 + c)
                    sp.dma_start(raw[:, c, :].rearrange("p (k f) -> p k f", k=KC),
                                 up_v[:, :, bass.ds((2 * b + c) * P, P)]).then_inc(up_in[c], 16)
                for c in range(2):
                    if not first(b):
                        sp.wait_ge(down_lo, 2 * b - 1 + c)
                    sp.dma_start(raw[:, 2 + c, :], w_down[bass.ds((2 * b + c) * P, P), :]).then_inc(down_in[c], 16)
            blocks(sp, step)

        @block.scalar
        def _(act):
            def split_up(b, c):
                act.wait_ge(up_in[c], 16 * (b + 1))
                if not first(b):
                    act.wait_ge(up_sum, 4 * b - 2 + 2 * c)
                nc.scalar.activation(phi[:, c, :], raw[:, c, :], ACT.Copy).then_inc(up_hi, 1)

            def step(b, s):
                if first(b):
                    split_up(b, 0)
                    split_up(b, 1)
                for n in range(4):
                    c, half = divmod(n, 2)
                    act.wait_ge(up_sum, 4 * b + n + 1)
                    if not first(b):
                        act.wait_ge(u_lo, 4 * b + n - 3)
                    nc.scalar.activation(relu[:, n, :], psu[n][:, :], ACT.Relu).then_inc(relu_done, 1)
                    if half:
                        if not (isinstance(b, int) and b == NBLK - 1):
                            split_up(b + 1, c)
                    act.wait_ge(square, 4 * b + n + 1)
                    if n == 0 and not first(b, 2):
                        act.wait_ge(down_sum, 16 * (b - 1))
                    nc.scalar.activation(uhi[:, 2 * s + c, half * NB:(half + 1) * NB], relu[:, n, :],
                                         ACT.Copy).then_inc(u_hi, 1)
                for c in range(2):
                    act.wait_ge(down_in[c], 16 * (b + 1))
                    nc.scalar.activation(dhi[:, 2 * s + c, :], raw[:, 2 + c, :], ACT.Copy).then_inc(down_hi, 1)
            blocks(act, step)

        @block.vector
        def _(dve):
            def split_up(b, c):
                dve.wait_ge(up_hi, 2 * b + c + 1)
                nc.vector.tensor_tensor(plo[:, c, :], raw[:, c, :], f32(phi[:, c, :]), ALU.subtract).then_inc(up_lo, 1)

            def add_down(b, first_group, count):
                for n in range(first_group, first_group + count):
                    r, half = divmod(n, 2)
                    dve.wait_ge(down_sum, 16 * b + n + 1)
                    to = X[:, r, half * NB:(half + 1) * NB]
                    nc.vector.tensor_tensor(to, psd[n % 4][:, :], to, ALU.add).then_inc(added, 1)

            def step(b, s):
                if first(b):
                    split_up(b, 0)
                    split_up(b, 1)
                for n in range(4):
                    c, half = divmod(n, 2)
                    dve.wait_ge(relu_done, 4 * b + n + 1)
                    nc.vector.tensor_tensor(relu[:, n, :], relu[:, n, :], relu[:, n, :], ALU.mult).then_inc(square, 1)
                    dve.wait_ge(u_hi, 4 * b + n + 1)
                    part = slice(half * NB, (half + 1) * NB)
                    nc.vector.tensor_tensor(ulo[:, 2 * s + c, part], relu[:, n, :], f32(uhi[:, 2 * s + c, part]),
                                            ALU.subtract).then_inc(u_lo, 1)
                    if half and not (isinstance(b, int) and b == NBLK - 1):
                        split_up(b + 1, c)
                for c in range(2):
                    dve.wait_ge(down_hi, 2 * b + c + 1)
                    nc.vector.tensor_tensor(dlo[:, 2 * s + c, :], raw[:, 2 + c, :], f32(dhi[:, 2 * s + c, :]),
                                            ALU.subtract).then_inc(down_lo, 1)
                if not first(b):
                    add_down(b - 1, 0, 16)
            blocks(dve, step)
            add_down(NBLK - 1, 0, 16)

        @block.tensor
        def _(pe):
            def up(b, s):
                for c in range(2):
                    pe.wait_ge(up_lo, 2 * b + c + 1)
                    for half in range(2):
                        n = 2 * c + half
                        if not first(b):
                            pe.wait_ge(relu_done, 4 * b + n - 3)
                        cols = slice(half * NB, (half + 1) * NB)
                        for k in range(KC):
                            hi, lo = phi[:, c, k * P:(k + 1) * P], plo[:, c, k * P:(k + 1) * P]
                            nc.tensor.matmul(psu[n][:, :], hi, Thi[:, k, cols], start=(k == 0), stop=False)
                            nc.tensor.matmul(psu[n][:, :], hi, Tlo[:, k, cols], start=False, stop=False)
                            last = nc.tensor.matmul(psu[n][:, :], lo, Thi[:, k, cols], start=False, stop=(k == KC - 1))
                        last.then_inc(up_sum, 1)

            def down(b, s):
                pe.wait_ge(u_lo, 4 * b + 4)
                pe.wait_ge(down_lo, 2 * b + 2)
                for n in range(16):
                    r, half = divmod(n, 2)
                    if not (first(b) and n < 4):
                        pe.wait_ge(added, 16 * b + n - 3)
                    rows, cols = slice(r * P, (r + 1) * P), slice(half * NB, (half + 1) * NB)
                    for c in range(2):
                        q = 2 * s + c
                        nc.tensor.matmul(psd[n % 4][:, :], uhi[:, q, rows], dhi[:, q, cols], start=(c == 0), stop=False)
                        nc.tensor.matmul(psd[n % 4][:, :], uhi[:, q, rows], dlo[:, q, cols], start=False, stop=False)
                        last = nc.tensor.matmul(psd[n % 4][:, :], ulo[:, q, rows], dhi[:, q, cols], start=False, stop=(c == 1))
                    last.then_inc(down_sum, 1)

            def step(b, s):
                up(b, s)
                if not first(b):
                    down(b - 1, 1 - s)
            blocks(pe, step)
            down(NBLK - 1, (NBLK - 1) % 2)


def final_norm(nc, env, g_dram, out):
    X = env["X"]
    with ExitStack() as ctx:
        def sem(n):
            return new_sem(nc, env, f"final_{n}")

        mem = Mem(nc, Map.Z, Map.W)
        y = mem.take("final_y", [P, RT, D], F32)
        g = mem.take("final_g", [P, D], F32)
        ss = mem.take("final_ss", [P, RT], F32)
        st = mem.take("final_st", [P, 4, RT], F32)
        g_in, sums, var, root, rstd, y_done, y_out = map(sem, ("g_in", "sums", "var", "root", "rstd", "y_done", "y_out"))
        block = ctx.enter_context(nc.Block())

        @block.sync
        def _(sp):
            sp.dma_start(g[:, :], g_dram.rearrange("(a d) -> a d", a=1).broadcast_to([P, D])).then_inc(g_in, 16)
            for r in range(RT):
                sp.wait_ge(y_done, r + 1)
                sp.dma_start(out[r * P:(r + 1) * P, :], y[:, r, :]).then_inc(y_out, 16)
            sp.wait_ge(y_out, 16 * RT)

        @block.scalar
        def _(act):
            for r in range(0, RT, 2):
                nc.scalar.activation(y[:, r, :], X[:, r, :], ACT.Square, accum_out=ss[:, r:r + 1]).then_inc(sums, 1)
            act.wait_ge(var, 1)
            nc.scalar.activation(st[:, 1, :], st[:, 0, :], ACT.Sqrt).then_inc(root, 1)

        @block.vector
        def _(dve):
            for r in range(1, RT, 2):
                nc.vector.tensor_tensor_reduce(y[:, r, :], X[:, r, :], X[:, r, :], 1.0, 0.0, ALU.mult,
                                               ALU.add, ss[:, r:r + 1]).then_inc(sums, 1)
            newton_rstd(nc, dve, st, ss[:, :], 1.0 / D, sums, RT, var, root, rstd)
            dve.wait_ge(g_in, 16)
            for r in range(RT):
                nc.vector.scalar_tensor_tensor(y[:, r, :], X[:, r, :], st[:, 2, r:r + 1], g[:, :], ALU.mult,
                                               ALU.mult).then_inc(y_done, 1)



def spread(ap, shape):
    return ap.broadcast_to(shape)


def rotary_tables(nc, env, positions):
    cos, sin = env["cos"], env["sin"]
    freq = [float(np.float32(THETA ** (-2.0 * i / ROT))) for i in range(NF)]
    two_pi = 2.0 * np.pi
    c1 = 6.28125
    c2 = round((two_pi - c1) * 2 ** 17) / 2.0 ** 17
    c3 = float(np.float32(two_pi - c1 - c2))
    to_int = 1.5 * 2 ** 23
    lim = float(np.nextafter(np.float32(np.pi), np.float32(0)))
    with ExitStack() as ctx:
        mem = Mem(nc, Map.W, Map.SMALL)
        pos_i = mem.take("rot_pos_i", [P, RT], I32)
        pos = mem.take("rot_pos", [P, RT], F32)
        ang, mult, r, arg = (mem.take(f"rot_{n}", [P, RT, NF], F32) for n in ("ang", "mult", "r", "arg"))
        pos_in, made, r_done, arg_done, tables = (new_sem(nc, env, f"rot_{n}") for n in (
            "pos_in", "made", "r_done", "arg_done", "tables"))
        block = ctx.enter_context(nc.Block())

        @block.sync
        def _(sp):
            sp.dma_start(pos_i[:, :], positions.rearrange("(r p) -> p r", p=P),
                         allow_slow_non_contiguous=True).then_inc(pos_in, 16)

        @block.vector
        def _(dve):
            dve.wait_ge(pos_in, 16)
            nc.vector.tensor_copy(pos[:, :], pos_i[:, :]).then_inc(made, 1)
            dve.wait_ge(made, 1)
            for f in range(NF):
                nc.vector.tensor_scalar(ang[:, :, f], pos[:, :], freq[f], None, ALU.mult).then_inc(made, 1)
            dve.wait_ge(made, 1 + NF)
            nc.vector.tensor_scalar(mult[:, :, :], ang[:, :, :], 1.0 / two_pi, to_int, ALU.mult, ALU.add).then_inc(made, 1)
            dve.wait_ge(made, 2 + NF)
            nc.vector.tensor_scalar(mult[:, :, :], mult[:, :, :], to_int, None, ALU.subtract).then_inc(made, 1)
            for n, c in enumerate((c1, c2, c3)):
                dve.wait_ge(made, 3 + NF + n)
                nc.vector.scalar_tensor_tensor(r[:, :, :], mult[:, :, :], -c, (r if n else ang)[:, :, :], ALU.mult,
                                               ALU.add).then_inc(made, 1)
            dve.wait_ge(made, 6 + NF)
            nc.vector.tensor_scalar(r[:, :, :], r[:, :, :], lim, -lim, ALU.min, ALU.max).then_inc(r_done, 1)
            dve.wait_ge(r_done, 1)
            nc.vector.scalar_tensor_tensor(arg[:, :, :], r[:, :, :], -1.0, r[:, :, :], ALU.mult, ALU.min).then_inc(made, 1)
            dve.wait_ge(made, 7 + NF)
            nc.vector.tensor_scalar(arg[:, :, :], arg[:, :, :], float(np.pi / 2), None, ALU.add).then_inc(arg_done, 1)

        @block.scalar
        def _(act):
            act.wait_ge(r_done, 1)
            nc.scalar.activation(sin[:, :, :], r[:, :, :], ACT.Sin).then_inc(tables, 1)
            act.wait_ge(arg_done, 1)
            nc.scalar.activation(cos[:, :, :], arg[:, :, :], ACT.Sin).then_inc(tables, 1)


def rotate(nc, eng, env, z, col, heads, tmp, done, base):
    for r in range(RT):
        v = z[:, r, col:col + heads * HD].rearrange("p (h d) -> p h d", d=HD)
        t1, t2 = v[:, :, 0:NF], v[:, :, NF:ROT]
        c = spread(env["cos"][:, r, :].unsqueeze(1), [P, heads, NF])
        s = spread(env["sin"][:, r, :].unsqueeze(1), [P, heads, NF])
        q = [tmp[:, 4 * r + n, 0:heads * NF].rearrange("p (h f) -> p h f", f=NF) for n in range(4)]
        for n, (a, b) in enumerate(((t1, c), (t2, s), (t2, c), (t1, s))):
            eng.tensor_tensor(q[n], a, b, ALU.mult).then_inc(done, 1)
    eng.wait_ge(done, base + 4 * RT)
    for r in range(RT):
        v = z[:, r, col:col + heads * HD].rearrange("p (h d) -> p h d", d=HD)
        q = [tmp[:, 4 * r + n, 0:heads * NF].rearrange("p (h f) -> p h f", f=NF) for n in range(4)]
        eng.tensor_tensor(v[:, :, 0:NF], q[0], q[1], ALU.subtract).then_inc(done, 1)
        eng.tensor_tensor(v[:, :, NF:ROT], q[2], q[3], ALU.add).then_inc(done, 1)
    return base + 6 * RT


def window_attention(nc, env, sinks):
    Z, ident = env["Z"], env["ident"]
    KW = CHUNK + SEQ
    with ExitStack() as ctx:
        def sem(n):
            return new_sem(nc, env, f"wa_{n}")

        mem = Mem(nc, Map.T, Map.SMALL)
        tmp = mem.take("wa_tmp", [P, 4 * RT, 10 * NF], F32)
        kdup = mem.take("wa_kdup", [P, RT, A_KV, 2, HD], F32)
        kT = mem.take("wa_kT", [P, A_KV, KW], F32)
        vs = mem.take("wa_vs", [P, RT, P], F32)
        qT = mem.take("wa_qT", [P, 2, 4, P], F32)
        prob = mem.take("wa_prob", [P, 2, 2, 4, P], F32)
        probT = mem.take("wa_probT", [P, 2, 8, P], F32)
        sink = mem.take("wa_sink", [P, A_HEADS], F32)
        mx = mem.take("wa_mx", [P, RT, 2, 4], F32)
        esink = mem.take("wa_esink", [P, RT, 2, 4], F32)
        den = mem.take("wa_den", [P, RT, 2, 4], F32)
        ps_s = [ctx.enter_context(nc.psum_tensor(f"wa_ps_s{i}", [P, 4, P], F32)) for i in range(2)]
        ps_t = [ctx.enter_context(nc.psum_tensor(f"wa_ps_t{i}", [P, 4, P], F32)) for i in range(2)]
        ps_q = [ctx.enter_context(nc.psum_tensor(f"wa_ps_q{i}", [P, 4, P], F32)) for i in range(2)]
        ps_o = [ctx.enter_context(nc.psum_tensor(f"wa_ps_o{i}", [P, 8, HD], F32)) for i in range(2)]
        (sink_in, rotated, dup, vs_zero, vs_in, k_zero, k_turned, kT_done, q_turned, qT_done, scored, masked, maxed,
         shifted, expd, sunk, summed, inverted, p_turned, pT_done, mixed, written) = map(sem, (
             "sink_in", "rotated", "dup", "vs_zero", "vs_in", "k_zero", "k_turned", "kT_done", "q_turned", "qT_done",
             "scored", "masked", "maxed", "shifted", "expd", "sunk", "summed", "inverted", "p_turned", "pT_done",
             "mixed", "written"))
        block = ctx.enter_context(nc.Block())
        ROTS = 6 * RT

        @block.sync
        def _(sp):
            sp.dma_start(sink[:, :], spread(sinks.rearrange("(a d) -> a d", a=1), [P, A_HEADS])).then_inc(sink_in, 16)
            sp.dma_start(vs[CHUNK:P, :, :], Z[0:CHUNK, :, EV:EV + P]).then_inc(vs_in, 16)
            sp.dma_start(vs[0:CHUNK, 1:RT, :], Z[CHUNK:P, 0:RT - 1, EV:EV + P]).then_inc(vs_in, 16)

        @block.gpsimd
        def _(pool):
            nc.gpsimd.memset(vs[0:CHUNK, 0, :], 0.0).then_inc(vs_zero, 1)
            nc.gpsimd.memset(kT[:, :, 0:CHUNK], 0.0).then_inc(k_zero, 1)

        @block.vector
        def _(dve):
            rotate(nc, nc.vector, env, Z, EQ, A_HEADS + A_KV, tmp, rotated, 0)
            dve.wait_ge(rotated, ROTS)
            for g in range(A_KV):
                for c in range(2):
                    nc.vector.tensor_copy(kdup[:, :, g, c, :], Z[:, :, EK + g * HD:EK + (g + 1) * HD]).then_inc(dup, 1)
            dve.wait_ge(sink_in, 16)

            def finish(i):
                dve.wait_ge(mixed, i + 1)
                dve.wait_ge(inverted, 2 * i + 2)
                rinv = spread(den[:, i, :, :].rearrange("p a c -> p c a").unsqueeze(3), [P, 4, 2, HD])
                nc.vector.tensor_tensor(Z[:, i, 0:NB].rearrange("p (c a d) -> p c a d", c=4, a=2),
                                        ps_o[i % 2][:, :, :].rearrange("p (c a) d -> p c a d", a=2), rinv,
                                        ALU.mult).then_inc(written, 1)

            for i in range(RT):
                dve.wait_ge(scored, i + 1)
                if i == 0:
                    for a in range(2):
                        nc.vector.memset(ps_s[a][0:CHUNK, :, 0:CHUNK], -1e30).then_inc(masked, 1)
                    dve.wait_ge(masked, 2)
                for a in range(2):
                    nc.vector.tensor_reduce(mx[:, i, a, :], ps_s[a][:, :, :], AX.X, ALU.max).then_inc(maxed, 1)
                dve.wait_ge(maxed, 3 * i + 2)
                nc.vector.tensor_tensor(mx[:, i, :, :], mx[:, i, :, :], sink[:, :].rearrange("p (c a) -> p a c", a=2),
                                        ALU.max).then_inc(maxed, 1)
                dve.wait_ge(maxed, 3 * i + 3)
                if i >= 2:
                    dve.wait_ge(p_turned, 2 * i - 2)
                for a in range(2):
                    nc.vector.tensor_tensor(prob[:, i % 2, a, :, :], ps_s[a][:, :, :],
                                            spread(mx[:, i, a, :].unsqueeze(2), [P, 4, P]), ALU.subtract).then_inc(shifted, 1)
                nc.vector.tensor_tensor(esink[:, i, :, :], sink[:, :].rearrange("p (c a) -> p a c", a=2), mx[:, i, :, :],
                                        ALU.subtract).then_inc(shifted, 1)
                if i >= 1:
                    finish(i - 1)
                dve.wait_ge(expd, 2 * i + 2)
                for a in range(2):
                    nc.vector.tensor_reduce(den[:, i, a, :], prob[:, i % 2, a, :, :], AX.X, ALU.add).then_inc(summed, 1)
                dve.wait_ge(summed, 2 * i + 2)
                dve.wait_ge(sunk, i + 1)
                nc.vector.tensor_tensor(den[:, i, :, :], den[:, i, :, :], esink[:, i, :, :], ALU.add).then_inc(inverted, 1)
                dve.wait_ge(inverted, 2 * i + 1)
                nc.vector.reciprocal(den[:, i, :, :], den[:, i, :, :]).then_inc(inverted, 1)
            finish(RT - 1)

        @block.scalar
        def _(act):
            for g in range(A_KV):
                for half in range(2):
                    act.wait_ge(k_turned, 2 * g + half + 1)
                    nc.scalar.activation(kT[:, g, CHUNK + half * NB:CHUNK + (half + 1) * NB], ps_t[half][:, :, :],
                                         ACT.Copy).then_inc(kT_done, 1)
            def queries(i):
                act.wait_ge(q_turned, i + 1)
                if i >= 2:
                    act.wait_ge(scored, i - 1)
                nc.scalar.activation(qT[:, i % 2, :, :], ps_q[i % 2][:, :, :], ACT.Copy, scale=HD ** -0.5).then_inc(qT_done, 1)

            queries(0)
            queries(1)
            for i in range(RT):
                for a in range(2):
                    act.wait_ge(shifted, 3 * i + 1 + a)
                    nc.scalar.activation(prob[:, i % 2, a, :, :], prob[:, i % 2, a, :, :], ACT.Exp).then_inc(expd, 1)
                act.wait_ge(shifted, 3 * i + 3)
                nc.scalar.activation(esink[:, i, :, :], esink[:, i, :, :], ACT.Exp).then_inc(sunk, 1)
                if i + 2 < RT:
                    queries(i + 2)
                if i >= 2:
                    act.wait_ge(mixed, i - 1)
                for a in range(2):
                    act.wait_ge(p_turned, 2 * i + a + 1)
                    nc.scalar.activation(probT[:, i % 2, 4 * a:4 * a + 4, :], ps_t[a][:, :, :], ACT.Copy).then_inc(pT_done, 1)

        @block.tensor
        def _(pe):
            pe.wait_ge(dup, 2 * A_KV)
            for g in range(A_KV):
                for half in range(2):
                    if g:
                        pe.wait_ge(kT_done, half + 1)
                    for r in range(4):
                        last = nc.tensor.transpose(ps_t[half][:, r, :], kdup[:, 4 * half + r, g, :, :], ident[:, :])
                    last.then_inc(k_turned, 1)

            def queries(i):
                if i >= 2:
                    pe.wait_ge(qT_done, i - 1)
                for c in range(4):
                    last = nc.tensor.transpose(ps_q[i % 2][:, c, :], Z[:, i, c * P:(c + 1) * P], ident[:, :])
                last.then_inc(q_turned, 1)

            def scores(i):
                pe.wait_ge(qT_done, i + 1)
                if i:
                    pe.wait_ge(shifted, 3 * i - 1)
                for c in range(4):
                    for a in range(2):
                        g = (2 * c + a) // 4
                        rows = slice(a * CHUNK, (a + 1) * CHUNK)
                        for u in range(2):
                            at = i * P + u * CHUNK
                            last = nc.tensor.matmul(ps_s[a][u * CHUNK:(u + 1) * CHUNK, c, :],
                                                    qT[rows, i % 2, c, u * CHUNK:(u + 1) * CHUNK],
                                                    kT[rows, g, at:at + P], start=True, stop=True)
                last.then_inc(scored, 1)

            def turn(i):
                for a in range(2):
                    pe.wait_ge(expd, 2 * i + a + 1)
                    if i:
                        pe.wait_ge(pT_done, 2 * i - 1 + a)
                    for c in range(4):
                        last = nc.tensor.transpose(ps_t[a][:, c, :], prob[:, i % 2, a, c, :], ident[:, :])
                    last.then_inc(p_turned, 1)

            def mix(i):
                pe.wait_ge(pT_done, 2 * i + 2)
                if i >= 2:
                    pe.wait_ge(written, i - 1)
                for u in range(2):
                    for a in range(2):
                        for c in range(4):
                            h = 2 * c + a
                            g = h // 4
                            v = Z[:, i, EV + g * HD:EV + (g + 1) * HD] if u else vs[:, i, g * HD:(g + 1) * HD]
                            last = nc.tensor.matmul(ps_o[i % 2][u * CHUNK:(u + 1) * CHUNK, h, :],
                                                    probT[:, i % 2, 4 * a + c, u * CHUNK:(u + 1) * CHUNK], v,
                                                    start=True, stop=True)
                last.then_inc(mixed, 1)

            queries(0)
            queries(1)
            pe.wait_ge(kT_done, 4)
            pe.wait_ge(k_zero, 1)
            pe.wait_ge(vs_zero, 1)
            pe.wait_ge(vs_in, 32)
            for i in range(RT):
                scores(i)
                if i + 2 < RT:
                    queries(i + 2)
                if i:
                    mix(i - 1)
                turn(i)
            mix(RT - 1)


def mlstm(nc, env, t):
    Z, ident = env["Z"], env["ident"]
    H = B_HEADS
    NT = RT * (RT + 1) // 2
    with ExitStack() as ctx:
        def sem(n):
            return new_sem(nc, env, f"ml_{n}")

        mem = Mem(nc, Map.T, Map.SMALL)
        xT = mem.take("ml_xT", [P, 4, CONV - 1 + SEQ], F32)
        qk = mem.take("ml_qk", [P, 4, SEQ], F32)
        va = mem.take("ml_va", [P, RT, H, B_DV + 1], F32)
        fr, ir, br, mk, mk2 = (mem.take(f"ml_{n}", [H, SEQ], F32) for n in ("fr", "ir", "br", "mk", "mk2"))
        E = mem.take("ml_E", [P, 2, H, P], F32)
        Wt = mem.take("ml_W", [P, 2, H, P], F32)
        dg = mem.take("ml_dg", [P, H, P], F32)
        late = mem.take("ml_late", [P, P], F32)
        sel = mem.take("ml_sel", [H, H, P], F32)
        last_row = mem.take("ml_last_row", [P, P], F32)
        nat = mem.take("ml_nat", [P, 3, RT, H], F32)
        total = mem.take("ml_total", [P, RT, H], F32)
        G = mem.take("ml_G", [P, RT, RT, H], F32)
        emn = mem.take("ml_emn", [P, RT, H], F32)
        den = mem.take("ml_den", [P, RT, H], F32)
        cw = mem.take("ml_cw", [P, CONV, 4], F32)
        cb = mem.take("ml_cb", [P, 4], F32)
        bi = mem.take("ml_bi", [H, 2], F32)
        ps_s = [ctx.enter_context(nc.psum_tensor(f"ml_ps_s{i}", [P, 2, NB], F32)) for i in range(2)]
        ps_n = ctx.enter_context(nc.psum_tensor("ml_ps_n", [P, 2, NB], F32))
        ps_a = ctx.enter_context(nc.psum_tensor("ml_ps_a", [P, H, P], F32))
        ps_x = ctx.enter_context(nc.psum_tensor("ml_ps_x", [P, NB], F32))
        (par_in, consts, padded, x_turned, xT_done, conved, silu_s, gate_s, silu_m, g_turned, gates_in, ga, ge, gl,
         gd, mark, back, back_done, tot_mm, tot_done, G_done, emn_sum, emn_done, va_done, a_bc, dg_done, e_done,
         s_done, w_done, mixed, den_abs, den_max, den_inv, written) = map(sem, (
             "par_in", "consts", "padded", "x_turned", "xT_done", "conved", "silu_s", "gate_s", "silu_m", "g_turned",
             "gates_in", "ga", "ge", "gl", "gd", "mark", "back", "back_done", "tot_mm", "tot_done", "G_done", "emn_sum",
             "emn_done", "va_done", "a_bc", "dg_done", "e_done", "s_done", "w_done", "mixed", "den_abs", "den_max",
             "den_inv", "written"))
        block = ctx.enter_context(nc.Block())
        pairs = [(i, j) for i in range(RT) for j in range(i + 1)]
        rows = [fr, ir]
        xbanks = [(c, half) for c in range(4) for half in range(2)]

        @block.sync
        def _(sp):
            sp.dma_start(cw[:, :, :], t["even_conv_w"][0].rearrange("t (c p) -> p t c", p=P),
                         allow_slow_non_contiguous=True).then_inc(par_in, 16)
            sp.dma_start(cb[:, :], t["even_conv_b"][0].rearrange("(c p) -> p c", p=P),
                         allow_slow_non_contiguous=True).then_inc(par_in, 16)
            sp.dma_start(bi[:, 0:1], t["even_bias_f"][0].rearrange("(h o) -> h o", o=1)).then_inc(par_in, 16)
            sp.dma_start(bi[:, 1:2], t["even_bias_i"][0].rearrange("(h o) -> h o", o=1)).then_inc(par_in, 16)

        @block.gpsimd
        def _(pool):
            nc.gpsimd.memset(xT[:, :, 0:CONV - 1], 0.0).then_inc(padded, 1)
            nc.gpsimd.memset(sel[:, :, :], 0.0).then_inc(consts, 1)
            nc.gpsimd.memset(last_row[:, :], 0.0).then_inc(consts, 1)
            nc.gpsimd.memset(late[:, :], 0.0).then_inc(consts, 1)
            nc.gpsimd.memset(mk[:, :], 1.0).then_inc(mark, 1)
            pool.wait_ge(mark, 1)
            nc.gpsimd.memset(mk[:, 0:SEQ:P], 0.0).then_inc(mark, 1)
            pool.wait_ge(consts, 3)
            nc.gpsimd.affine_select(out=sel[:, :, :], in_=sel[:, :, :], compare_op=ALU.not_equal, fill=1.0, base=0,
                                    pattern=[[-1, H], [0, P]], channel_multiplier=1).then_inc(consts, 1)
            nc.gpsimd.affine_select(out=last_row[:, :], in_=last_row[:, :], compare_op=ALU.not_equal, fill=1.0,
                                    base=1 - P, pattern=[[0, P]], channel_multiplier=1).then_inc(consts, 1)
            nc.gpsimd.affine_select(out=late[:, :], in_=late[:, :], compare_op=ALU.is_ge, fill=1e30, base=0,
                                    pattern=[[1, P]], channel_multiplier=-1).then_inc(consts, 1)
            nc.gpsimd.memset(va[:, :, :, B_DV:B_DV + 1], 1.0).then_inc(va_done, 1)
            for r in range(RT):
                nc.gpsimd.tensor_copy(va[:, r, :, 0:B_DV],
                                      Z[:, r, EBV:EBV + H * B_DV].rearrange("p (h d) -> p h d", h=H)).then_inc(va_done, 1)

        @block.scalar
        def _(act):
            act.wait_ge(par_in, 64)
            for n in range(2):
                for half in range(2):
                    act.wait_ge(g_turned, 2 * n + half + 1)
                    nc.scalar.activation(rows[n][:, half * NB:(half + 1) * NB], ps_s[n][0:H, half, :], ACT.Identity,
                                         bias=bi[:, n:n + 1]).then_inc(gates_in, 1)
            for n, (c, half) in enumerate(xbanks):
                act.wait_ge(x_turned, n + 1)
                nc.scalar.activation(xT[:, c, CONV - 1 + half * NB:CONV - 1 + (half + 1) * NB], ps_n[:, half, :],
                                     ACT.Copy).then_inc(xT_done, 1)
            act.wait_ge(ga, 1)
            nc.scalar.activation(mk2[:, :], br[:, :], ACT.Exp, scale=-1.0).then_inc(ge, 1)
            act.wait_ge(ge, 1)
            nc.scalar.activation(mk2[:, :], mk2[:, :], ACT.Ln, bias=1.0).then_inc(gl, 1)
            for c in range(4):
                act.wait_ge(conved, CONV * (c + 1))
                nc.scalar.activation(xT[:, c, CONV - 1:], qk[:, c, :], ACT.Sigmoid).then_inc(silu_s, 1)
            for r in range(RT):
                o = Z[:, r, EBO:EBO + NB]
                nc.scalar.activation(o, o, ACT.Sigmoid).then_inc(gate_s, 1)
            act.wait_ge(back, 1)
            nc.scalar.activation(nat[:, :, :, :], ps_x[:, 0:3 * RT * H].rearrange("p (a r h) -> p a r h", a=3, r=RT),
                                 ACT.Copy).then_inc(back_done, 1)
            act.wait_ge(emn_sum, 1)
            nc.scalar.activation(emn[:, :, :], emn[:, :, :], ACT.Exp, scale=-1.0).then_inc(emn_done, 1)
            act.wait_ge(G_done, 2 * RT - 1)
            for n, (i, j) in enumerate(pairs):
                if j == 0:
                    act.wait_ge(dg_done, i + 1)
                if n >= 2:
                    act.wait_ge(w_done, n - 1)
                for a in range(2):
                    for c in range(2):
                        h = 2 * c + a
                        src = dg[:, h, :] if j == i else ps_a[:, h, :]
                        nc.scalar.activation(E[:, n % 2, 2 * a + c, :], src, ACT.Exp, scale=-1.0,
                                             bias=G[:, i, j, h:h + 1]).then_inc(e_done, 1)

        @block.vector
        def _(dve):
            dve.wait_ge(gates_in, 2)
            nc.vector.scalar_tensor_tensor(br[:, :], fr[:, :], -1.0, fr[:, :], ALU.mult, ALU.max).then_inc(ga, 1)
            dve.wait_ge(padded, 1)
            for c in range(4):
                dve.wait_ge(xT_done, 2 * c + 2)
                nc.vector.tensor_scalar(qk[:, c, :], xT[:, c, CONV - 1:], cw[:, CONV - 1, c:c + 1], cb[:, c:c + 1],
                                        ALU.mult, ALU.add).then_inc(conved, 1)
                for tap in range(CONV - 1):
                    dve.wait_ge(conved, CONV * c + 1 + tap)
                    nc.vector.scalar_tensor_tensor(qk[:, c, :], xT[:, c, tap:tap + SEQ], cw[:, tap, c:c + 1], qk[:, c, :],
                                                   ALU.mult, ALU.add).then_inc(conved, 1)
            dve.wait_ge(gl, 1)
            nc.vector.scalar_tensor_tensor(fr[:, :], fr[:, :], 0.0, mk2[:, :], ALU.min, ALU.subtract).then_inc(gd, 1)
            dve.wait_ge(gd, 1)
            dve.wait_ge(mark, 2)
            nc.vector.tensor_tensor_scan(br[:, :], mk[:, :], fr[:, :], 0.0, ALU.mult, ALU.add).then_inc(gd, 1)
            dve.wait_ge(gd, 2)
            dve.wait_ge(gates_in, 4)
            nc.vector.tensor_tensor(ir[:, :], ir[:, :], br[:, :], ALU.subtract).then_inc(gd, 1)
            nc.vector.memset(mk[:, :], 0.0).then_inc(gd, 1)
            dve.wait_ge(gd, 4)
            nc.vector.tensor_copy(mk[:, P:SEQ:P], br[:, P - 1:SEQ - 1:P]).then_inc(gd, 1)
            dve.wait_ge(gd, 5)
            nc.vector.tensor_tensor_scan(fr[:, :], mk[:, :], ir[:, :], 0.0, ALU.add, ALU.max).then_inc(gd, 1)
            for c in range(4):
                dve.wait_ge(silu_s, c + 1)
                nc.vector.tensor_tensor(qk[:, c, :], qk[:, c, :], xT[:, c, CONV - 1:], ALU.mult).then_inc(silu_m, 1)
            dve.wait_ge(back_done, 1)
            nc.vector.tensor_tensor(emn[:, :, :], nat[:, 1, :, :], nat[:, 2, :, :], ALU.add).then_inc(emn_sum, 1)
            dve.wait_ge(tot_mm, 1)
            nc.vector.tensor_copy(total[:, :, :], ps_x[:, P:P + RT * H].rearrange("p (r h) -> p r h", h=H)).then_inc(tot_done, 1)
            dve.wait_ge(tot_done, 1)
            for i in range(RT):
                if i:
                    dve.wait_ge(G_done, 2 * i - 1)
                    nc.vector.tensor_tensor(G[:, i, 0:i, :], G[:, i - 1, 0:i, :],
                                            spread(total[:, i - 1, :].unsqueeze(1), [P, i, H]), ALU.add).then_inc(G_done, 1)
                nc.vector.tensor_copy(G[:, i, i, :], nat[:, 0, i, :]).then_inc(G_done, 1)
            dve.wait_ge(consts, 6)

            def diagonal(i):
                dve.wait_ge(a_bc, i + 1)
                if i:
                    dve.wait_ge(e_done, 4 * pairs.index((i - 1, i - 1)) + 4)
                nc.vector.tensor_tensor(dg[:, :, :], ps_a[:, :, :], spread(late[:, :].unsqueeze(1), [P, H, P]),
                                        ALU.add).then_inc(dg_done, 1)

            def finish(i):
                dve.wait_ge(mixed, pairs.index((i, i)) + 1)
                num = ps_n[:, :, 0:2 * (B_DV + 1)].rearrange("p a (c d) -> p a c d", d=B_DV + 1)
                d = den[:, i, :].rearrange("p (a c) -> p a c", a=2)
                dve.wait_ge(emn_done, 1)
                nc.vector.scalar_tensor_tensor(d, num[:, :, :, B_DV], -1.0, emn[:, i, :].rearrange("p (c a) -> p a c", a=2),
                                               ALU.mult, ALU.max).then_inc(den_abs, 1)
                dve.wait_ge(den_abs, i + 1)
                nc.vector.tensor_tensor(d, num[:, :, :, B_DV], d, ALU.max).then_inc(den_max, 1)
                dve.wait_ge(den_max, i + 1)
                nc.vector.reciprocal(den[:, i, :], den[:, i, :]).then_inc(den_inv, 1)
                dve.wait_ge(den_inv, i + 1)
                dve.wait_ge(gate_s, RT)
                for a in range(2):
                    for c in range(2):
                        h = 2 * c + a
                        o = Z[:, i, EBO + h * B_DV:EBO + (h + 1) * B_DV]
                        nc.vector.scalar_tensor_tensor(o, num[:, a, c, 0:B_DV], den[:, i, 2 * a + c:2 * a + c + 1], o,
                                                       ALU.mult, ALU.mult).then_inc(written, 1)

            for n, (i, j) in enumerate(pairs):
                if j == 0:
                    diagonal(i)
                dve.wait_ge(s_done, n + 1)
                dve.wait_ge(e_done, 4 * n + 4)
                if n >= 2:
                    dve.wait_ge(mixed, n - 1)
                nc.vector.scalar_tensor_tensor(
                    Wt[:, n % 2, :, :], ps_s[n % 2][:, :, 0:2 * P], B_DK ** -0.5,
                    E[:, n % 2, :, :].rearrange("p (a c) t -> p a (c t)", a=2), ALU.mult, ALU.mult).then_inc(w_done, 1)
                if j == 0 and i:
                    finish(i - 1)
            finish(RT - 1)

        @block.tensor
        def _(pe):
            for n, col in enumerate((EBF, EBI)):
                for r in range(RT):
                    last = nc.tensor.transpose(ps_s[n][0:H, r // 4, (r % 4) * P:(r % 4 + 1) * P], Z[:, r, col:col + H],
                                               ident[:, :])
                    if r % 4 == 3:
                        last.then_inc(g_turned, 1)
            for n, (c, half) in enumerate(xbanks):
                if n >= 2:
                    pe.wait_ge(xT_done, n - 1)
                for r in range(4):
                    last = nc.tensor.transpose(ps_n[:, half, r * P:(r + 1) * P],
                                               Z[:, 4 * half + r, EBQK + c * P:EBQK + (c + 1) * P], ident[:, :])
                last.then_inc(x_turned, 1)
            pe.wait_ge(gd, 6)
            for n, row in enumerate((ir, br, fr)):
                for r in range(RT):
                    last = nc.tensor.transpose(ps_x[:, (n * RT + r) * H:(n * RT + r + 1) * H], row[:, r * P:(r + 1) * P],
                                               ident[0:H, 0:H])
            last.then_inc(back, 1)
            pe.wait_ge(back_done, 1)
            pe.wait_ge(consts, 6)
            nc.tensor.matmul(ps_x[:, P:P + RT * H], last_row[:, :], nat[:, 1, :, :], start=True, stop=True).then_inc(tot_mm, 1)

            def broadcast(i):
                if i:
                    pe.wait_ge(dg_done, i)
                if i > 1:
                    pe.wait_ge(e_done, 4 * pairs.index((i - 1, i - 1)))
                for h in range(H):
                    last = nc.tensor.matmul(ps_a[:, h, :], sel[:, h, :], fr[:, i * P:(i + 1) * P], start=True, stop=True)
                last.then_inc(a_bc, 1)

            def scores(n):
                i, j = pairs[n]
                if n >= 2:
                    pe.wait_ge(w_done, n - 1)
                for c in range(2):
                    for a in range(2):
                        part = slice(a * B_DK, (a + 1) * B_DK)
                        last = nc.tensor.matmul(ps_s[n % 2][:, a, c * P:(c + 1) * P],
                                                qk[part, 2 + c, j * P:(j + 1) * P], qk[part, c, i * P:(i + 1) * P],
                                                start=True, stop=True)
                last.then_inc(s_done, 1)

            def mix(n):
                i, j = pairs[n]
                pe.wait_ge(w_done, n + 1)
                if j == 0 and i:
                    pe.wait_ge(written, 4 * i)
                for a in range(2):
                    for c in range(2):
                        h = 2 * c + a
                        last = nc.tensor.matmul(ps_n[:, a, c * (B_DV + 1):(c + 1) * (B_DV + 1)],
                                                Wt[:, n % 2, 2 * a + c, :], va[:, j, h, :], start=(j == 0 and c == 0),
                                                stop=(j == i and c == 1), skip_group_check=True)
                last.then_inc(mixed, 1)

            pe.wait_ge(silu_m, 4)
            pe.wait_ge(va_done, 1 + RT)
            for n, (i, j) in enumerate(pairs):
                if j == 0:
                    broadcast(i)
                scores(n)
                if n:
                    mix(n - 1)
            mix(len(pairs) - 1)


def sparse_prelude(nc, env, g_dram, kThi, kTlo, ikhi, iklo):
    Z, ident = env["Z"], env["ident"]
    with ExitStack() as ctx:
        def sem(n):
            return new_sem(nc, env, f"sp_{n}")

        mem = Mem(nc, Map.T + 44 * KB, Map.SMALL)
        tmp = mem.take("sp_tmp", [P, 4 * RT, 20 * NF], F32)
        itmp = mem.take("sp_itmp", [P, 4 * RT, 9 * NF], F32)
        kdup = mem.take("sp_kdup", [P, RT, C_KV + 1, 2, HD], F32)
        sq = mem.take("sp_sq", [P, RT, HD], F32)
        g = mem.take("sp_g", [P, HD], F32)
        ss = mem.take("sp_ss", [P, RT], F32)
        st = mem.take("sp_st", [P, 4, RT], F32)
        ps = [ctx.enter_context(nc.psum_tensor(f"sp_ps{i}", [P, 4, P], F32)) for i in range(4)]
        g_in, squared, sums, var, root, rstd, normed, irot, rotated, scaled, dup, turned, hi_done, lo_done = map(sem, (
            "g_in", "squared", "sums", "var", "root", "rstd", "normed", "irot", "rotated", "scaled", "dup", "turned", "hi_done",
            "lo_done"))
        units = [(C_KV, ikhi[:, h * NB:(h + 1) * NB], iklo[:, h * NB:(h + 1) * NB], h) for h in range(2)]
        units += [(k, kThi[:, k, h * NB:(h + 1) * NB], kTlo[:, k, h * NB:(h + 1) * NB], h)
                  for k in range(C_KV) for h in range(2)]
        block = ctx.enter_context(nc.Block())
        ik = Z[:, :, OIK:OIK + HD]

        @block.sync
        def _(sp):
            sp.dma_start(g[:, :], spread(g_dram.rearrange("(a d) -> a d", a=1), [P, HD])).then_inc(g_in, 16)

        @block.vector
        def _(dve):
            nc.vector.tensor_tensor(sq[:, :, :], ik, ik, ALU.mult).then_inc(squared, 1)
            dve.wait_ge(squared, 1)
            nc.vector.tensor_reduce(ss[:, :], sq[:, :, :], AX.X, ALU.add).then_inc(sums, 1)
            newton_rstd(nc, dve, st, ss[:, :], 1.0 / HD, sums, 1, var, root, rstd)
            nc.vector.tensor_tensor(ik, ik, spread(st[:, 2, :].unsqueeze(2), [P, RT, HD]), ALU.mult).then_inc(normed, 1)
            dve.wait_ge(normed, 1)
            dve.wait_ge(g_in, 16)
            nc.vector.tensor_tensor(ik, ik, spread(g[:, :].unsqueeze(1), [P, RT, HD]), ALU.mult).then_inc(normed, 1)
            dve.wait_ge(normed, 2)
            rotate(nc, nc.vector, env, Z, OIQ, IH + 1, itmp, irot, 0)
            rotate(nc, nc.vector, env, Z, OQ, C_HEADS + C_KV, tmp, rotated, 0)
            nc.vector.tensor_scalar(Z[:, :, OIW:OIW + IH], Z[:, :, OIW:OIW + IH], float(np.float32(IH ** -0.5)), None,
                                    ALU.mult).then_inc(scaled, 1)
            for n, (col, hi, lo, half) in enumerate(units):
                dve.wait_ge(hi_done, n + 1)
                nc.vector.tensor_tensor(lo, ps[n % 4][:, :, :].rearrange("p a b -> p (a b)"), f32(hi),
                                        ALU.subtract).then_inc(lo_done, 1)

        @block.gpsimd
        def _(pool):
            pool.wait_ge(irot, 6 * RT)
            for c in range(2):
                nc.gpsimd.tensor_copy(kdup[:, :, C_KV, c, :], ik).then_inc(dup, 1)
            pool.wait_ge(rotated, 6 * RT)
            for k in range(C_KV):
                for c in range(2):
                    nc.gpsimd.tensor_copy(kdup[:, :, k, c, :], Z[:, :, OK_ + k * HD:OK_ + (k + 1) * HD]).then_inc(dup, 1)

        @block.scalar
        def _(act):
            act.wait_ge(var, 1)
            nc.scalar.activation(st[:, 1, :], st[:, 0, :], ACT.Sqrt).then_inc(root, 1)
            for n, (col, hi, lo, half) in enumerate(units):
                act.wait_ge(turned, n + 1)
                nc.scalar.activation(hi, ps[n % 4][:, :, :].rearrange("p a b -> p (a b)"), ACT.Copy).then_inc(hi_done, 1)

        @block.tensor
        def _(pe):
            for n, (col, hi, lo, half) in enumerate(units):
                pe.wait_ge(dup, 2 if n < 2 else 2 * (C_KV + 1))
                if n >= 4:
                    pe.wait_ge(lo_done, n - 3)
                for r in range(4):
                    last = nc.tensor.transpose(ps[n % 4][:, r, :], kdup[:, 4 * half + r, col, :, :], ident[:, :])
                last.then_inc(turned, 1)


def sparse_attention(nc, env, g_dram):
    Z, ident, identb = env["Z"], env["ident"], env["identb"]
    TAKEN, BARRED, OFF = -3.3e38, -3.2e38, -1e30
    EASY = TOPK // P
    H = C_HEADS
    ROUNDS = TOPK // 8
    PER = ROUNDS // H
    keep = Mem(nc, Map.T, Map.T + 44 * KB)
    kThi = keep.take("sa_kThi", [P, C_KV, SEQ], F32R)
    kTlo = keep.take("sa_kTlo", [P, C_KV, SEQ], F32R)
    ikhi = keep.take("sa_ikhi", [P, SEQ], F32R)
    iklo = keep.take("sa_iklo", [P, SEQ], F32R)
    sparse_prelude(nc, env, g_dram, kThi, kTlo, ikhi, iklo)
    with ExitStack() as ctx:
        def sem(n):
            return new_sem(nc, env, f"sa_{n}")

        mem = Mem(nc, Map.T + 44 * KB, Map.SMALL)
        score = mem.take("sa_score", [P, 2, SEQ], F32)
        top8 = mem.take("sa_top8", [P, 2, 8], F32)
        mask = mem.take("sa_mask", [P, 2, SEQ], BF16)
        qfull = mem.take("sa_qfull", [P, 2, 4, P], F32)
        qT = mem.take("sa_qT", [P, 2, 4, P], F32R)
        iqT = mem.take("sa_iqT", [P, 2, IH, P], F32R)
        rel = mem.take("sa_rel", [P, 2, NB], F32)
        prob = mem.take("sa_prob", [P, 2, SEQ], F32)
        probT = mem.take("sa_probT", [P, 2, RT, P], F32)
        twice = mem.take("sa_twice", [P, 2, 4, 2, HD], F32)
        nmax = mem.take("sa_nmax", [P, RT, H], F32)
        rsum = mem.take("sa_rsum", [P, RT, H], F32)
        ps_s = [ctx.enter_context(nc.psum_tensor(f"sa_ps_s{i}", [P, SEQ], F32)) for i in range(2)]
        ps_t = [ctx.enter_context(nc.psum_tensor(f"sa_ps_t{i}", [P, 4, P], F32)) for i in range(2)]
        ps_o = ctx.enter_context(nc.psum_tensor("sa_ps_o", [P, 8, HD], F32))
        ps_x = ctx.enter_context(nc.psum_tensor("sa_ps_x", [P, 4, P], F32))
        (doubled, x_full, x_free, x_hi, q_lo, zeroed, acc_done, barred, top_found, taken, mask_done, scored, max_done,
         exp_done, t_done, pT_done, mixed, inv_done, out_done) = map(sem, (
             "doubled", "x_full", "x_free", "x_hi", "q_lo", "zeroed", "acc_done", "barred", "top_found", "taken", "mask_done",
             "scored", "max_done", "exp_done", "t_done", "pT_done", "mixed", "inv_done", "out_done"))
        block = ctx.enter_context(nc.Block())

        def parts(i):
            return (i * P + P + NB - 1) // NB

        aux = {}

        def use(step, item):
            aux.setdefault(step, []).append(item)

        for u in range(2):
            use(-1, ("iq", EASY, u))
        use(-1, ("q", 0, 0))
        for i in range(RT):
            for h in range(H):
                n = i * H + h
                ii = i + 2
                if EASY <= ii < RT and h < IH * parts(ii):
                    use(n, ("s", ii, h // parts(ii), h % parts(ii)))
                if h % 4 == 1 and n + 4 < RT * H:
                    nxt = n + 3
                    use(n, ("q", nxt // H, nxt % H // 4))
                if h in (10, 14) and EASY < i + 3 < RT:
                    use(n, ("iq", i + 3, (h - 10) // 4))
        order = [item for step in sorted(aux) for item in aux[step]]
        turn_items = [item for item in order if item[0] != "s"]
        score_items = [item for item in order if item[0] == "s"]
        place = {item: n for n, item in enumerate(order)}
        turn_at = {item: n for n, item in enumerate(turn_items)}
        score_at = {item: n for n, item in enumerate(score_items)}
        steps = [(i, h) for i in range(RT) for h in range(H)]
        turns = [(n, b) for n, (i, h) in enumerate(steps) for b in range(i // 4 + 1)]
        turns_at = {nb: m for m, nb in enumerate(turns)}

        def last_turn(n):
            return turns_at[(n, steps[n][0] // 4)]

        def source(item):
            kind, i, g = item
            col = (OQ if kind == "q" else OIQ) + g * 4 * HD
            return Z[:, i, col:col + 4 * HD].rearrange("p (h d) -> p h d", d=HD)

        def target(item):
            kind, i, g = item
            return qT[:, (4 * i + g) % 2, :, :] if kind == "q" else iqT[:, i % 2, 4 * g:4 * g + 4, :]

        @block.tensor
        def _(pe):
            def fill(item):
                n = place[item]
                if n:
                    pe.wait_ge(x_free, n)
                if item[0] == "s":
                    _, i, head, part = item
                    wide = min(NB, (i + 1) * P - part * NB)
                    keys = slice(part * NB, part * NB + wide)
                    if head in (0, 4) and part == 0:
                        pe.wait_ge(q_lo, turn_at[("iq", i, head // 4)] + 1)
                    bank = ps_x[:, :, :].rearrange("p a b -> p (a b)")[:, 0:wide]
                    nc.tensor.matmul(bank, iqT[:, i % 2, head, :], ikhi[:, keys], start=True, stop=False)
                    last = nc.tensor.matmul(bank, iqT[:, i % 2, head, :], iklo[:, keys], start=False, stop=True)
                else:
                    m = turn_at[item]
                    pe.wait_ge(doubled, 2 * m + 2)
                    for u in range(4):
                        last = nc.tensor.transpose(ps_x[:, u, :], twice[:, m % 2, u, :, :], ident[:, :])
                last.then_inc(x_full, 1)

            def logits(n):
                i, h = steps[n]
                if h == 0:
                    pe.wait_ge(mask_done, i + 1)
                if h % 4 == 0:
                    pe.wait_ge(q_lo, turn_at[("q", i, h // 4)] + 1)
                if n >= 2:
                    pe.wait_ge(exp_done, n - 1)
                for part in range(parts(i)):
                    keys = slice(part * NB, min((i + 1) * P, (part + 1) * NB))
                    bank = ps_s[n % 2][:, keys]
                    q = qT[:, (4 * i + h // 4) % 2, h % 4, :]
                    nc.tensor.matmul(bank, identb[:, :], mask[:, i % 2, keys], start=True, stop=False)
                    nc.tensor.matmul(bank, q, kThi[:, h // 4, keys], start=False, stop=False)
                    last = nc.tensor.matmul(bank, q, kTlo[:, h // 4, keys], start=False, stop=True)
                last.then_inc(scored, 1)

            def turn(n):
                i, h = steps[n]
                pe.wait_ge(exp_done, n + 1)
                for b in range(i // 4 + 1):
                    m = turns_at[(n, b)]
                    if m >= 2:
                        pe.wait_ge(pT_done, m - 1)
                    for j in range(4 * b, min(i + 1, 4 * b + 4)):
                        last = nc.tensor.transpose(ps_t[m % 2][:, j - 4 * b, :], prob[:, n % 2, j * P:(j + 1) * P], ident[:, :])
                    last.then_inc(t_done, 1)

            def mix(n):
                i, h = steps[n]
                pe.wait_ge(pT_done, last_turn(n) + 1)
                if n:
                    pe.wait_ge(out_done, n)
                for j in range(i + 1):
                    last = nc.tensor.matmul(ps_o[:, h % 8, :], probT[:, n % 2, j, :],
                                            Z[:, j, OV + h // 4 * HD:OV + (h // 4 + 1) * HD], start=(j == 0), stop=(j == i))
                last.then_inc(mixed, 1)

            for item in aux[-1]:
                fill(item)
            for n in range(len(steps) + 2):
                if n < len(steps):
                    logits(n)
                if n - 2 >= 0:
                    mix(n - 2)
                for item in aux.get(n, []):
                    fill(item)
                if 0 <= n - 1 < len(steps):
                    turn(n - 1)

        @block.scalar
        def _(act):
            def empty(item):
                n = place[item]
                act.wait_ge(x_full, n + 1)
                if item[0] == "s":
                    _, i, head, part = item
                    m = score_at[item]
                    wide = min(NB, (i + 1) * P - part * NB)
                    if m >= 2:
                        act.wait_ge(acc_done, m - 1)
                    nc.scalar.activation(rel[:, m % 2, 0:wide], ps_x[:, :, :].rearrange("p a b -> p (a b)")[:, 0:wide],
                                         ACT.Relu).then_inc(x_free, 1)
                else:
                    m = turn_at[item]
                    if m >= 2:
                        act.wait_ge(q_lo, m - 1)
                    if item[0] == "q" and 4 * item[1] + item[2] >= 2:
                        act.wait_ge(scored, (4 * item[1] + item[2] - 1) * 4)
                    if item[0] == "iq" and item[1] >= EASY + 2:
                        old = item[1] - 2
                        act.wait_ge(x_full, place[("s", old, IH - 1, parts(old) - 1)] + 1)
                    nc.scalar.activation(qfull[:, m % 2, :, :], ps_x[:, :, :], ACT.Copy, scale=HD ** -0.5).then_inc(x_hi, 1)
                    nc.scalar.activation(target(item), ps_x[:, :, :], ACT.Copy, scale=HD ** -0.5).then_inc(x_free, 1)

            def softmax(n):
                i, h = steps[n]
                act.wait_ge(max_done, n + 1)
                if n >= 2:
                    act.wait_ge(t_done, last_turn(n - 2) + 1)
                nc.scalar.activation(prob[:, n % 2, 0:(i + 1) * P], ps_s[n % 2][:, 0:(i + 1) * P], ACT.Exp,
                                     bias=nmax[:, i, h:h + 1], accum_out=rsum[:, i, h:h + 1]).then_inc(exp_done, 1)

            def keep_turned(n):
                i, h = steps[n]
                if n >= 2:
                    act.wait_ge(mixed, n - 1)
                for b in range(i // 4 + 1):
                    m = turns_at[(n, b)]
                    act.wait_ge(t_done, m + 1)
                    count = min(i + 1 - 4 * b, 4)
                    nc.scalar.activation(probT[:, n % 2, 4 * b:4 * b + count, :], ps_t[m % 2][:, 0:count, :],
                                         ACT.Copy).then_inc(pT_done, 1)

            def write(n):
                i, h = steps[n]
                act.wait_ge(mixed, n + 1)
                act.wait_ge(inv_done, n + 1)
                nc.scalar.activation(Z[:, i, OQ + h * HD:OQ + (h + 1) * HD], ps_o[:, h % 8, :], ACT.Copy,
                                     scale=rsum[:, i, h:h + 1]).then_inc(out_done, 1)

            for item in aux[-1]:
                empty(item)
            for n in range(len(steps) + 2):
                if n < len(steps):
                    softmax(n)
                if n - 2 >= 0:
                    write(n - 2)
                for item in aux.get(n, []):
                    empty(item)
                if 0 <= n - 1 < len(steps):
                    keep_turned(n - 1)

        @block.gpsimd
        def _(pool):
            def double(m):
                if m >= 2:
                    pool.wait_ge(x_full, place[turn_items[m - 2]] + 1)
                    pool.wait_ge(q_lo, m - 1)
                for c in range(2):
                    nc.gpsimd.tensor_copy(twice[:, m % 2, :, c, :], source(turn_items[m])).then_inc(doubled, 1)

            double(0)
            for m, item in enumerate(turn_items):
                if m + 1 < len(turn_items):
                    double(m + 1)
                pool.wait_ge(doubled, min(2 * m + 4, 2 * len(turn_items)))
                pool.wait_ge(x_hi, m + 1)
                pool.wait_ge(x_free, place[item] + 1)
                to = target(item)[HD:P, :, :]
                nc.gpsimd.tensor_tensor(to, qfull[HD:P, m % 2, :, :], f32(to), ALU.subtract).then_inc(q_lo, 1)

        @block.vector
        def _(dve):
            def accumulate(item):
                _, i, head, part = item
                m = score_at[item]
                wide = min(NB, (i + 1) * P - part * NB)
                to = score[:, i % 2, part * NB:part * NB + wide]
                w = Z[:, i, OIW + head:OIW + head + 1]
                dve.wait_ge(x_free, place[item] + 1)
                if head == 0:
                    if i >= EASY + 2:
                        dve.wait_ge(mask_done, i - 1)
                    nc.vector.tensor_scalar(to, rel[:, m % 2, 0:wide], w, None, ALU.mult).then_inc(acc_done, 1)
                else:
                    dve.wait_ge(acc_done, m - parts(i) + 1)
                    nc.vector.scalar_tensor_tensor(to, rel[:, m % 2, 0:wide], w, to, ALU.mult, ALU.add).then_inc(acc_done, 1)

            def bar(i):
                dve.wait_ge(acc_done, score_at[("s", i, IH - 1, parts(i) - 1)] + 1)
                nc.vector.memset(score[0:CHUNK, i % 2, i * P + CHUNK:(i + 1) * P], BARRED).then_inc(barred, 1)

            def find(i, k):
                m = (i - EASY) * ROUNDS + k
                if k == 0:
                    dve.wait_ge(barred, i - EASY + 1)
                else:
                    dve.wait_ge(taken, m)
                nc.vector.max(top8[:, m % 2, :], score[:, i % 2, 0:(i + 1) * P]).then_inc(top_found, 1)

            def take(i, k):
                m = (i - EASY) * ROUNDS + k
                s = score[:, i % 2, 0:(i + 1) * P]
                dve.wait_ge(top_found, m + 1)
                nc.vector.match_replace(out=s, in_to_replace=top8[:, m % 2, :], in_values=s, imm_value=TAKEN).then_inc(taken, 1)

            def make_mask(i):
                keys = slice(0, (i + 1) * P)
                if i >= 2:
                    dve.wait_ge(scored, (i - 1) * H)
                if i < EASY:
                    nc.vector.memset(mask[:, i % 2, keys], 0.0).then_inc(zeroed, 1)
                    dve.wait_ge(zeroed, i + 1)
                    nc.vector.memset(mask[0:CHUNK, i % 2, i * P + CHUNK:(i + 1) * P], OFF).then_inc(mask_done, 1)
                else:
                    dve.wait_ge(taken, (i - EASY + 1) * ROUNDS)
                    nc.vector.tensor_scalar(mask[:, i % 2, keys], score[:, i % 2, keys], TAKEN, OFF, ALU.not_equal,
                                            ALU.mult).then_inc(mask_done, 1)

            for i in range(EASY):
                make_mask(i)
            for n in range(len(steps) + 1):
                if n < len(steps):
                    i, h = steps[n]
                    dve.wait_ge(scored, n + 1)
                    nc.vector.tensor_reduce(nmax[:, i, h:h + 1], ps_s[n % 2][:, 0:(i + 1) * P], AX.X, ALU.max,
                                            negate=True).then_inc(max_done, 1)
                    nxt = i + 1
                    select = EASY <= nxt < RT
                    if select:
                        find(nxt, PER * h)
                if n >= 1:
                    i2, h2 = steps[n - 1]
                    dve.wait_ge(exp_done, n)
                    nc.vector.reciprocal(rsum[:, i2, h2:h2 + 1], rsum[:, i2, h2:h2 + 1]).then_inc(inv_done, 1)
                if n < len(steps):
                    if select:
                        take(nxt, PER * h)
                    for item in aux.get(n, []):
                        if item[0] == "s":
                            accumulate(item)
                            if item[2] == IH - 1 and item[3] == parts(item[1]) - 1:
                                bar(item[1])
                    if select:
                        for k in range(PER * h + 1, PER * (h + 1)):
                            find(nxt, k)
                            take(nxt, k)
                        if h == H - 1:
                            make_mask(nxt)


def program(nc, t):
    mem = Mem(nc, Map.X, Map.Z)
    env = {"X": mem.take("X", [P, RT, D], F32), "sems": []}
    mem = Mem(nc, Map.Z, Map.T)
    env["Z"] = mem.take("Z", [P, RT, ZW], F32)
    mem = Mem(nc, Map.T, Map.W)
    env["Thi"] = mem.take("Thi", [P, KC, SEQ], F32R)
    env["Tlo"] = mem.take("Tlo", [P, KC, SEQ], F32R)
    mem = Mem(nc, Map.SMALL, nc.sbuf_usable_end - BASE)
    env["ident"] = mem.take("ident", [P, P], F32)
    env["identb"] = mem.take("identb", [P, P], BF16)
    env["cos"] = mem.take("cos", [P, RT, NF], F32)
    env["sin"] = mem.take("sin", [P, RT, NF], F32)
    constants(nc, env)
    norm_transpose(nc, env, "n0", t["norm_mix"][0], load_x=t["x"][0])
    project(nc, env, "in0", t["even_w_in"][0], EVEN_IN, env["Z"])
    rotary_tables(nc, env, t["positions"][0])
    window_attention(nc, env, t["even_sinks"][0])
    mlstm(nc, env, t)
    Z = env["Z"]
    norm_transpose(nc, env, "y0", None, src=lambda r, k: Z[:, r, k * P:(k + 1) * P] if k < 4
                   else Z[:, r, EBO + (k - 4) * P:EBO + (k - 3) * P])
    project(nc, env, "out0", t["even_w_out"][0], D, env["X"], add=True)
    norm_transpose(nc, env, "n1", t["norm_mlp"][0])
    mlp(nc, env, "mlp0", t["w_up"][0], t["w_down"][0])
    reset_semaphores(nc, env)
    norm_transpose(nc, env, "n2", t["norm_mix"][1])
    project(nc, env, "in1", t["odd_w_in"][0], ODD_IN, Z)
    sparse_attention(nc, env, t["odd_idx_k_norm"][0])
    norm_transpose(nc, env, "y1", None, src=lambda r, k: Z[:, r, k * P:(k + 1) * P])
    project(nc, env, "out1", t["odd_w_out"][0], D, env["X"], add=True)
    norm_transpose(nc, env, "n3", t["norm_mlp"][1])
    mlp(nc, env, "mlp1", t["w_up"][1], t["w_down"][1])
    final_norm(nc, env, t["final_norm"], t["out"][0])


INPUTS = ["x", "positions", "norm_mix", "even_w_in", "even_sinks", "even_conv_w", "even_conv_b", "even_bias_i",
          "even_bias_f", "even_w_out", "odd_w_in", "odd_idx_k_norm", "odd_w_out", "norm_mlp", "w_up", "w_down",
          "final_norm"]


def kernel(**inputs):
    import numpy as _np
    import concourse.bacc as _bacc
    from concourse import mybir as _mybir
    from concourse.bass_utils import run_bass_kernel_spmd as _run

    nc = _bacc.Bacc("TRN2", target_bir_lowering=False, num_devices=1)
    arrays, t = {}, {}
    for name in INPUTS:
        a = _np.ascontiguousarray(inputs[name])
        arrays[f"in_{name}"] = a
        t[name] = nc.dram_tensor(f"in_{name}", a.shape, _mybir.dt.from_np(a.dtype), kind="ExternalInput").ap()
    t["out"] = nc.dram_tensor("out_y", (1, SEQ, D), _mybir.dt.float32, kind="ExternalOutput").ap()
    program(nc, t)
    r = _run(nc, [arrays], core_ids=[0])
    return r.results[0]["out_y"]
```

```python
from contextlib import ExitStack

import numpy as np

import concourse.bass as bass
from concourse import mybir

F32 = mybir.dt.float32
F32R = mybir.dt.float32r
BF16 = mybir.dt.bfloat16
I32 = mybir.dt.int32
I16 = mybir.dt.int16
U16 = mybir.dt.uint16
ALU = mybir.AluOpType
ACT = mybir.ActivationFunctionType
AX = mybir.AxisListType

P = 128
D = 1024
SEQ = 1024
KC = D // P
RT = SEQ // P
CHUNK = 64
HD = 64
ROT = HD // 4
NF = ROT // 2
THETA = 500000.0
EPS = 1e-5
A_HEADS, A_KV = 8, 2
B_HEADS, B_DV, B_DK, CONV = 4, 128, 64, 4
C_HEADS, C_KV = 16, 4
IH = 8
TOPK = 256
D_FF = 4096
FC = D_FF // P
NB = 512
EVEN_IN, ODD_IN = 2312, 2120
EASY = TOPK // P
BARRED, OFF = -3.2e38, -1e30
ZW = EVEN_IN
EQ, EK, EV, EBQK, EBV, EBO, EBI, EBF = 0, 512, 640, 768, 1280, 1792, 2304, 2308
OQ, OK_, OV, OIQ, OIK, OIW = 0, 1024, 1280, 1536, 2048, 2112

KB = 1024
BASE = 16 * KB + 128


class Map:
    X = 0
    Z = 32 * KB
    T = Z + RT * ZW * 4
    W = T + 64 * KB
    SMALL = W + 36 * KB


class Mem:

    def __init__(self, nc, start, end):
        self.nc, self.at, self.end = nc, BASE + start, BASE + end

    def take(self, name, shape, dt):
        size = int(np.prod(shape[1:])) * (2 if dt in (BF16, I16, U16) else 4)
        assert self.at + size <= self.end, (name, self.at + size - self.end)
        t = self.nc.alloc_sbuf_tensor_at(name, shape, dt, offset=self.at)
        self.at += (size + 31) // 32 * 32
        return t


def new_sem(nc, env, name):
    s = nc.alloc_semaphore(name)
    env["sems"].append(s)
    return s


def reset_semaphores(nc, env):
    nc.clear_and_free_semaphores(env["sems"])
    nc.all_engine_barrier()
    env["sems"] = []


def f32(ap):
    return ap.bitcast(F32)


def newton_rstd(nc, dve, st, ss, scale, sums, summed, var, root, rstd):
    dve.wait_ge(sums, summed)
    nc.vector.tensor_scalar(st[:, 0, :], ss, scale, EPS, ALU.mult, ALU.add).then_inc(var, 1)
    newton(nc, dve, st, root, rstd)


def newton(nc, dve, st, root, rstd):
    dve.wait_ge(root, 1)
    nc.vector.reciprocal(st[:, 2, :], st[:, 1, :]).then_inc(rstd, 1)
    dve.wait_ge(rstd, 1)
    nc.vector.tensor_tensor(st[:, 3, :], st[:, 2, :], st[:, 2, :], ALU.mult).then_inc(rstd, 1)
    dve.wait_ge(rstd, 2)
    nc.vector.tensor_tensor(st[:, 1, :], st[:, 3, :], st[:, 0, :], ALU.mult).then_inc(rstd, 1)
    dve.wait_ge(rstd, 3)
    nc.vector.tensor_scalar(st[:, 3, :], st[:, 1, :], -0.5, 1.5, ALU.mult, ALU.add).then_inc(rstd, 1)
    dve.wait_ge(rstd, 4)
    nc.vector.tensor_tensor(st[:, 2, :], st[:, 2, :], st[:, 3, :], ALU.mult).then_inc(rstd, 1)
    dve.wait_ge(rstd, 5)


def norm_transpose(nc, env, tag, g_dram, load_x=None, src=None):
    X, Thi, Tlo, ident = env["X"], env["Thi"], env["Tlo"], env["ident"]
    with ExitStack() as ctx:
        def sem(n):
            return new_sem(nc, env, f"{tag}_{n}")

        if src is None:
            mem = Mem(nc, Map.Z, Map.T)
            xn = mem.take(f"{tag}_xn", [P, 4, D], F32)
            junk = mem.take(f"{tag}_junk", [P, RT, D], F32)
            g = mem.take(f"{tag}_g", [P, KC], F32)
            ss = mem.take(f"{tag}_ss", [P, RT], F32)
            st = mem.take(f"{tag}_st", [P, 4, RT], F32)
        ps = [ctx.enter_context(nc.psum_tensor(f"{tag}_ps{i}", [P, NB], F32)) for i in range(4)]
        x_in, g_in, sums, var, root, rstd, xn_ready = map(sem, ("x_in", "g_in", "sums", "var", "root", "rstd", "xn_ready"))
        turned, hi_done, lo_done = map(sem, ("turned", "hi_done", "lo_done"))
        banks = [(half, k) for half in range(2) for k in range(KC)]
        block = ctx.enter_context(nc.Block())

        @block.sync
        def _(sp):
            if src is None:
                if load_x is not None:
                    for r in range(RT):
                        sp.dma_start(X[:, r, :], load_x[r * P:(r + 1) * P, :]).then_inc(x_in, 16)
                sp.dma_start(g[:, :], g_dram.rearrange("(k p) -> p k", p=P), allow_slow_non_contiguous=True).then_inc(g_in, 16)

        @block.vector
        def _(dve):
            if src is None:
                for r in range(1, RT, 2):
                    if load_x is not None:
                        dve.wait_ge(x_in, 16 * RT)
                    nc.vector.tensor_tensor_reduce(junk[:, r, :], X[:, r, :], X[:, r, :], 1.0, 0.0, ALU.mult,
                                                   ALU.add, ss[:, r:r + 1]).then_inc(sums, 1)
                newton_rstd(nc, dve, st, ss[:, :], 1.0 / D, sums, RT, var, root, rstd)
                dve.wait_ge(g_in, 16)
            for n, (half, k) in enumerate(banks):
                if src is None and k == 0:
                    if half:
                        dve.wait_ge(turned, KC)
                    for r in range(4):
                        nc.vector.tensor_scalar(xn[:, r, :], X[:, 4 * half + r, :], st[:, 2, 4 * half + r:4 * half + r + 1],
                                                None, ALU.mult).then_inc(xn_ready, 1)
                dve.wait_ge(hi_done, n + 1)
                lo, hi = Tlo[:, k, half * NB:(half + 1) * NB], f32(Thi[:, k, half * NB:(half + 1) * NB])
                if src is None:
                    nc.vector.scalar_tensor_tensor(lo, ps[n % 4][:, :], g[:, k:k + 1], hi, ALU.mult,
                                                   ALU.subtract).then_inc(lo_done, 1)
                else:
                    nc.vector.tensor_tensor(lo, ps[n % 4][:, :], hi, ALU.subtract).then_inc(lo_done, 1)

        @block.scalar
        def _(act):
            if src is None:
                for r in range(0, RT, 2):
                    if load_x is not None:
                        act.wait_ge(x_in, 16 * RT)
                    nc.scalar.activation(junk[:, r, :], X[:, r, :], ACT.Square, accum_out=ss[:, r:r + 1]).then_inc(sums, 1)
                act.wait_ge(var, 1)
                nc.scalar.activation(st[:, 1, :], st[:, 0, :], ACT.Sqrt).then_inc(root, 1)
                act.wait_ge(g_in, 16)
            for n, (half, k) in enumerate(banks):
                act.wait_ge(turned, n + 1)
                hi = Thi[:, k, half * NB:(half + 1) * NB]
                if src is None:
                    nc.scalar.activation(hi, ps[n % 4][:, :], ACT.Copy, scale=g[:, k:k + 1]).then_inc(hi_done, 1)
                else:
                    nc.scalar.activation(hi, ps[n % 4][:, :], ACT.Copy).then_inc(hi_done, 1)

        @block.tensor
        def _(pe):
            for n, (half, k) in enumerate(banks):
                if src is None and k == 0:
                    pe.wait_ge(xn_ready, 4 * half + 4)
                if n >= 4:
                    pe.wait_ge(lo_done, n - 3)
                for r in range(4):
                    rows = xn[:, r, k * P:(k + 1) * P] if src is None else src(4 * half + r, k)
                    last = nc.tensor.transpose(ps[n % 4][:, r * P:(r + 1) * P], rows, ident[:, :])
                last.then_inc(turned, 1)


def constants(nc, env):
    with ExitStack() as ctx:
        made = new_sem(nc, env, "const_made")
        ident = env["ident"]
        block = ctx.enter_context(nc.Block())

        @block.gpsimd
        def _(pool):
            nc.gpsimd.memset(ident[:, :], 0.0).then_inc(made, 1)
            pool.wait_ge(made, 1)
            nc.gpsimd.affine_select(out=ident[:, :], in_=ident[:, :], compare_op=ALU.not_equal, fill=1.0, base=0,
                                    pattern=[[-1, P]], channel_multiplier=1).then_inc(made, 1)

        @block.vector
        def _(dve):
            dve.wait_ge(made, 2)
            nc.vector.tensor_scalar(env["barring"][:, :], ident[:, :], OFF, None, ALU.mult).then_inc(made, 1)


def project(nc, env, tag, w, width, dest, add=False, cols=None, side=None):
    Thi, Tlo = env["Thi"], env["Tlo"]
    full, tail = divmod(width, NB)
    RAW, RING, LEAD = 4, 4, 3
    with ExitStack() as ctx:
        def sem(n):
            return new_sem(nc, env, f"{tag}_{n}")

        mem = Mem(nc, Map.W, Map.SMALL)
        raw = mem.take(f"{tag}_raw", [P, RAW, NB], F32)
        whi = mem.take(f"{tag}_whi", [P, RING, NB], F32R)
        wlo = mem.take(f"{tag}_wlo", [P, RING, NB], F32R)
        ps = [ctx.enter_context(nc.psum_tensor(f"{tag}_ps{i}", [P, NB], F32)) for i in range(RT)]
        w_in = [sem(f"w_in{i}") for i in range(RAW)]
        hi_done, lo_done, used, summed, out_act, out_dve = map(
            sem, ("hi_done", "lo_done", "used", "summed", "out_act", "out_dve"))
        block = ctx.enter_context(nc.Block())

        widths = [NB] * full + ([tail] if tail else [])
        if cols:
            widths = [n for _, n in cols]

        def at(b, n):
            return bass.ds(b * NB, n) if not cols else slice(cols[b][0], cols[b][0] + n)

        def blocks(eng, step):
            step(0, widths[0], widths[1])
            if full > 3 and not cols:
                with eng.Fori(1, full - 1) as b:
                    step(b, NB, NB)
                rest = range(full - 1, len(widths))
            else:
                rest = range(1, len(widths))
            for b in rest:
                step(b, widths[b], widths[b + 1] if b + 1 < len(widths) else 0)

        def chunks(split, b, n, after):
            if isinstance(b, int) and b == 0:
                for k in range(LEAD):
                    split(b, k, n)
            for k in range(LEAD, KC):
                split(b, k, n)
            if after:
                for k in range(LEAD):
                    split(b + 1, k, after)

        @block.sync
        def _(sp):
            if side:
                side.load(sp)

            def step(b, n, after):
                for k in range(KC):
                    if not (isinstance(b, int) and b == 0 and k < RAW):
                        sp.wait_ge(lo_done, KC * b + k - RAW + 1)
                    sp.dma_start(raw[:, k % RAW, 0:n], w[k * P:(k + 1) * P, at(b, n)]).then_inc(w_in[k % RAW], 16)
            blocks(sp, step)

        @block.scalar
        def _(act):
            def split(b, k, n):
                act.wait_ge(w_in[k % RAW], (b * (KC // RAW) + k // RAW + 1) * 16)
                if k >= RING:
                    act.wait_ge(used, (KC - 1) * b + k - RING + 1)
                elif not (isinstance(b, int) and b == 0):
                    if k < RING - 1:
                        act.wait_ge(used, (KC - 1) * (b - 1) + KC + k - RING + 1)
                    else:
                        act.wait_ge(summed, RT * b)
                nc.scalar.activation(whi[:, k % RING, 0:n], raw[:, k % RAW, 0:n], ACT.Copy).then_inc(hi_done, 1)
                if side:
                    side.scalar(act, b, k)

            def step(b, n, after):
                chunks(split, b, n, after)
                if add:
                    return
                for r in range(0, RT, 2):
                    act.wait_ge(summed, RT * b + r + 1)
                    nc.scalar.activation(dest[:, r, at(b, n)], ps[r][:, 0:n], ACT.Copy).then_inc(out_act, 1)
            blocks(act, step)

        @block.vector
        def _(dve):
            def split(b, k, n):
                dve.wait_ge(hi_done, KC * b + k + 1)
                nc.vector.tensor_tensor(wlo[:, k % RING, 0:n], raw[:, k % RAW, 0:n], f32(whi[:, k % RING, 0:n]),
                                        ALU.subtract).then_inc(lo_done, 1)
                if side:
                    side.vector(dve, b, k, out_act, out_dve)

            def step(b, n, after):
                chunks(split, b, n, after)
                for r in range(0 if add else 1, RT, 1 if add else 2):
                    dve.wait_ge(summed, RT * b + r + 1)
                    to = dest[:, r, at(b, n)]
                    if add:
                        nc.vector.tensor_tensor(to, ps[r][:, 0:n], to, ALU.add).then_inc(out_dve, 1)
                    else:
                        nc.vector.tensor_copy(to, ps[r][:, 0:n]).then_inc(out_dve, 1)
            blocks(dve, step)

        @block.tensor
        def _(pe):
            def step(b, n, after):
                for k in range(KC):
                    pe.wait_ge(lo_done, KC * b + k + 1)
                    hi, lo = whi[:, k % RING, 0:n], wlo[:, k % RING, 0:n]
                    for r in range(RT):
                        if k == 0 and not (isinstance(b, int) and b == 0):
                            if add:
                                pe.wait_ge(out_dve, RT * (b - 1) + r + 1)
                            else:
                                pe.wait_ge(out_dve if r % 2 else out_act, RT // 2 * (b - 1) + r // 2 + 1)
                        rows = slice(r * P, (r + 1) * P)
                        nc.tensor.matmul(ps[r][:, 0:n], Thi[:, k, rows], hi, start=(k == 0), stop=False)
                        nc.tensor.matmul(ps[r][:, 0:n], Thi[:, k, rows], lo, start=False, stop=False)
                        last = nc.tensor.matmul(ps[r][:, 0:n], Tlo[:, k, rows], hi, start=False, stop=(k == KC - 1))
                        if k == KC - 1:
                            last.then_inc(summed, 1)
                        elif r == RT - 1:
                            last.then_inc(used, 1)
            blocks(pe, step)


def mlp(nc, env, tag, w_up, w_down):
    X, Thi, Tlo = env["X"], env["Thi"], env["Tlo"]
    NBLK = FC // 2
    HEAD, BODY = 3, 6
    with ExitStack() as ctx:
        def sem(n):
            return new_sem(nc, env, f"{tag}_{n}")

        mem = Mem(nc, Map.Z, Map.T)
        uhi = mem.take(f"{tag}_uhi", [P, 4, SEQ], F32R)
        ulo = mem.take(f"{tag}_ulo", [P, 4, SEQ], F32R)
        dhi = mem.take(f"{tag}_dhi", [P, 4, D], F32R)
        dlo = mem.take(f"{tag}_dlo", [P, 4, D], F32R)
        relu = mem.take(f"{tag}_relu", [P, 4, NB], F32)
        mem = Mem(nc, Map.W, Map.SMALL)
        raw = mem.take(f"{tag}_raw", [P, 4, D], F32)
        phi = mem.take(f"{tag}_phi", [P, 2, D], F32R)
        plo = mem.take(f"{tag}_plo", [P, 2, D], F32R)
        psu = [ctx.enter_context(nc.psum_tensor(f"{tag}_psu{i}", [P, NB], F32)) for i in range(4)]
        psd = [ctx.enter_context(nc.psum_tensor(f"{tag}_psd{i}", [P, NB], F32)) for i in range(4)]
        up_in = [sem(f"up_in{i}") for i in range(2)]
        down_in = [sem(f"down_in{i}") for i in range(2)]
        up_hi, up_lo, down_hi, down_lo = map(sem, ("up_hi", "up_lo", "down_hi", "down_lo"))
        up_sum, relu_done, square, u_hi, u_lo, down_sum, added = map(
            sem, ("up_sum", "relu_done", "square", "u_hi", "u_lo", "down_sum", "added"))
        block = ctx.enter_context(nc.Block())
        up_v = w_up.rearrange("(k p) f -> p k f", p=P)

        def first(b, count=1):
            return isinstance(b, int) and b < count

        def blocks(eng, step):
            for b in range(HEAD):
                step(b, b % 2)
            with eng.Fori(0, BODY) as j:
                step(2 * j + HEAD, HEAD % 2)
                step(2 * j + HEAD + 1, (HEAD + 1) % 2)
            for b in range(HEAD + 2 * BODY, NBLK):
                step(b, b % 2)

        @block.sync
        def _(sp):
            def step(b, s):
                for c in range(2):
                    if not first(b):
                        sp.wait_ge(up_lo, 2 * b - 1 + c)
                    sp.dma_start(raw[:, c, :].rearrange("p (k f) -> p k f", k=KC),
                                 up_v[:, :, bass.ds((2 * b + c) * P, P)]).then_inc(up_in[c], 16)
                for c in range(2):
                    if not first(b):
                        sp.wait_ge(down_lo, 2 * b - 1 + c)
                    sp.dma_start(raw[:, 2 + c, :], w_down[bass.ds((2 * b + c) * P, P), :]).then_inc(down_in[c], 16)
            blocks(sp, step)

        @block.scalar
        def _(act):
            def split_up(b, c):
                act.wait_ge(up_in[c], 16 * (b + 1))
                if not first(b):
                    act.wait_ge(up_sum, 4 * b - 2 + 2 * c)
                nc.scalar.activation(phi[:, c, :], raw[:, c, :], ACT.Copy).then_inc(up_hi, 1)

            def step(b, s):
                if first(b):
                    split_up(b, 0)
                    split_up(b, 1)
                for n in range(4):
                    c, half = divmod(n, 2)
                    act.wait_ge(up_sum, 4 * b + n + 1)
                    if not first(b):
                        act.wait_ge(u_lo, 4 * b + n - 3)
                    nc.scalar.activation(relu[:, n, :], psu[n][:, :], ACT.Relu).then_inc(relu_done, 1)
                    if half:
                        if not (isinstance(b, int) and b == NBLK - 1):
                            split_up(b + 1, c)
                    act.wait_ge(square, 4 * b + n + 1)
                    if n == 0 and not first(b, 2):
                        act.wait_ge(down_sum, 16 * (b - 1))
                    nc.scalar.activation(uhi[:, 2 * s + c, half * NB:(half + 1) * NB], relu[:, n, :],
                                         ACT.Copy).then_inc(u_hi, 1)
                for c in range(2):
                    act.wait_ge(down_in[c], 16 * (b + 1))
                    nc.scalar.activation(dhi[:, 2 * s + c, :], raw[:, 2 + c, :], ACT.Copy).then_inc(down_hi, 1)
            blocks(act, step)

        @block.vector
        def _(dve):
            def split_up(b, c):
                dve.wait_ge(up_hi, 2 * b + c + 1)
                nc.vector.tensor_tensor(plo[:, c, :], raw[:, c, :], f32(phi[:, c, :]), ALU.subtract).then_inc(up_lo, 1)

            def add_down(b, first_group, count):
                for n in range(first_group, first_group + count):
                    r, half = divmod(n, 2)
                    dve.wait_ge(down_sum, 16 * b + n + 1)
                    to = X[:, r, half * NB:(half + 1) * NB]
                    nc.vector.tensor_tensor(to, psd[n % 4][:, :], to, ALU.add).then_inc(added, 1)

            def step(b, s):
                if first(b):
                    split_up(b, 0)
                    split_up(b, 1)
                for n in range(4):
                    c, half = divmod(n, 2)
                    dve.wait_ge(relu_done, 4 * b + n + 1)
                    nc.vector.tensor_tensor(relu[:, n, :], relu[:, n, :], relu[:, n, :], ALU.mult).then_inc(square, 1)
                    dve.wait_ge(u_hi, 4 * b + n + 1)
                    part = slice(half * NB, (half + 1) * NB)
                    nc.vector.tensor_tensor(ulo[:, 2 * s + c, part], relu[:, n, :], f32(uhi[:, 2 * s + c, part]),
                                            ALU.subtract).then_inc(u_lo, 1)
                    if half and not (isinstance(b, int) and b == NBLK - 1):
                        split_up(b + 1, c)
                for c in range(2):
                    dve.wait_ge(down_hi, 2 * b + c + 1)
                    nc.vector.tensor_tensor(dlo[:, 2 * s + c, :], raw[:, 2 + c, :], f32(dhi[:, 2 * s + c, :]),
                                            ALU.subtract).then_inc(down_lo, 1)
                if not first(b):
                    add_down(b - 1, 0, 16)
            blocks(dve, step)
            add_down(NBLK - 1, 0, 16)

        @block.tensor
        def _(pe):
            def up(b, s):
                for c in range(2):
                    pe.wait_ge(up_lo, 2 * b + c + 1)
                    for half in range(2):
                        n = 2 * c + half
                        if not first(b):
                            pe.wait_ge(relu_done, 4 * b + n - 3)
                        cols = slice(half * NB, (half + 1) * NB)
                        for k in range(KC):
                            hi, lo = phi[:, c, k * P:(k + 1) * P], plo[:, c, k * P:(k + 1) * P]
                            nc.tensor.matmul(psu[n][:, :], hi, Thi[:, k, cols], start=(k == 0), stop=False)
                            nc.tensor.matmul(psu[n][:, :], hi, Tlo[:, k, cols], start=False, stop=False)
                            last = nc.tensor.matmul(psu[n][:, :], lo, Thi[:, k, cols], start=False, stop=(k == KC - 1))
                        last.then_inc(up_sum, 1)

            def down(b, s):
                pe.wait_ge(u_lo, 4 * b + 4)
                pe.wait_ge(down_lo, 2 * b + 2)
                for n in range(16):
                    r, half = divmod(n, 2)
                    if not (first(b) and n < 4):
                        pe.wait_ge(added, 16 * b + n - 3)
                    rows, cols = slice(r * P, (r + 1) * P), slice(half * NB, (half + 1) * NB)
                    for c in range(2):
                        q = 2 * s + c
                        nc.tensor.matmul(psd[n % 4][:, :], uhi[:, q, rows], dhi[:, q, cols], start=(c == 0), stop=False)
                        nc.tensor.matmul(psd[n % 4][:, :], uhi[:, q, rows], dlo[:, q, cols], start=False, stop=False)
                        last = nc.tensor.matmul(psd[n % 4][:, :], ulo[:, q, rows], dhi[:, q, cols], start=False, stop=(c == 1))
                    last.then_inc(down_sum, 1)

            def step(b, s):
                up(b, s)
                if not first(b):
                    down(b - 1, 1 - s)
            blocks(pe, step)
            down(NBLK - 1, (NBLK - 1) % 2)


def final_norm(nc, env, g_dram, out):
    X = env["X"]
    with ExitStack() as ctx:
        def sem(n):
            return new_sem(nc, env, f"final_{n}")

        mem = Mem(nc, Map.Z, Map.W)
        y = mem.take("final_y", [P, RT, D], F32)
        g = mem.take("final_g", [P, D], F32)
        ss = mem.take("final_ss", [P, RT], F32)
        st = mem.take("final_st", [P, 4, RT], F32)
        g_in, sums, var, root, rstd, y_done, y_out = map(sem, ("g_in", "sums", "var", "root", "rstd", "y_done", "y_out"))
        block = ctx.enter_context(nc.Block())

        @block.sync
        def _(sp):
            sp.dma_start(g[:, :], g_dram.rearrange("(a d) -> a d", a=1).broadcast_to([P, D])).then_inc(g_in, 16)
            for r in range(RT):
                sp.wait_ge(y_done, r + 1)
                sp.dma_start(out[r * P:(r + 1) * P, :], y[:, r, :]).then_inc(y_out, 16)
            sp.wait_ge(y_out, 16 * RT)

        @block.scalar
        def _(act):
            for r in range(0, RT, 2):
                nc.scalar.activation(y[:, r, :], X[:, r, :], ACT.Square, accum_out=ss[:, r:r + 1]).then_inc(sums, 1)
            act.wait_ge(var, 1)
            nc.scalar.activation(st[:, 1, :], st[:, 0, :], ACT.Sqrt).then_inc(root, 1)

        @block.vector
        def _(dve):
            for r in range(1, RT, 2):
                nc.vector.tensor_tensor_reduce(y[:, r, :], X[:, r, :], X[:, r, :], 1.0, 0.0, ALU.mult,
                                               ALU.add, ss[:, r:r + 1]).then_inc(sums, 1)
            newton_rstd(nc, dve, st, ss[:, :], 1.0 / D, sums, RT, var, root, rstd)
            dve.wait_ge(g_in, 16)
            for r in range(RT):
                nc.vector.scalar_tensor_tensor(y[:, r, :], X[:, r, :], st[:, 2, r:r + 1], g[:, :], ALU.mult,
                                               ALU.mult).then_inc(y_done, 1)



def spread(ap, shape):
    return ap.broadcast_to(shape)


def rotary_tables(nc, env, positions):
    cos, sin = env["cos"], env["sin"]
    freq = [float(np.float32(THETA ** (-2.0 * i / ROT))) for i in range(NF)]
    two_pi = 2.0 * np.pi
    c1 = 6.28125
    c2 = round((two_pi - c1) * 2 ** 17) / 2.0 ** 17
    c3 = float(np.float32(two_pi - c1 - c2))
    to_int = 1.5 * 2 ** 23
    lim = float(np.nextafter(np.float32(np.pi), np.float32(0)))
    with ExitStack() as ctx:
        mem = Mem(nc, Map.W, Map.SMALL)
        pos_i = mem.take("rot_pos_i", [P, RT], I32)
        pos = mem.take("rot_pos", [P, RT], F32)
        ang, mult, r, arg = (mem.take(f"rot_{n}", [P, RT, NF], F32) for n in ("ang", "mult", "r", "arg"))
        pos_in, made, r_done, arg_done, tables = (new_sem(nc, env, f"rot_{n}") for n in (
            "pos_in", "made", "r_done", "arg_done", "tables"))
        block = ctx.enter_context(nc.Block())

        @block.sync
        def _(sp):
            sp.dma_start(pos_i[:, :], positions.rearrange("(r p) -> p r", p=P),
                         allow_slow_non_contiguous=True).then_inc(pos_in, 16)

        @block.vector
        def _(dve):
            dve.wait_ge(pos_in, 16)
            nc.vector.tensor_copy(pos[:, :], pos_i[:, :]).then_inc(made, 1)
            dve.wait_ge(made, 1)
            for f in range(NF):
                nc.vector.tensor_scalar(ang[:, :, f], pos[:, :], freq[f], None, ALU.mult).then_inc(made, 1)
            dve.wait_ge(made, 1 + NF)
            nc.vector.tensor_scalar(mult[:, :, :], ang[:, :, :], 1.0 / two_pi, to_int, ALU.mult, ALU.add).then_inc(made, 1)
            dve.wait_ge(made, 2 + NF)
            nc.vector.tensor_scalar(mult[:, :, :], mult[:, :, :], to_int, None, ALU.subtract).then_inc(made, 1)
            for n, c in enumerate((c1, c2, c3)):
                dve.wait_ge(made, 3 + NF + n)
                nc.vector.scalar_tensor_tensor(r[:, :, :], mult[:, :, :], -c, (r if n else ang)[:, :, :], ALU.mult,
                                               ALU.add).then_inc(made, 1)
            dve.wait_ge(made, 6 + NF)
            nc.vector.tensor_scalar(r[:, :, :], r[:, :, :], lim, -lim, ALU.min, ALU.max).then_inc(r_done, 1)
            dve.wait_ge(r_done, 1)
            nc.vector.scalar_tensor_tensor(arg[:, :, :], r[:, :, :], -1.0, r[:, :, :], ALU.mult, ALU.min).then_inc(made, 1)
            dve.wait_ge(made, 7 + NF)
            nc.vector.tensor_scalar(arg[:, :, :], arg[:, :, :], float(np.pi / 2), None, ALU.add).then_inc(arg_done, 1)

        @block.scalar
        def _(act):
            act.wait_ge(r_done, 1)
            nc.scalar.activation(sin[:, :, :], r[:, :, :], ACT.Sin).then_inc(tables, 1)
            act.wait_ge(arg_done, 1)
            nc.scalar.activation(cos[:, :, :], arg[:, :, :], ACT.Sin).then_inc(tables, 1)


def rotate(nc, eng, env, z, col, heads, tmp, done, base, tiles=range(RT)):
    if base:
        eng.wait_ge(done, base)
    parts = []
    for n, r in enumerate(tiles):
        v = z[:, r, col:col + heads * HD].rearrange("p (h d) -> p h d", d=HD)
        t1, t2 = v[:, :, 0:NF], v[:, :, NF:ROT]
        c = spread(env["cos"][:, r, :].unsqueeze(1), [P, heads, NF])
        s = spread(env["sin"][:, r, :].unsqueeze(1), [P, heads, NF])
        q = [tmp[:, 4 * n + j, 0:heads * NF].rearrange("p (h f) -> p h f", f=NF) for j in range(4)]
        for j, (a, b) in enumerate(((t1, c), (t2, s), (t2, c), (t1, s))):
            eng.tensor_tensor(q[j], a, b, ALU.mult).then_inc(done, 1)
        parts.append((t1, t2, q))
    for n, (t1, t2, q) in enumerate(parts):
        if n == 0:
            eng.wait_ge(done, base + 4 * len(parts))
        eng.tensor_tensor(t1, q[0], q[1], ALU.subtract).then_inc(done, 1)
        eng.tensor_tensor(t2, q[2], q[3], ALU.add).then_inc(done, 1)


def window_attention(nc, env, sinks):
    Z, ident = env["Z"], env["ident"]
    KW = CHUNK + SEQ
    with ExitStack() as ctx:
        def sem(n):
            return new_sem(nc, env, f"wa_{n}")

        mem = Mem(nc, Map.T, Map.SMALL)
        tmp = mem.take("wa_tmp", [P, 4 * RT, 10 * NF], F32)
        kdup = mem.take("wa_kdup", [P, RT, A_KV, 2, HD], F32)
        kT = mem.take("wa_kT", [P, A_KV, KW], F32)
        vs = mem.take("wa_vs", [P, RT, P], F32)
        qT = mem.take("wa_qT", [P, 2, 4, P], F32)
        prob = mem.take("wa_prob", [P, 2, 2, 4, P], F32)
        probT = mem.take("wa_probT", [P, 2, 8, P], F32)
        sink = mem.take("wa_sink", [P, A_HEADS], F32)
        mx = mem.take("wa_mx", [P, RT, 2, 4], F32)
        esink = mem.take("wa_esink", [P, RT, 2, 4], F32)
        den = mem.take("wa_den", [P, RT, 2, 4], F32)
        ps_s = [ctx.enter_context(nc.psum_tensor(f"wa_ps_s{i}", [P, 4, P], F32)) for i in range(2)]
        ps_t = [ctx.enter_context(nc.psum_tensor(f"wa_ps_t{i}", [P, 4, P], F32)) for i in range(2)]
        ps_q = [ctx.enter_context(nc.psum_tensor(f"wa_ps_q{i}", [P, 4, P], F32)) for i in range(2)]
        ps_o = [ctx.enter_context(nc.psum_tensor(f"wa_ps_o{i}", [P, 8, HD], F32)) for i in range(2)]
        (sink_in, rotated, dup, vs_zero, vs_in, k_zero, k_turned, kT_done, q_turned, qT_done, scored, masked, maxed,
         shifted, expd, sunk, summed, inverted, p_turned, pT_done, mixed, written) = map(sem, (
             "sink_in", "rotated", "dup", "vs_zero", "vs_in", "k_zero", "k_turned", "kT_done", "q_turned", "qT_done",
             "scored", "masked", "maxed", "shifted", "expd", "sunk", "summed", "inverted", "p_turned", "pT_done",
             "mixed", "written"))
        block = ctx.enter_context(nc.Block())
        ROTS = 6 * RT

        @block.sync
        def _(sp):
            sp.dma_start(sink[:, :], spread(sinks.rearrange("(a d) -> a d", a=1), [P, A_HEADS])).then_inc(sink_in, 16)
            sp.dma_start(vs[CHUNK:P, :, :], Z[0:CHUNK, :, EV:EV + P]).then_inc(vs_in, 16)
            sp.dma_start(vs[0:CHUNK, 1:RT, :], Z[CHUNK:P, 0:RT - 1, EV:EV + P]).then_inc(vs_in, 16)

        @block.gpsimd
        def _(pool):
            nc.gpsimd.memset(vs[0:CHUNK, 0, :], 0.0).then_inc(vs_zero, 1)
            nc.gpsimd.memset(kT[:, :, 0:CHUNK], 0.0).then_inc(k_zero, 1)

        @block.vector
        def _(dve):
            rotate(nc, nc.vector, env, Z, EQ, A_HEADS + A_KV, tmp, rotated, 0)
            dve.wait_ge(rotated, ROTS)
            for g in range(A_KV):
                for c in range(2):
                    nc.vector.tensor_copy(kdup[:, :, g, c, :], Z[:, :, EK + g * HD:EK + (g + 1) * HD]).then_inc(dup, 1)
            dve.wait_ge(sink_in, 16)

            def finish(i):
                dve.wait_ge(mixed, i + 1)
                dve.wait_ge(inverted, 2 * i + 2)
                rinv = spread(den[:, i, :, :].rearrange("p a c -> p c a").unsqueeze(3), [P, 4, 2, HD])
                nc.vector.tensor_tensor(Z[:, i, 0:NB].rearrange("p (c a d) -> p c a d", c=4, a=2),
                                        ps_o[i % 2][:, :, :].rearrange("p (c a) d -> p c a d", a=2), rinv,
                                        ALU.mult).then_inc(written, 1)

            for i in range(RT):
                dve.wait_ge(scored, i + 1)
                if i == 0:
                    for a in range(2):
                        nc.vector.memset(ps_s[a][0:CHUNK, :, 0:CHUNK], -1e30).then_inc(masked, 1)
                    dve.wait_ge(masked, 2)
                for a in range(2):
                    nc.vector.tensor_reduce(mx[:, i, a, :], ps_s[a][:, :, :], AX.X, ALU.max).then_inc(maxed, 1)
                dve.wait_ge(maxed, 3 * i + 2)
                nc.vector.tensor_tensor(mx[:, i, :, :], mx[:, i, :, :], sink[:, :].rearrange("p (c a) -> p a c", a=2),
                                        ALU.max).then_inc(maxed, 1)
                dve.wait_ge(maxed, 3 * i + 3)
                if i >= 2:
                    dve.wait_ge(p_turned, 2 * i - 2)
                for a in range(2):
                    nc.vector.tensor_tensor(prob[:, i % 2, a, :, :], ps_s[a][:, :, :],
                                            spread(mx[:, i, a, :].unsqueeze(2), [P, 4, P]), ALU.subtract).then_inc(shifted, 1)
                nc.vector.tensor_tensor(esink[:, i, :, :], sink[:, :].rearrange("p (c a) -> p a c", a=2), mx[:, i, :, :],
                                        ALU.subtract).then_inc(shifted, 1)
                if i >= 1:
                    finish(i - 1)
                dve.wait_ge(expd, 2 * i + 2)
                for a in range(2):
                    nc.vector.tensor_reduce(den[:, i, a, :], prob[:, i % 2, a, :, :], AX.X, ALU.add).then_inc(summed, 1)
                dve.wait_ge(summed, 2 * i + 2)
                dve.wait_ge(sunk, i + 1)
                nc.vector.tensor_tensor(den[:, i, :, :], den[:, i, :, :], esink[:, i, :, :], ALU.add).then_inc(inverted, 1)
                dve.wait_ge(inverted, 2 * i + 1)
                nc.vector.reciprocal(den[:, i, :, :], den[:, i, :, :]).then_inc(inverted, 1)
            finish(RT - 1)

        @block.scalar
        def _(act):
            for g in range(A_KV):
                for half in range(2):
                    act.wait_ge(k_turned, 2 * g + half + 1)
                    nc.scalar.activation(kT[:, g, CHUNK + half * NB:CHUNK + (half + 1) * NB], ps_t[half][:, :, :],
                                         ACT.Copy).then_inc(kT_done, 1)
            def queries(i):
                act.wait_ge(q_turned, i + 1)
                if i >= 2:
                    act.wait_ge(scored, i - 1)
                nc.scalar.activation(qT[:, i % 2, :, :], ps_q[i % 2][:, :, :], ACT.Copy, scale=HD ** -0.5).then_inc(qT_done, 1)

            queries(0)
            queries(1)
            for i in range(RT):
                for a in range(2):
                    act.wait_ge(shifted, 3 * i + 1 + a)
                    nc.scalar.activation(prob[:, i % 2, a, :, :], prob[:, i % 2, a, :, :], ACT.Exp).then_inc(expd, 1)
                act.wait_ge(shifted, 3 * i + 3)
                nc.scalar.activation(esink[:, i, :, :], esink[:, i, :, :], ACT.Exp).then_inc(sunk, 1)
                if i + 2 < RT:
                    queries(i + 2)
                if i >= 2:
                    act.wait_ge(mixed, i - 1)
                for a in range(2):
                    act.wait_ge(p_turned, 2 * i + a + 1)
                    nc.scalar.activation(probT[:, i % 2, 4 * a:4 * a + 4, :], ps_t[a][:, :, :], ACT.Copy).then_inc(pT_done, 1)

        @block.tensor
        def _(pe):
            pe.wait_ge(dup, 2 * A_KV)
            for g in range(A_KV):
                for half in range(2):
                    if g:
                        pe.wait_ge(kT_done, half + 1)
                    for r in range(4):
                        last = nc.tensor.transpose(ps_t[half][:, r, :], kdup[:, 4 * half + r, g, :, :], ident[:, :])
                    last.then_inc(k_turned, 1)

            def queries(i):
                if i >= 2:
                    pe.wait_ge(qT_done, i - 1)
                for c in range(4):
                    last = nc.tensor.transpose(ps_q[i % 2][:, c, :], Z[:, i, c * P:(c + 1) * P], ident[:, :])
                last.then_inc(q_turned, 1)

            def scores(i):
                pe.wait_ge(qT_done, i + 1)
                if i:
                    pe.wait_ge(shifted, 3 * i - 1)
                for c in range(4):
                    for a in range(2):
                        g = (2 * c + a) // 4
                        rows = slice(a * CHUNK, (a + 1) * CHUNK)
                        for u in range(2):
                            at = i * P + u * CHUNK
                            last = nc.tensor.matmul(ps_s[a][u * CHUNK:(u + 1) * CHUNK, c, :],
                                                    qT[rows, i % 2, c, u * CHUNK:(u + 1) * CHUNK],
                                                    kT[rows, g, at:at + P], start=True, stop=True)
                last.then_inc(scored, 1)

            def turn(i):
                for a in range(2):
                    pe.wait_ge(expd, 2 * i + a + 1)
                    if i:
                        pe.wait_ge(pT_done, 2 * i - 1 + a)
                    for c in range(4):
                        last = nc.tensor.transpose(ps_t[a][:, c, :], prob[:, i % 2, a, c, :], ident[:, :])
                    last.then_inc(p_turned, 1)

            def mix(i):
                pe.wait_ge(pT_done, 2 * i + 2)
                if i >= 2:
                    pe.wait_ge(written, i - 1)
                for u in range(2):
                    for a in range(2):
                        for c in range(4):
                            h = 2 * c + a
                            g = h // 4
                            v = Z[:, i, EV + g * HD:EV + (g + 1) * HD] if u else vs[:, i, g * HD:(g + 1) * HD]
                            last = nc.tensor.matmul(ps_o[i % 2][u * CHUNK:(u + 1) * CHUNK, h, :],
                                                    probT[:, i % 2, 4 * a + c, u * CHUNK:(u + 1) * CHUNK], v,
                                                    start=True, stop=True)
                last.then_inc(mixed, 1)

            queries(0)
            queries(1)
            pe.wait_ge(kT_done, 4)
            pe.wait_ge(k_zero, 1)
            pe.wait_ge(vs_zero, 1)
            pe.wait_ge(vs_in, 32)
            for i in range(RT):
                scores(i)
                if i + 2 < RT:
                    queries(i + 2)
                if i:
                    mix(i - 1)
                turn(i)
            mix(RT - 1)


def mlstm(nc, env, t):
    Z, ident = env["Z"], env["ident"]
    H = B_HEADS
    NT = RT * (RT + 1) // 2
    with ExitStack() as ctx:
        def sem(n):
            return new_sem(nc, env, f"ml_{n}")

        mem = Mem(nc, Map.T, Map.SMALL)
        xT = mem.take("ml_xT", [P, 4, CONV - 1 + SEQ], F32)
        qk = mem.take("ml_qk", [P, 4, SEQ], F32)
        va = mem.take("ml_va", [P, RT, H, B_DV + 1], F32)
        fr, ir, br, mk, mk2 = (mem.take(f"ml_{n}", [H, SEQ], F32) for n in ("fr", "ir", "br", "mk", "mk2"))
        E = mem.take("ml_E", [P, 2, H, P], F32)
        Wt = mem.take("ml_W", [P, 2, H, P], F32)
        dg = mem.take("ml_dg", [P, H, P], F32)
        late = mem.take("ml_late", [P, P], F32)
        sel = mem.take("ml_sel", [H, H, P], F32)
        last_row = mem.take("ml_last_row", [P, P], F32)
        nat = mem.take("ml_nat", [P, 3, RT, H], F32)
        total = mem.take("ml_total", [P, RT, H], F32)
        G = mem.take("ml_G", [P, RT, RT, H], F32)
        emn = mem.take("ml_emn", [P, RT, H], F32)
        den = mem.take("ml_den", [P, RT, H], F32)
        cw = mem.take("ml_cw", [P, CONV, 4], F32)
        cb = mem.take("ml_cb", [P, 4], F32)
        bi = mem.take("ml_bi", [H, 2], F32)
        ps_s = [ctx.enter_context(nc.psum_tensor(f"ml_ps_s{i}", [P, 2, NB], F32)) for i in range(2)]
        ps_n = ctx.enter_context(nc.psum_tensor("ml_ps_n", [P, 2, NB], F32))
        ps_a = ctx.enter_context(nc.psum_tensor("ml_ps_a", [P, H, P], F32))
        ps_x = ctx.enter_context(nc.psum_tensor("ml_ps_x", [P, NB], F32))
        (par_in, consts, padded, x_turned, xT_done, conved, silu_s, gate_s, silu_m, g_turned, gates_in, ga, ge, gl,
         gd, mark, back, back_done, tot_mm, tot_done, G_done, emn_sum, emn_done, va_done, a_bc, dg_done, e_done,
         s_done, w_done, mixed, den_abs, den_max, den_inv, written) = map(sem, (
             "par_in", "consts", "padded", "x_turned", "xT_done", "conved", "silu_s", "gate_s", "silu_m", "g_turned",
             "gates_in", "ga", "ge", "gl", "gd", "mark", "back", "back_done", "tot_mm", "tot_done", "G_done", "emn_sum",
             "emn_done", "va_done", "a_bc", "dg_done", "e_done", "s_done", "w_done", "mixed", "den_abs", "den_max",
             "den_inv", "written"))
        block = ctx.enter_context(nc.Block())
        pairs = [(i, j) for i in range(RT) for j in range(i + 1)]
        rows = [fr, ir]
        xbanks = [(c, half) for c in range(4) for half in range(2)]

        @block.sync
        def _(sp):
            sp.dma_start(cw[:, :, :], t["even_conv_w"][0].rearrange("t (c p) -> p t c", p=P),
                         allow_slow_non_contiguous=True).then_inc(par_in, 16)
            sp.dma_start(cb[:, :], t["even_conv_b"][0].rearrange("(c p) -> p c", p=P),
                         allow_slow_non_contiguous=True).then_inc(par_in, 16)
            sp.dma_start(bi[:, 0:1], t["even_bias_f"][0].rearrange("(h o) -> h o", o=1)).then_inc(par_in, 16)
            sp.dma_start(bi[:, 1:2], t["even_bias_i"][0].rearrange("(h o) -> h o", o=1)).then_inc(par_in, 16)

        @block.gpsimd
        def _(pool):
            nc.gpsimd.memset(xT[:, :, 0:CONV - 1], 0.0).then_inc(padded, 1)
            nc.gpsimd.memset(sel[:, :, :], 0.0).then_inc(consts, 1)
            nc.gpsimd.memset(last_row[:, :], 0.0).then_inc(consts, 1)
            nc.gpsimd.memset(late[:, :], 0.0).then_inc(consts, 1)
            nc.gpsimd.memset(mk[:, :], 1.0).then_inc(mark, 1)
            pool.wait_ge(mark, 1)
            nc.gpsimd.memset(mk[:, 0:SEQ:P], 0.0).then_inc(mark, 1)
            pool.wait_ge(consts, 3)
            nc.gpsimd.affine_select(out=sel[:, :, :], in_=sel[:, :, :], compare_op=ALU.not_equal, fill=1.0, base=0,
                                    pattern=[[-1, H], [0, P]], channel_multiplier=1).then_inc(consts, 1)
            nc.gpsimd.affine_select(out=last_row[:, :], in_=last_row[:, :], compare_op=ALU.not_equal, fill=1.0,
                                    base=1 - P, pattern=[[0, P]], channel_multiplier=1).then_inc(consts, 1)
            nc.gpsimd.affine_select(out=late[:, :], in_=late[:, :], compare_op=ALU.is_ge, fill=1e30, base=0,
                                    pattern=[[1, P]], channel_multiplier=-1).then_inc(consts, 1)
            nc.gpsimd.memset(va[:, :, :, B_DV:B_DV + 1], 1.0).then_inc(va_done, 1)
            for r in range(RT):
                nc.gpsimd.tensor_copy(va[:, r, :, 0:B_DV],
                                      Z[:, r, EBV:EBV + H * B_DV].rearrange("p (h d) -> p h d", h=H)).then_inc(va_done, 1)

        @block.scalar
        def _(act):
            act.wait_ge(par_in, 64)
            for n in range(2):
                for half in range(2):
                    act.wait_ge(g_turned, 2 * n + half + 1)
                    nc.scalar.activation(rows[n][:, half * NB:(half + 1) * NB], ps_s[n][0:H, half, :], ACT.Identity,
                                         bias=bi[:, n:n + 1]).then_inc(gates_in, 1)
            for n, (c, half) in enumerate(xbanks):
                act.wait_ge(x_turned, n + 1)
                nc.scalar.activation(xT[:, c, CONV - 1 + half * NB:CONV - 1 + (half + 1) * NB], ps_n[:, half, :],
                                     ACT.Copy).then_inc(xT_done, 1)
            act.wait_ge(ga, 1)
            nc.scalar.activation(mk2[:, :], br[:, :], ACT.Exp, scale=-1.0).then_inc(ge, 1)
            act.wait_ge(ge, 1)
            nc.scalar.activation(mk2[:, :], mk2[:, :], ACT.Ln, bias=1.0).then_inc(gl, 1)
            for c in range(4):
                act.wait_ge(conved, CONV * (c + 1))
                nc.scalar.activation(xT[:, c, CONV - 1:], qk[:, c, :], ACT.Sigmoid).then_inc(silu_s, 1)
            for r in range(RT):
                o = Z[:, r, EBO:EBO + NB]
                nc.scalar.activation(o, o, ACT.Sigmoid).then_inc(gate_s, 1)
            act.wait_ge(back, 1)
            nc.scalar.activation(nat[:, :, :, :], ps_x[:, 0:3 * RT * H].rearrange("p (a r h) -> p a r h", a=3, r=RT),
                                 ACT.Copy).then_inc(back_done, 1)
            act.wait_ge(emn_sum, 1)
            nc.scalar.activation(emn[:, :, :], emn[:, :, :], ACT.Exp, scale=-1.0).then_inc(emn_done, 1)
            act.wait_ge(G_done, 2 * RT - 1)
            for n, (i, j) in enumerate(pairs):
                if j == 0:
                    act.wait_ge(dg_done, i + 1)
                if n >= 2:
                    act.wait_ge(w_done, n - 1)
                for a in range(2):
                    for c in range(2):
                        h = 2 * c + a
                        src = dg[:, h, :] if j == i else ps_a[:, h, :]
                        nc.scalar.activation(E[:, n % 2, 2 * a + c, :], src, ACT.Exp, scale=-1.0,
                                             bias=G[:, i, j, h:h + 1]).then_inc(e_done, 1)

        @block.vector
        def _(dve):
            dve.wait_ge(gates_in, 2)
            nc.vector.scalar_tensor_tensor(br[:, :], fr[:, :], -1.0, fr[:, :], ALU.mult, ALU.max).then_inc(ga, 1)
            dve.wait_ge(padded, 1)
            for c in range(4):
                dve.wait_ge(xT_done, 2 * c + 2)
                nc.vector.tensor_scalar(qk[:, c, :], xT[:, c, CONV - 1:], cw[:, CONV - 1, c:c + 1], cb[:, c:c + 1],
                                        ALU.mult, ALU.add).then_inc(conved, 1)
                for tap in range(CONV - 1):
                    dve.wait_ge(conved, CONV * c + 1 + tap)
                    nc.vector.scalar_tensor_tensor(qk[:, c, :], xT[:, c, tap:tap + SEQ], cw[:, tap, c:c + 1], qk[:, c, :],
                                                   ALU.mult, ALU.add).then_inc(conved, 1)
            dve.wait_ge(gl, 1)
            nc.vector.scalar_tensor_tensor(fr[:, :], fr[:, :], 0.0, mk2[:, :], ALU.min, ALU.subtract).then_inc(gd, 1)
            dve.wait_ge(gd, 1)
            dve.wait_ge(mark, 2)
            nc.vector.tensor_tensor_scan(br[:, :], mk[:, :], fr[:, :], 0.0, ALU.mult, ALU.add).then_inc(gd, 1)
            dve.wait_ge(gd, 2)
            dve.wait_ge(gates_in, 4)
            nc.vector.tensor_tensor(ir[:, :], ir[:, :], br[:, :], ALU.subtract).then_inc(gd, 1)
            nc.vector.memset(mk[:, :], 0.0).then_inc(gd, 1)
            dve.wait_ge(gd, 4)
            nc.vector.tensor_copy(mk[:, P:SEQ:P], br[:, P - 1:SEQ - 1:P]).then_inc(gd, 1)
            dve.wait_ge(gd, 5)
            nc.vector.tensor_tensor_scan(fr[:, :], mk[:, :], ir[:, :], 0.0, ALU.add, ALU.max).then_inc(gd, 1)
            for c in range(4):
                dve.wait_ge(silu_s, c + 1)
                nc.vector.tensor_tensor(qk[:, c, :], qk[:, c, :], xT[:, c, CONV - 1:], ALU.mult).then_inc(silu_m, 1)
            dve.wait_ge(back_done, 1)
            nc.vector.tensor_tensor(emn[:, :, :], nat[:, 1, :, :], nat[:, 2, :, :], ALU.add).then_inc(emn_sum, 1)
            dve.wait_ge(tot_mm, 1)
            nc.vector.tensor_copy(total[:, :, :], ps_x[:, P:P + RT * H].rearrange("p (r h) -> p r h", h=H)).then_inc(tot_done, 1)
            dve.wait_ge(tot_done, 1)
            for i in range(RT):
                if i:
                    dve.wait_ge(G_done, 2 * i - 1)
                    nc.vector.tensor_tensor(G[:, i, 0:i, :], G[:, i - 1, 0:i, :],
                                            spread(total[:, i - 1, :].unsqueeze(1), [P, i, H]), ALU.add).then_inc(G_done, 1)
                nc.vector.tensor_copy(G[:, i, i, :], nat[:, 0, i, :]).then_inc(G_done, 1)
            dve.wait_ge(consts, 6)

            def diagonal(i):
                dve.wait_ge(a_bc, i + 1)
                if i:
                    dve.wait_ge(e_done, 4 * pairs.index((i - 1, i - 1)) + 4)
                nc.vector.tensor_tensor(dg[:, :, :], ps_a[:, :, :], spread(late[:, :].unsqueeze(1), [P, H, P]),
                                        ALU.add).then_inc(dg_done, 1)

            def finish(i):
                dve.wait_ge(mixed, pairs.index((i, i)) + 1)
                num = ps_n[:, :, 0:2 * (B_DV + 1)].rearrange("p a (c d) -> p a c d", d=B_DV + 1)
                d = den[:, i, :].rearrange("p (a c) -> p a c", a=2)
                dve.wait_ge(emn_done, 1)
                nc.vector.scalar_tensor_tensor(d, num[:, :, :, B_DV], -1.0, emn[:, i, :].rearrange("p (c a) -> p a c", a=2),
                                               ALU.mult, ALU.max).then_inc(den_abs, 1)
                dve.wait_ge(den_abs, i + 1)
                nc.vector.tensor_tensor(d, num[:, :, :, B_DV], d, ALU.max).then_inc(den_max, 1)
                dve.wait_ge(den_max, i + 1)
                nc.vector.reciprocal(den[:, i, :], den[:, i, :]).then_inc(den_inv, 1)
                dve.wait_ge(den_inv, i + 1)
                dve.wait_ge(gate_s, RT)
                for a in range(2):
                    for c in range(2):
                        h = 2 * c + a
                        o = Z[:, i, EBO + h * B_DV:EBO + (h + 1) * B_DV]
                        nc.vector.scalar_tensor_tensor(o, num[:, a, c, 0:B_DV], den[:, i, 2 * a + c:2 * a + c + 1], o,
                                                       ALU.mult, ALU.mult).then_inc(written, 1)

            for n, (i, j) in enumerate(pairs):
                if j == 0:
                    diagonal(i)
                dve.wait_ge(s_done, n + 1)
                dve.wait_ge(e_done, 4 * n + 4)
                if n >= 2:
                    dve.wait_ge(mixed, n - 1)
                nc.vector.scalar_tensor_tensor(
                    Wt[:, n % 2, :, :], ps_s[n % 2][:, :, 0:2 * P], B_DK ** -0.5,
                    E[:, n % 2, :, :].rearrange("p (a c) t -> p a (c t)", a=2), ALU.mult, ALU.mult).then_inc(w_done, 1)
                if j == 0 and i:
                    finish(i - 1)
            finish(RT - 1)

        @block.tensor
        def _(pe):
            for n, col in enumerate((EBF, EBI)):
                for r in range(RT):
                    last = nc.tensor.transpose(ps_s[n][0:H, r // 4, (r % 4) * P:(r % 4 + 1) * P], Z[:, r, col:col + H],
                                               ident[:, :])
                    if r % 4 == 3:
                        last.then_inc(g_turned, 1)
            for n, (c, half) in enumerate(xbanks):
                if n >= 2:
                    pe.wait_ge(xT_done, n - 1)
                for r in range(4):
                    last = nc.tensor.transpose(ps_n[:, half, r * P:(r + 1) * P],
                                               Z[:, 4 * half + r, EBQK + c * P:EBQK + (c + 1) * P], ident[:, :])
                last.then_inc(x_turned, 1)
            pe.wait_ge(gd, 6)
            for n, row in enumerate((ir, br, fr)):
                for r in range(RT):
                    last = nc.tensor.transpose(ps_x[:, (n * RT + r) * H:(n * RT + r + 1) * H], row[:, r * P:(r + 1) * P],
                                               ident[0:H, 0:H])
            last.then_inc(back, 1)
            pe.wait_ge(back_done, 1)
            pe.wait_ge(consts, 6)
            nc.tensor.matmul(ps_x[:, P:P + RT * H], last_row[:, :], nat[:, 1, :, :], start=True, stop=True).then_inc(tot_mm, 1)

            def broadcast(i):
                if i:
                    pe.wait_ge(dg_done, i)
                if i > 1:
                    pe.wait_ge(e_done, 4 * pairs.index((i - 1, i - 1)))
                for h in range(H):
                    last = nc.tensor.matmul(ps_a[:, h, :], sel[:, h, :], fr[:, i * P:(i + 1) * P], start=True, stop=True)
                last.then_inc(a_bc, 1)

            def scores(n):
                i, j = pairs[n]
                if n >= 2:
                    pe.wait_ge(w_done, n - 1)
                for c in range(2):
                    for a in range(2):
                        part = slice(a * B_DK, (a + 1) * B_DK)
                        last = nc.tensor.matmul(ps_s[n % 2][:, a, c * P:(c + 1) * P],
                                                qk[part, 2 + c, j * P:(j + 1) * P], qk[part, c, i * P:(i + 1) * P],
                                                start=True, stop=True)
                last.then_inc(s_done, 1)

            def mix(n):
                i, j = pairs[n]
                pe.wait_ge(w_done, n + 1)
                if j == 0 and i:
                    pe.wait_ge(written, 4 * i)
                for a in range(2):
                    for c in range(2):
                        h = 2 * c + a
                        last = nc.tensor.matmul(ps_n[:, a, c * (B_DV + 1):(c + 1) * (B_DV + 1)],
                                                Wt[:, n % 2, 2 * a + c, :], va[:, j, h, :], start=(j == 0 and c == 0),
                                                stop=(j == i and c == 1), skip_group_check=True)
                last.then_inc(mixed, 1)

            pe.wait_ge(silu_m, 4)
            pe.wait_ge(va_done, 1 + RT)
            for n, (i, j) in enumerate(pairs):
                if j == 0:
                    broadcast(i)
                scores(n)
                if n:
                    mix(n - 1)
            mix(len(pairs) - 1)


def rotate_all(nc, eng, env, z, col, heads, tmp, done, base):
    v = z[:, :, col:col + heads * HD].rearrange("p r (h d) -> p r h d", d=HD)
    t1, t2 = v[:, :, :, 0:NF], v[:, :, :, NF:ROT]
    c = spread(env["cos"][:, :, :].unsqueeze(2), [P, RT, heads, NF])
    s = spread(env["sin"][:, :, :].unsqueeze(2), [P, RT, heads, NF])
    q = [tmp(j).rearrange("p r (h f) -> p r h f", f=NF) for j in range(4)]
    for j, (a, b) in enumerate(((t1, c), (t2, s), (t2, c), (t1, s))):
        eng.tensor_tensor(q[j], a, b, ALU.mult).then_inc(done, 1)
    eng.wait_ge(done, base + 4)
    eng.tensor_tensor(t1, q[0], q[1], ALU.subtract).then_inc(done, 1)
    eng.tensor_tensor(t2, q[2], q[3], ALU.add).then_inc(done, 1)


GROUPS = [(2, 3, 4), (5, 6, 7)]


def key_buffers(nc, env):
    low = Mem(nc, Map.Z + RT * ODD_IN * 4, Map.T)
    high = Mem(nc, Map.W + 24 * KB, Map.SMALL)
    return [{i: (low if i < 5 else high).take(f"{n}{i}", [P, (i + 1) * P], dt) for i in range(EASY, RT)}
            for n, dt in (("hi", I16), ("lo", U16))]


class Selection:

    def __init__(self, nc, env, tag, tiles, hi, lo, mem, junk, pace=0):
        self.nc, self.tiles, self.hi, self.lo, self.junk, self.pace = nc, tiles, hi, lo, junk, pace
        n = len(tiles)
        self.cand, self.count, self.up, self.T, self.TL, self.need = (
            mem.take(f"{tag}_{x}", [P, n], F32) for x in ("cand", "count", "up", "T", "TL", "need"))
        self.step, self.counted, self.masks = (new_sem(nc, env, f"{tag}_{x}") for x in ("step", "counted", "masks"))
        self.work = self.steps()
        self.total = 1 + 2 * 16 * 2 + n + n
        self.done = 0

    def bisect(self, keys, first, result, n, c):
        nc, m = self.nc, len(self.tiles)
        nc.vector.memset(self.cand[:, :], first).then_inc(self.step, 1)
        n += 1
        bit = 2 ** 15
        while bit:
            self.dve.wait_ge(self.step, n)
            for x, i in enumerate(self.tiles):
                nc.vector.tensor_scalar(self.junk[x][:, 0:(i + 1) * P].bitcast(U16), keys[i][:, :], self.cand[:, x:x + 1],
                                        None, ALU.is_ge, ALU.add, accum_out=self.count[:, x:x + 1]).then_inc(self.counted, 1)
            c += m
            yield
            self.dve.wait_ge(self.counted, c)
            nc.vector.tensor_scalar(self.up[:, :], self.count[:, :], float(TOPK), 0.5, ALU.is_ge,
                                    ALU.subtract).then_inc(self.step, 1)
            n += 1
            self.dve.wait_ge(self.step, n)
            if bit > 1:
                nc.vector.scalar_tensor_tensor(self.cand[:, :], self.up[:, :], float(bit), self.cand[:, :], ALU.mult,
                                               ALU.add).then_inc(self.step, 1)
            else:
                nc.vector.scalar_tensor_tensor(result[:, :], self.up[:, :], -0.5, self.cand[:, :], ALU.add,
                                               ALU.add).then_inc(self.step, 1)
            n += 1
            yield
            bit //= 2

    def steps(self):
        nc, m = self.nc, len(self.tiles)
        yield
        yield from self.bisect(self.hi, 0.0, self.T, 0, 0)
        n, c = 33, 16 * m
        self.dve.wait_ge(self.step, n)
        for x, i in enumerate(self.tiles):
            hi, lo, above = self.hi[i][:, :], self.lo[i][:, :], self.junk[x][:, 0:(i + 1) * P].bitcast(U16)
            nc.vector.tensor_scalar(above, hi, self.T[:, x:x + 1], 65535.0, ALU.is_gt, ALU.mult).then_inc(self.step, 1)
            nc.vector.scalar_tensor_tensor(lo, hi, self.T[:, x:x + 1], lo, ALU.is_equal, ALU.mult).then_inc(self.step, 1)
            n += 2
            self.dve.wait_ge(self.step, n)
            nc.vector.tensor_tensor(lo, lo, above, ALU.max).then_inc(self.step, 1)
            n += 1
            yield
        yield from self.bisect(self.lo, 2.0 ** 15, self.TL, n, c)
        n += 33
        self.dve.wait_ge(self.step, n)
        for x, i in enumerate(self.tiles):
            wide = (i + 1) * P
            hi, lo, mask = self.hi[i][:, :], self.lo[i][:, :], self.hi[i][:, :].bitcast(BF16)
            level, not_above, place = (b[:, 0:wide].bitcast(dt) for b, dt in zip(self.junk, (BF16, BF16, I16)))
            T, TL, need = self.T[:, x:x + 1], self.TL[:, x:x + 1], self.need[:, x:x + 1]
            nc.vector.tensor_scalar(level, hi, T, None, ALU.is_equal).then_inc(self.step, 1)
            nc.vector.tensor_scalar(not_above, hi, T, None, ALU.is_le).then_inc(self.step, 1)
            n += 2
            self.dve.wait_ge(self.step, n)
            nc.vector.scalar_tensor_tensor(level, lo, TL, level, ALU.is_equal, ALU.mult).then_inc(self.step, 1)
            nc.vector.scalar_tensor_tensor(not_above, lo, TL, not_above, ALU.is_le, ALU.mult).then_inc(self.step, 1)
            n += 2
            self.dve.wait_ge(self.step, n)
            nc.vector.tensor_scalar(lo, not_above, 0.5, None, ALU.is_gt, ALU.add, accum_out=need).then_inc(self.step, 1)
            nc.vector.tensor_tensor_scan(place, level, level, 0.0, ALU.add, ALU.max).then_inc(self.step, 1)
            n += 2
            self.dve.wait_ge(self.step, n)
            nc.vector.tensor_scalar(need, need, float(TOPK - wide), None, ALU.add).then_inc(self.step, 1)
            n += 1
            self.dve.wait_ge(self.step, n)
            nc.vector.scalar_tensor_tensor(level, place, need, level, ALU.is_le, ALU.mult).then_inc(self.step, 1)
            n += 1
            self.dve.wait_ge(self.step, n)
            nc.vector.scalar_tensor_tensor(mask, level, 0.0, not_above, ALU.is_equal, ALU.mult).then_inc(self.masks, 1)
            if x + 1 < m:
                self.dve.wait_ge(self.masks, x + 1)
            yield

    def advance(self, dve, upto):
        self.dve = dve
        while self.done < min(upto, self.total):
            next(self.work, None)
            self.done += 1

    def load(self, sp):
        pass

    def scalar(self, act, b, k):
        pass

    def vector(self, dve, b, k, out_act, out_dve):
        if b == 0 and k < 3:
            return
        last = b == 1 and k == KC - 1
        self.advance(dve, self.total if last else self.done + self.pace)
        if last:
            dve.wait_ge(self.masks, len(self.tiles))


class IndexPrelude:

    def __init__(self, nc, env, g_dram):
        self.nc, self.env, self.g_dram = nc, env, g_dram
        small = Mem(nc, Map.SMALL + 2 * KB, nc.sbuf_usable_end - BASE)
        self.g = small.take("ixp_g", [P, HD], F32)
        self.ss = small.take("ixp_ss", [P, RT], F32)
        self.st = small.take("ixp_st", [P, 4, RT], F32)
        self.g_in, self.squared, self.sums, self.var, self.root, self.rstd, self.normed, self.irot, self.krot = (
            new_sem(nc, env, f"ixp_{n}") for n in ("g_in", "squared", "sums", "var", "root", "rstd", "normed", "irot", "krot"))

    def load(self, sp):
        sp.dma_start(self.g[:, :], spread(self.g_dram.rearrange("(a d) -> a d", a=1), [P, HD])).then_inc(self.g_in, 16)

    def scalar(self, act, b, k):
        if b == 2 and k == 5:
            act.wait_ge(self.var, 1)
            self.nc.scalar.activation(self.st[:, 1, :], self.st[:, 0, :], ACT.Sqrt).then_inc(self.root, 1)

    def vector(self, dve, b, k, out_act, out_dve):
        nc, Z = self.nc, self.env["Z"]
        ik = Z[:, :, OIK:OIK + HD]
        if (b, k) == (2, 3):
            dve.wait_ge(out_act, RT)
            dve.wait_ge(out_dve, RT)
            sq = Z[:, :, 4 * HD:5 * HD]
            nc.vector.tensor_tensor(sq, ik, ik, ALU.mult).then_inc(self.squared, 1)
            dve.wait_ge(self.squared, 1)
            nc.vector.tensor_reduce(self.ss[:, :], sq, AX.X, ALU.add).then_inc(self.sums, 1)
            dve.wait_ge(self.sums, 1)
            nc.vector.tensor_scalar(self.st[:, 0, :], self.ss[:, :], 1.0 / HD, EPS, ALU.mult, ALU.add).then_inc(self.var, 1)
        if (b, k) == (2, 4):
            rotate_all(nc, nc.vector, self.env, Z, OIQ, IH, lambda j: Z[:, :, j * HD:(j + 1) * HD], self.irot, 0)
        if (b, k) == (2, 6):
            newton(nc, dve, self.st, self.root, self.rstd)
            nc.vector.tensor_tensor(ik, ik, spread(self.st[:, 2, :].unsqueeze(2), [P, RT, HD]), ALU.mult).then_inc(self.normed, 1)
            dve.wait_ge(self.normed, 1)
            dve.wait_ge(self.g_in, 16)
            nc.vector.tensor_tensor(ik, ik, spread(self.g[:, :].unsqueeze(1), [P, RT, HD]), ALU.mult).then_inc(self.normed, 1)
            nc.vector.tensor_scalar(Z[:, :, OIW:OIW + IH], Z[:, :, OIW:OIW + IH], float(np.float32(IH ** -0.5)), None,
                                    ALU.mult).then_inc(self.normed, 1)
        if (b, k) == (2, 7):
            dve.wait_ge(self.normed, 3)
            rotate_all(nc, nc.vector, self.env, Z, OIK, 1,
                       lambda j: Z[:, :, 5 * HD + j * NF:5 * HD + (j + 1) * NF], self.krot, 0)


def indexer(nc, env, hi_keys, lo_keys):
    Z, ident = env["Z"], env["ident"]
    tiles = list(range(EASY, RT))
    with ExitStack() as ctx:
        def sem(n):
            return new_sem(nc, env, f"ix_{n}")

        mem = Mem(nc, Map.W, Map.W + 24 * KB)
        ikhi = mem.take("ix_ikhi", [P, SEQ], F32R)
        iklo = mem.take("ix_iklo", [P, SEQ], F32R)
        iqT = [mem.take("ix_iqT0", [P, IH, P], F32R)]
        iqT += [Mem(nc, mem.at - BASE, Map.SMALL).take("ix_iqT1", [P, IH, P], F32R)]
        kdup = mem.take("ix_kdup", [P, RT, 2, HD], F32)
        twice = mem.take("ix_twice", [P, 2, 4, 2, HD], F32)
        rel = mem.take("ix_rel", [P, 2, NB], F32)
        score = {i: Z[:, i, 0:(i + 1) * P] for i in tiles}
        flips = Z[:, 0, 0:SEQ].bitcast(I32)
        ktmp = Z[:, 1, 0:SEQ].rearrange("p (j r f) -> p j r f", j=4, r=RT)
        ps_x = [ctx.enter_context(nc.psum_tensor(f"ix_ps_x{i}", [P, 4, P], F32)) for i in range(2)]
        ps = [ctx.enter_context(nc.psum_tensor(f"ix_ps{i}", [P, NB], F32)) for i in range(4)]
        krot, dup, turned, hi_done, lo_done, doubled, full, relu_done, acc_done, barred, flip, sorted_, upper, lower = map(sem, (
            "krot", "dup", "turned", "hi_done", "lo_done", "doubled", "full", "relu_done", "acc_done", "barred", "flip",
            "sorted", "upper", "lower"))
        ik = Z[:, :, OIK:OIK + HD]
        turns = [("k", h) for h in range(2)] + [(i, h) for i in tiles for h in range(2)]
        units = [(i, head, part) for i in tiles for head in range(IH) for part in range((i * P + P + NB - 1) // NB)]
        first_unit = {i: min(n for n, u in enumerate(units) if u[0] == i) for i in tiles}
        last_unit = {i: max(n for n, u in enumerate(units) if u[0] == i) for i in tiles}
        block = ctx.enter_context(nc.Block())

        def keys(unit):
            i, _, part = unit
            return slice(part * NB, min((i + 1) * P, (part + 1) * NB))

        def halves(i):
            return score[i].bitcast(I16).rearrange("p (n two) -> p n two", two=2)

        @block.gpsimd
        def _(pool):
            def keep_upper(i):
                pool.wait_ge(sorted_, i - EASY + 1)
                nc.gpsimd.tensor_copy(hi_keys[i][:, :], halves(i)[:, :, 1]).then_inc(upper, 1)

            for c in range(2):
                nc.gpsimd.tensor_copy(kdup[:, :, c, :], ik).then_inc(dup, 1)
            for m in range(2, len(turns)):
                i, h = turns[m]
                if m >= 4:
                    pool.wait_ge(turned, m - 1)
                col = OIQ + h * 4 * HD
                for c in range(2):
                    nc.gpsimd.tensor_copy(twice[:, m % 2, :, c, :],
                                          Z[:, i, col:col + 4 * HD].rearrange("p (h d) -> p h d", d=HD)).then_inc(doubled, 1)
                if m == 5:
                    rotate_all(nc, nc.gpsimd, env, Z, OK_, C_KV, lambda j: ktmp[:, j, :, :], krot, 0)
                if h == 1 and i >= EASY + 2:
                    keep_upper(i - 2)
            keep_upper(RT - 2)
            keep_upper(RT - 1)

        @block.tensor
        def _(pe):
            def turn(m):
                i, h = turns[m]
                if m >= 2:
                    pe.wait_ge(lo_done, m - 1)
                if i == "k":
                    pe.wait_ge(dup, 2)
                else:
                    pe.wait_ge(doubled, 2 * (m - 2) + 2)
                for r in range(4):
                    src = kdup[:, 4 * h + r, :, :] if i == "k" else twice[:, m % 2, r, :, :]
                    last = nc.tensor.transpose(ps_x[m % 2][:, r, :], src, ident[:, :])
                last.then_inc(turned, 1)

            for m in range(4):
                turn(m)
            for n, (i, head, part) in enumerate(units):
                if n == first_unit[i] and i + 1 < RT:
                    for h in range(2):
                        turn(4 + 2 * (i - EASY) + h)
                if part == 0 and head % 4 == 0:
                    pe.wait_ge(lo_done, 3 + 2 * (i - EASY) + head // 4)
                if n >= 4:
                    pe.wait_ge(relu_done, n - 3)
                k = keys((i, head, part))
                wide = k.stop - k.start
                nc.tensor.matmul(ps[n % 4][:, 0:wide], iqT[i % 2][:, head, :], ikhi[:, k], start=True, stop=False)
                nc.tensor.matmul(ps[n % 4][:, 0:wide], iqT[i % 2][:, head, :], iklo[:, k], start=False,
                                 stop=True).then_inc(full, 1)

        @block.scalar
        def _(act):
            def hi(m):
                i, h = turns[m]
                act.wait_ge(turned, m + 1)
                if i == "k":
                    nc.scalar.activation(ikhi[:, h * NB:(h + 1) * NB], ps_x[m % 2][:, :, :].rearrange("p a b -> p (a b)"),
                                         ACT.Copy).then_inc(hi_done, 1)
                else:
                    if i >= EASY + 2:
                        act.wait_ge(full, last_unit[i - 2] + 1)
                    nc.scalar.activation(iqT[i % 2][:, 4 * h:4 * h + 4, :], ps_x[m % 2][:, :, :], ACT.Copy,
                                         scale=HD ** -0.5).then_inc(hi_done, 1)

            for m in range(4):
                hi(m)
            for n, unit in enumerate(units):
                i = unit[0]
                wide = keys(unit).stop - keys(unit).start
                if n == first_unit[i] and i + 1 < RT:
                    for h in range(2):
                        hi(4 + 2 * (i - EASY) + h)
                act.wait_ge(full, n + 1)
                if n >= 2:
                    act.wait_ge(acc_done, n - 1)
                nc.scalar.activation(rel[:, n % 2, 0:wide], ps[n % 4][:, 0:wide], ACT.Relu).then_inc(relu_done, 1)

        @block.vector
        def _(dve):
            def lo(m):
                i, h = turns[m]
                dve.wait_ge(hi_done, m + 1)
                if i == "k":
                    part = slice(h * NB, (h + 1) * NB)
                    nc.vector.tensor_tensor(iklo[:, part], ps_x[m % 2][:, :, :].rearrange("p a b -> p (a b)"),
                                            f32(ikhi[:, part]), ALU.subtract).then_inc(lo_done, 1)
                else:
                    to = iqT[i % 2][HD:P, 4 * h:4 * h + 4, :].rearrange("p a b -> p (a b)")
                    nc.vector.scalar_tensor_tensor(to, ps_x[m % 2][HD:P, :, :].rearrange("p a b -> p (a b)"), HD ** -0.5,
                                                   f32(to), ALU.mult, ALU.subtract).then_inc(lo_done, 1)

            for m in range(4):
                lo(m)
            for n, unit in enumerate(units):
                i, head, part = unit
                if n == first_unit[i] and i + 1 < RT:
                    for h in range(2):
                        lo(4 + 2 * (i - EASY) + h)
                k = keys(unit)
                to, r = score[i][:, k.start:k.stop], rel[:, n % 2, 0:k.stop - k.start]
                w = Z[:, i, OIW + head:OIW + head + 1]
                dve.wait_ge(relu_done, n + 1)
                if head == 0:
                    nc.vector.tensor_scalar(to, r, w, 0.0, ALU.mult, ALU.add).then_inc(acc_done, 1)
                else:
                    dve.wait_ge(acc_done, n - (last_unit[i] - first_unit[i] + 1) // IH + 1)
                    nc.vector.scalar_tensor_tensor(to, r, w, to, ALU.mult, ALU.add).then_inc(acc_done, 1)
                if n == last_unit[i]:
                    dve.wait_ge(acc_done, n + 1)
                    nc.vector.memset(score[i][0:CHUNK, i * P + CHUNK:(i + 1) * P], BARRED).then_inc(barred, 1)
                    dve.wait_ge(barred, i - EASY + 1)
                    s, flips_i = score[i].bitcast(I32), flips[:, 0:(i + 1) * P]
                    nc.vector.tensor_scalar(flips_i, s, 31, 1, ALU.arith_shift_right,
                                            ALU.logical_shift_right).then_inc(flip, 1)
                    dve.wait_ge(flip, i - EASY + 1)
                    nc.vector.tensor_tensor(s, s, flips_i, ALU.bitwise_xor).then_inc(sorted_, 1)
                    dve.wait_ge(sorted_, i - EASY + 1)
                    nc.vector.tensor_copy(lo_keys[i][:, :].bitcast(I16), halves(i)[:, :, 0]).then_inc(lower, 1)


def sparse_attention(nc, env, hi_keys, lo_keys, small):
    Z, ident, barring = env["Z"], env["ident"], env["barring"]
    H = C_HEADS
    with ExitStack() as ctx:
        def sem(n):
            return new_sem(nc, env, f"sa_{n}")

        mem = Mem(nc, Map.T, Map.W + 24 * KB)
        kThi = mem.take("sa_kThi", [P, C_KV, SEQ], F32R)
        kTlo = mem.take("sa_kTlo", [P, C_KV, SEQ], F32R)
        easy = mem.take("sa_easy", [P, EASY, EASY * P], BF16)
        junk = [mem.take(f"sa_junk{x}", [P, SEQ], BF16) for x in range(3)]
        second = Selection(nc, env, "sel1", GROUPS[1], hi_keys, lo_keys, small, junk)
        qfull = mem.take("sa_qfull", [P, 2, 4, P], F32)
        qT = mem.take("sa_qT", [P, 2, 4, P], F32R)
        kdup = Mem(nc, mem.at - BASE, Map.W + 24 * KB).take("sa_kdup", [P, RT, C_KV, 2, HD], F32)
        prob = mem.take("sa_prob", [P, 2, SEQ], F32)
        probT = mem.take("sa_probT", [P, 2, RT, P], F32)
        twice = mem.take("sa_twice", [P, 2, 4, 2, HD], F32)
        rtmp = mem.take("sa_rtmp", [P, 2 * 4, H * NF], F32)
        nmax = mem.take("sa_nmax", [P, RT, H], F32)
        rsum = mem.take("sa_rsum", [P, RT, H], F32)
        ps_s = [ctx.enter_context(nc.psum_tensor(f"sa_ps_s{i}", [P, SEQ], F32)) for i in range(2)]
        ps_t = [ctx.enter_context(nc.psum_tensor(f"sa_ps_t{i}", [P, 4, P], F32)) for i in range(2)]
        ps_o = ctx.enter_context(nc.psum_tensor("sa_ps_o", [P, 8, HD], F32))
        ps_x = ctx.enter_context(nc.psum_tensor("sa_ps_x", [P, 4, P], F32))
        (kdup_done, k_turned, khi_done, klo_done, rotated, doubled, x_full, x_hi, x_free, q_lo, zeroed, mask_done,
         scored, max_done, exp_done, t_done, pT_done, mixed, inv_done, out_done) = map(sem, (
             "kdup_done", "k_turned", "khi_done", "klo_done", "rotated", "doubled", "x_full", "x_hi", "x_free", "q_lo",
             "zeroed", "mask_done", "scored", "max_done", "exp_done", "t_done", "pT_done", "mixed", "inv_done",
             "out_done"))
        steps = [(i, h) for i in range(RT) for h in range(H)]
        groups = [(i, g) for i in range(RT) for g in range(H // 4)]
        kunits = [(k, h) for k in range(C_KV) for h in range(2)]
        kbanks = [ps_t[0][:, :, :], ps_t[1][:, :, :], ps_s[0][:, 0:NB].rearrange("p (a b) -> p a b", b=P),
                  ps_s[1][:, 0:NB].rearrange("p (a b) -> p a b", b=P)]
        turns = [(n, b) for n, (i, h) in enumerate(steps) for b in range(i // 4 + 1)]
        turns_at = {nb: m for m, nb in enumerate(turns)}
        block = ctx.enter_context(nc.Block())

        def parts(i):
            return (i * P + P + NB - 1) // NB

        def mask(i, keys):
            return easy[:, i, keys] if i < EASY else hi_keys[i][:, keys].bitcast(BF16)

        def last_turn(n):
            return turns_at[(n, steps[n][0] // 4)]

        def group_beside(n):
            return n // 4 + 1 if n % 4 == 1 and n // 4 + 1 < len(groups) else None

        @block.tensor
        def _(pe):
            def turn_queries(m):
                if m:
                    pe.wait_ge(x_free, m)
                pe.wait_ge(doubled, 2 * m + 2)
                for u in range(4):
                    last = nc.tensor.transpose(ps_x[:, u, :], twice[:, m % 2, u, :, :], ident[:, :])
                last.then_inc(x_full, 1)

            def logits(n):
                i, h = steps[n]
                if h == 0 and i < EASY:
                    pe.wait_ge(mask_done, i + 1)
                if h == 0 and i in GROUPS[1]:
                    pe.wait_ge(second.masks, GROUPS[1].index(i) + 1)
                if h % 4 == 0:
                    pe.wait_ge(q_lo, n // 4 + 1)
                if n >= 2:
                    pe.wait_ge(exp_done, n - 1)
                for part in range(parts(i)):
                    keys = slice(part * NB, min((i + 1) * P, (part + 1) * NB))
                    bank = ps_s[n % 2][:, keys]
                    q = qT[:, n // 4 % 2, h % 4, :]
                    nc.tensor.matmul(bank, barring[:, :], mask(i, keys), start=True, stop=False)
                    nc.tensor.matmul(bank, q, kThi[:, h // 4, keys], start=False, stop=False)
                    last = nc.tensor.matmul(bank, q, kTlo[:, h // 4, keys], start=False, stop=True)
                last.then_inc(scored, 1)

            def turn(n):
                i, h = steps[n]
                pe.wait_ge(exp_done, n + 1)
                for b in range(i // 4 + 1):
                    m = turns_at[(n, b)]
                    if m >= 2:
                        pe.wait_ge(pT_done, m - 1)
                    for j in range(4 * b, min(i + 1, 4 * b + 4)):
                        last = nc.tensor.transpose(ps_t[m % 2][:, j - 4 * b, :], prob[:, n % 2, j * P:(j + 1) * P], ident[:, :])
                    last.then_inc(t_done, 1)

            def mix(n):
                i, h = steps[n]
                pe.wait_ge(pT_done, last_turn(n) + 1)
                if n:
                    pe.wait_ge(out_done, n)
                for j in range(i + 1):
                    last = nc.tensor.matmul(ps_o[:, h % 8, :], probT[:, n % 2, j, :],
                                            Z[:, j, OV + h // 4 * HD:OV + (h // 4 + 1) * HD], start=(j == 0), stop=(j == i))
                last.then_inc(mixed, 1)

            for m, (k, half) in enumerate(kunits):
                pe.wait_ge(kdup_done, 2 * k + 2)
                if m >= 4:
                    pe.wait_ge(klo_done, m - 3)
                for r in range(4):
                    last = nc.tensor.transpose(kbanks[m % 4][:, r, :], kdup[:, 4 * half + r, k, :, :], ident[:, :])
                last.then_inc(k_turned, 1)
            turn_queries(0)
            pe.wait_ge(klo_done, len(kunits))
            for n in range(len(steps) + 3):
                if n < len(steps):
                    logits(n)
                if 0 <= n - 2 < len(steps):
                    turn(n - 2)
                if group_beside(n):
                    turn_queries(group_beside(n))
                if n - 3 >= 0:
                    mix(n - 3)

        @block.scalar
        def _(act):
            def empty(m):
                act.wait_ge(x_full, m + 1)
                if m >= 2:
                    act.wait_ge(q_lo, m - 1)
                    act.wait_ge(scored, 4 * (m - 1))
                nc.scalar.activation(qfull[:, m % 2, :, :], ps_x[:, :, :], ACT.Copy, scale=HD ** -0.5).then_inc(x_hi, 1)
                nc.scalar.activation(qT[:, m % 2, :, :], ps_x[:, :, :], ACT.Copy, scale=HD ** -0.5).then_inc(x_free, 1)

            def softmax(n):
                i, h = steps[n]
                act.wait_ge(max_done, n + 1)
                if n >= 2:
                    act.wait_ge(t_done, last_turn(n - 2) + 1)
                nc.scalar.activation(prob[:, n % 2, 0:(i + 1) * P], ps_s[n % 2][:, 0:(i + 1) * P], ACT.Exp,
                                     bias=nmax[:, i, h:h + 1], accum_out=rsum[:, i, h:h + 1]).then_inc(exp_done, 1)

            def keep_turned(n):
                i, h = steps[n]
                if n >= 2:
                    act.wait_ge(mixed, n - 1)
                for b in range(i // 4 + 1):
                    m = turns_at[(n, b)]
                    act.wait_ge(t_done, m + 1)
                    count = min(i + 1 - 4 * b, 4)
                    nc.scalar.activation(probT[:, n % 2, 4 * b:4 * b + count, :], ps_t[m % 2][:, 0:count, :],
                                         ACT.Copy).then_inc(pT_done, 1)

            def write(n):
                i, h = steps[n]
                act.wait_ge(mixed, n + 1)
                act.wait_ge(inv_done, n + 1)
                nc.scalar.activation(Z[:, i, OQ + h * HD:OQ + (h + 1) * HD], ps_o[:, h % 8, :], ACT.Copy,
                                     scale=rsum[:, i, h:h + 1]).then_inc(out_done, 1)

            for m, (k, half) in enumerate(kunits):
                act.wait_ge(k_turned, m + 1)
                nc.scalar.activation(kThi[:, k, half * NB:(half + 1) * NB].rearrange("p (a b) -> p a b", b=P), kbanks[m % 4],
                                     ACT.Copy).then_inc(khi_done, 1)
            empty(0)
            for n in range(len(steps) + 3):
                if n < len(steps):
                    softmax(n)
                if 0 <= n - 2 < len(steps):
                    keep_turned(n - 2)
                if group_beside(n):
                    empty(group_beside(n))
                if n - 3 >= 0:
                    write(n - 3)

        @block.gpsimd
        def _(pool):
            def double(m):
                i, g = groups[m]
                if m >= 2:
                    pool.wait_ge(x_full, m - 1)
                    pool.wait_ge(q_lo, m - 1)
                if g == 0:
                    rotate_queries(i)
                    pool.wait_ge(rotated, 6 * (i + 1))
                for c in range(2):
                    nc.gpsimd.tensor_copy(twice[:, m % 2, :, c, :], Z[:, i, OQ + 4 * g * HD:OQ + 4 * (g + 1) * HD]
                                          .rearrange("p (h d) -> p h d", d=HD)).then_inc(doubled, 1)

            def rotate_queries(i):
                rotate(nc, nc.gpsimd, env, Z, OQ, H, rtmp[:, 4 * (i % 2):4 * (i % 2) + 4, :], rotated, 6 * i, [i])

            double(0)
            for k in range(C_KV):
                for c in range(2):
                    nc.gpsimd.tensor_copy(kdup[:, :, k, c, :], Z[:, :, OK_ + k * HD:OK_ + (k + 1) * HD]).then_inc(kdup_done, 1)
            for m in range(len(groups)):
                if m + 1 < len(groups):
                    double(m + 1)
                pool.wait_ge(doubled, min(2 * m + 4, 2 * len(groups)))
                pool.wait_ge(kdup_done, 2 * C_KV)
                pool.wait_ge(x_hi, m + 1)
                pool.wait_ge(x_free, m + 1)
                to = qT[HD:P, m % 2, :, :]
                nc.gpsimd.tensor_tensor(to, qfull[HD:P, m % 2, :, :], f32(to), ALU.subtract).then_inc(q_lo, 1)

        @block.vector
        def _(dve):
            for i in range(EASY):
                nc.vector.memset(easy[:, i, :], 0.0).then_inc(zeroed, 1)
            dve.wait_ge(zeroed, EASY)
            for i in range(EASY):
                nc.vector.memset(easy[0:CHUNK, i, i * P + CHUNK:(i + 1) * P], 1.0).then_inc(mask_done, 1)
            for m, (k, half) in enumerate(kunits):
                dve.wait_ge(khi_done, m + 1)
                part = slice(half * NB, (half + 1) * NB)
                nc.vector.tensor_tensor(kTlo[:, k, part].rearrange("p (a b) -> p a b", b=P), kbanks[m % 4],
                                        f32(kThi[:, k, part]).rearrange("p (a b) -> p a b", b=P), ALU.subtract).then_inc(klo_done, 1)
            span = GROUPS[1][0] * H - 6
            for n in range(len(steps) + 1):
                if n < len(steps):
                    i, h = steps[n]
                    dve.wait_ge(scored, n + 1)
                    nc.vector.tensor_reduce(nmax[:, i, h:h + 1], ps_s[n % 2][:, 0:(i + 1) * P], AX.X, ALU.max,
                                            negate=True).then_inc(max_done, 1)
                due = -(-second.total * (n + 1) // span)
                if second.done < due:
                    second.advance(dve, second.done + 1)
                if n >= 1:
                    i2, h2 = steps[n - 1]
                    dve.wait_ge(exp_done, n)
                    nc.vector.reciprocal(rsum[:, i2, h2:h2 + 1], rsum[:, i2, h2:h2 + 1]).then_inc(inv_done, 1)
                second.advance(dve, due)


def program(nc, t):
    mem = Mem(nc, Map.X, Map.Z)
    env = {"X": mem.take("X", [P, RT, D], F32), "sems": []}
    mem = Mem(nc, Map.Z, Map.T)
    env["Z"] = mem.take("Z", [P, RT, ZW], F32)
    mem = Mem(nc, Map.T, Map.W)
    env["Thi"] = mem.take("Thi", [P, KC, SEQ], F32R)
    env["Tlo"] = mem.take("Tlo", [P, KC, SEQ], F32R)
    mem = Mem(nc, Map.SMALL, nc.sbuf_usable_end - BASE)
    env["ident"] = mem.take("ident", [P, P], F32)
    env["barring"] = mem.take("barring", [P, P], BF16)
    env["cos"] = mem.take("cos", [P, RT, NF], F32)
    env["sin"] = mem.take("sin", [P, RT, NF], F32)
    constants(nc, env)
    norm_transpose(nc, env, "n0", t["norm_mix"][0], load_x=t["x"][0])
    project(nc, env, "in0", t["even_w_in"][0], EVEN_IN, env["Z"])
    rotary_tables(nc, env, t["positions"][0])
    window_attention(nc, env, t["even_sinks"][0])
    mlstm(nc, env, t)
    Z = env["Z"]
    norm_transpose(nc, env, "y0", None, src=lambda r, k: Z[:, r, k * P:(k + 1) * P] if k < 4
                   else Z[:, r, EBO + (k - 4) * P:EBO + (k - 3) * P])
    project(nc, env, "out0", t["even_w_out"][0], D, env["X"], add=True)
    norm_transpose(nc, env, "n1", t["norm_mlp"][0])
    mlp(nc, env, "mlp0", t["w_up"][0], t["w_down"][0])
    reset_semaphores(nc, env)
    norm_transpose(nc, env, "n2", t["norm_mix"][1])
    hi_keys, lo_keys = key_buffers(nc, env)
    Z = env["Z"] = Mem(nc, Map.Z, Map.T).take("Z_odd", [P, RT, ODD_IN], F32)
    project(nc, env, "in1", t["odd_w_in"][0], ODD_IN, Z, cols=[(OIQ, NB), (OIK, HD + IH), (OK_, NB)],
            side=IndexPrelude(nc, env, t["odd_idx_k_norm"][0]))
    indexer(nc, env, hi_keys, lo_keys)
    small = Mem(nc, Map.SMALL + 3 * KB, nc.sbuf_usable_end - BASE)
    junk = [Z[:, r, NB:2 * NB].bitcast(BF16) for r in (1, 3, 5)]
    first = Selection(nc, env, "sel0", GROUPS[0], hi_keys, lo_keys, small, junk, pace=6)
    project(nc, env, "inq", t["odd_w_in"][0], ODD_IN, Z, cols=[(0, NB), (NB, NB)], side=first)
    sparse_attention(nc, env, hi_keys, lo_keys, small)
    norm_transpose(nc, env, "y1", None, src=lambda r, k: Z[:, r, k * P:(k + 1) * P])
    project(nc, env, "out1", t["odd_w_out"][0], D, env["X"], add=True)
    norm_transpose(nc, env, "n3", t["norm_mlp"][1])
    mlp(nc, env, "mlp1", t["w_up"][1], t["w_down"][1])
    final_norm(nc, env, t["final_norm"], t["out"][0])


INPUTS = ["x", "positions", "norm_mix", "even_w_in", "even_sinks", "even_conv_w", "even_conv_b", "even_bias_i",
          "even_bias_f", "even_w_out", "odd_w_in", "odd_idx_k_norm", "odd_w_out", "norm_mlp", "w_up", "w_down",
          "final_norm"]


def kernel(**inputs):
    import numpy as _np
    import concourse.bacc as _bacc
    from concourse import mybir as _mybir
    from concourse.bass_utils import run_bass_kernel_spmd as _run

    nc = _bacc.Bacc("TRN2", target_bir_lowering=False, num_devices=1)
    arrays, t = {}, {}
    for name in INPUTS:
        a = _np.ascontiguousarray(inputs[name])
        arrays[f"in_{name}"] = a
        t[name] = nc.dram_tensor(f"in_{name}", a.shape, _mybir.dt.from_np(a.dtype), kind="ExternalInput").ap()
    t["out"] = nc.dram_tensor("out_y", (1, SEQ, D), _mybir.dt.float32, kind="ExternalOutput").ap()
    program(nc, t)
    r = _run(nc, [arrays], core_ids=[0])
    return r.results[0]["out_y"]
```

```python
from contextlib import ExitStack

import numpy as np

import concourse.bass as bass
from concourse import mybir

F32 = mybir.dt.float32
F32R = mybir.dt.float32r
BF16 = mybir.dt.bfloat16
I32 = mybir.dt.int32
I16 = mybir.dt.int16
U16 = mybir.dt.uint16
ALU = mybir.AluOpType
ACT = mybir.ActivationFunctionType
AX = mybir.AxisListType

P = 128
D = 1024
SEQ = 1024
KC = D // P
RT = SEQ // P
CHUNK = 64
HD = 64
ROT = HD // 4
NF = ROT // 2
THETA = 500000.0
EPS = 1e-5
A_HEADS, A_KV = 8, 2
B_HEADS, B_DV, B_DK, CONV = 4, 128, 64, 4
C_HEADS, C_KV = 16, 4
IH = 8
TOPK = 256
D_FF = 4096
FC = D_FF // P
NB = 512
EVEN_IN, ODD_IN = 2312, 2120
EASY = TOPK // P
BARRED, OFF = -3.2e38, -1e30
ZW = EVEN_IN
EQ, EK, EV, EBQK, EBV, EBO, EBI, EBF = 0, 512, 640, 768, 1280, 1792, 2304, 2308
OQ, OK_, OV, OIQ, OIK, OIW = 0, 1024, 1280, 1536, 2048, 2112

KB = 1024
BASE = 16 * KB + 128


class Map:
    X = 0
    Z = 32 * KB
    T = Z + RT * ZW * 4
    W = T + 64 * KB
    SMALL = W + 36 * KB


class Mem:

    def __init__(self, nc, start, end):
        self.nc, self.at, self.end = nc, BASE + start, BASE + end

    def take(self, name, shape, dt):
        size = int(np.prod(shape[1:])) * (2 if dt in (BF16, I16, U16) else 4)
        assert self.at + size <= self.end, (name, self.at + size - self.end)
        t = self.nc.alloc_sbuf_tensor_at(name, shape, dt, offset=self.at)
        self.at += (size + 31) // 32 * 32
        return t


def new_sem(nc, env, name):
    s = nc.alloc_semaphore(name)
    env["sems"].append(s)
    return s


def reset_semaphores(nc, env):
    nc.clear_and_free_semaphores(env["sems"])
    nc.all_engine_barrier()
    env["sems"] = []


def f32(ap):
    return ap.bitcast(F32)


def inverse_root(nc, dve, st, rstd, base):
    nc.vector.reciprocal(st[:, 2, :], st[:, 1, :]).then_inc(rstd, 1)
    dve.wait_ge(rstd, base + 1)
    nc.vector.tensor_tensor(st[:, 1, :], st[:, 2, :], st[:, 2, :], ALU.mult).then_inc(rstd, 1)
    dve.wait_ge(rstd, base + 2)
    nc.vector.tensor_tensor(st[:, 1, :], st[:, 1, :], st[:, 0, :], ALU.mult).then_inc(rstd, 1)
    dve.wait_ge(rstd, base + 3)
    nc.vector.tensor_scalar(st[:, 1, :], st[:, 1, :], -0.5, 1.5, ALU.mult, ALU.add).then_inc(rstd, 1)
    dve.wait_ge(rstd, base + 4)
    nc.vector.tensor_tensor(st[:, 2, :], st[:, 2, :], st[:, 1, :], ALU.mult).then_inc(rstd, 1)
    dve.wait_ge(rstd, base + 5)


def norm_transpose(nc, env, tag, g_dram, ahead, load_x=None, src=None):
    X, Thi, Tlo, ident = env["X"], env["Thi"], env["Tlo"], env["ident"]
    with ExitStack() as ctx:
        def sem(n):
            return new_sem(nc, env, f"{tag}_{n}")

        if src is None:
            mem = Mem(nc, Map.Z, Map.T)
            xn = mem.take(f"{tag}_xn", [P, RT, D], F32)
            g = mem.take(f"{tag}_g", [P, KC], F32)
            ss = mem.take(f"{tag}_ss", [P, RT], F32)
            st = mem.take(f"{tag}_st", [P, 3, RT], F32)
        ps = [ctx.enter_context(nc.psum_tensor(f"{tag}_ps{i}", [P, NB], F32)) for i in range(8)]
        x_in = [sem(f"x_in{r}") for r in range(RT)] if load_x is not None else None
        sums = [sem(f"sums{h}") for h in range(2)]
        g_in, var, root, rstd, xn_ready, turned, hi_done, lo_done = map(sem, (
            "g_in", "var", "root", "rstd", "xn_ready", "turned", "hi_done", "lo_done"))
        banks = [(half, k) for half in range(2) for k in range(KC)]
        late = 0 if load_x is None else KC
        block = ctx.enter_context(nc.Block())

        @block.sync
        def _(sp):
            if src is None:
                if load_x is not None:
                    for r in range(RT):
                        sp.dma_start(X[:, r, :], load_x[r * P:(r + 1) * P, :]).then_inc(x_in[r], 16)
                sp.dma_start(g[:, :], g_dram.rearrange("(k p) -> p k", p=P), allow_slow_non_contiguous=True).then_inc(g_in, 16)
            ahead.load(sp)

        @block.vector
        def _(dve):
            def normalise(half):
                part = slice(4 * half, 4 * half + 4)
                for r in range(4 * half + 1, 4 * half + 4, 2):
                    if load_x is not None:
                        dve.wait_ge(x_in[r], 16)
                    nc.vector.tensor_tensor_reduce(xn[:, r, :], X[:, r, :], X[:, r, :], 1.0, 0.0, ALU.mult,
                                                   ALU.add, ss[:, r:r + 1]).then_inc(sums[half], 1)
                dve.wait_ge(sums[half], 4)
                nc.vector.tensor_scalar(st[:, 0, part], ss[:, part], 1.0 / D, EPS, ALU.mult, ALU.add).then_inc(var, 1)
                dve.wait_ge(root, half + 1)
                inverse_root(nc, dve, st[:, :, part], rstd, 5 * half)
                for r in range(4 * half, 4 * half + 4):
                    nc.vector.tensor_scalar(xn[:, r, :], X[:, r, :], st[:, 2, r:r + 1], None, ALU.mult).then_inc(xn_ready, 1)

            if src is None:
                normalise(0)
            for n, (half, k) in enumerate(banks):
                if src is None and n == late:
                    normalise(1)
                if src is None and n == 0:
                    dve.wait_ge(g_in, 16)
                dve.wait_ge(hi_done, n + 1)
                lo, hi = Tlo[:, k, half * NB:(half + 1) * NB], f32(Thi[:, k, half * NB:(half + 1) * NB])
                if src is None:
                    nc.vector.scalar_tensor_tensor(lo, ps[n % 8][:, :], g[:, k:k + 1], hi, ALU.mult,
                                                   ALU.subtract).then_inc(lo_done, 1)
                else:
                    nc.vector.tensor_tensor(lo, ps[n % 8][:, :], hi, ALU.subtract).then_inc(lo_done, 1)

        @block.scalar
        def _(act):
            def squares(half):
                for r in range(4 * half, 4 * half + 4, 2):
                    if load_x is not None:
                        act.wait_ge(x_in[r], 16)
                    nc.scalar.activation(xn[:, r, :], X[:, r, :], ACT.Square, accum_out=ss[:, r:r + 1]).then_inc(sums[half], 1)
                part = slice(4 * half, 4 * half + 4)
                act.wait_ge(var, half + 1)
                nc.scalar.activation(st[:, 1, part], st[:, 0, part], ACT.Sqrt).then_inc(root, 1)

            if src is None:
                squares(0)
            for n, (half, k) in enumerate(banks):
                if src is None and n == late:
                    squares(1)
                if src is None and n == 0:
                    act.wait_ge(g_in, 16)
                act.wait_ge(turned, n + 1)
                hi = Thi[:, k, half * NB:(half + 1) * NB]
                if src is None:
                    nc.scalar.activation(hi, ps[n % 8][:, :], ACT.Copy, scale=g[:, k:k + 1]).then_inc(hi_done, 1)
                else:
                    nc.scalar.activation(hi, ps[n % 8][:, :], ACT.Copy).then_inc(hi_done, 1)

        @block.tensor
        def _(pe):
            for n, (half, k) in enumerate(banks):
                if src is None and k == 0:
                    pe.wait_ge(xn_ready, 4 * half + 4)
                if n >= 8:
                    pe.wait_ge(lo_done, n - 7)
                for r in range(4):
                    rows = xn[:, 4 * half + r, k * P:(k + 1) * P] if src is None else src(4 * half + r, k)
                    last = nc.tensor.transpose(ps[n % 8][:, r * P:(r + 1) * P], rows, ident[:, :])
                last.then_inc(turned, 1)


def constants(nc, env):
    with ExitStack() as ctx:
        made = new_sem(nc, env, "const_made")
        ident = env["ident"]
        block = ctx.enter_context(nc.Block())

        @block.gpsimd
        def _(pool):
            nc.gpsimd.memset(ident[:, :], 0.0).then_inc(made, 1)
            pool.wait_ge(made, 1)
            nc.gpsimd.affine_select(out=ident[:, :], in_=ident[:, :], compare_op=ALU.not_equal, fill=1.0, base=0,
                                    pattern=[[-1, P]], channel_multiplier=1).then_inc(made, 1)


class ProjectWeights:

    RAW = 4

    def __init__(self, nc, env, tag, w, width=NB, col=0):
        self.w, self.width, self.col = w, width, col
        self.mem = Mem(nc, Map.W, Map.SMALL)
        self.raw = self.mem.take(f"{tag}_raw", [P, self.RAW, NB], F32)
        self.w_in = [new_sem(nc, env, f"{tag}_w_in{i}") for i in range(self.RAW)]

    def load(self, sp):
        for k in range(self.RAW):
            sp.dma_start(self.raw[:, k, 0:self.width],
                         self.w[k * P:(k + 1) * P, self.col:self.col + self.width]).then_inc(self.w_in[k], 16)


class MlpWeights:

    def __init__(self, nc, env, tag, w_up, w_down):
        self.up_v, self.w_down = w_up.rearrange("(k p) f -> p k f", p=P), w_down
        self.mem = Mem(nc, Map.W, Map.SMALL)
        self.raw = self.mem.take(f"{tag}_raw", [P, 4, D], F32)
        self.up_in = [new_sem(nc, env, f"{tag}_up_in{i}") for i in range(2)]
        self.down_in = [new_sem(nc, env, f"{tag}_down_in{i}") for i in range(2)]

    def load_block(self, sp, b, before_up, before_down):
        for c in range(2):
            before_up(c)
            sp.dma_start(self.raw[:, c, :].rearrange("p (k f) -> p k f", k=KC),
                         self.up_v[:, :, bass.ds((2 * b + c) * P, P)]).then_inc(self.up_in[c], 16)
        for c in range(2):
            before_down(c)
            sp.dma_start(self.raw[:, 2 + c, :], self.w_down[bass.ds((2 * b + c) * P, P), :]).then_inc(self.down_in[c], 16)

    def load(self, sp):
        self.load_block(sp, 0, lambda c: None, lambda c: None)


def project(nc, env, tag, w, width, dest, add=False, cols=None, side=None, ahead=None):
    Thi, Tlo = env["Thi"], env["Tlo"]
    full, tail = divmod(width, NB)
    RAW, RING, LEAD = ProjectWeights.RAW, 4, 3
    with ExitStack() as ctx:
        def sem(n):
            return new_sem(nc, env, f"{tag}_{n}")

        weights = ahead or ProjectWeights(nc, env, tag, w, cols[0][1], cols[0][0])
        mem, raw, w_in = weights.mem, weights.raw, weights.w_in
        whi = mem.take(f"{tag}_whi", [P, RING, NB], F32R)
        wlo = mem.take(f"{tag}_wlo", [P, RING, NB], F32R)
        ps = [ctx.enter_context(nc.psum_tensor(f"{tag}_ps{i}", [P, NB], F32)) for i in range(RT)]
        hi_done, lo_done, used, summed, out_act, out_dve = map(
            sem, ("hi_done", "lo_done", "used", "summed", "out_act", "out_dve"))
        block = ctx.enter_context(nc.Block())

        widths = [NB] * full + ([tail] if tail else [])
        if cols:
            widths = [n for _, n in cols]

        def at(b, n):
            return bass.ds(b * NB, n) if not cols else slice(cols[b][0], cols[b][0] + n)

        def blocks(eng, step):
            step(0, widths[0], widths[1])
            if full > 3 and not cols:
                with eng.Fori(1, full - 1) as b:
                    step(b, NB, NB)
                rest = range(full - 1, len(widths))
            else:
                rest = range(1, len(widths))
            for b in rest:
                step(b, widths[b], widths[b + 1] if b + 1 < len(widths) else 0)

        def chunks(split, b, n, after):
            if isinstance(b, int) and b == 0:
                for k in range(LEAD):
                    split(b, k, n)
            for k in range(LEAD, KC):
                split(b, k, n)
            if after:
                for k in range(LEAD):
                    split(b + 1, k, after)

        @block.sync
        def _(sp):
            if side:
                side.load(sp)

            if not ahead:
                weights.load(sp)

            def step(b, n, after):
                for k in range(RAW if isinstance(b, int) and b == 0 else 0, KC):
                    sp.wait_ge(lo_done, KC * b + k - RAW + 1)
                    sp.dma_start(raw[:, k % RAW, 0:n], w[k * P:(k + 1) * P, at(b, n)]).then_inc(w_in[k % RAW], 16)
            blocks(sp, step)

        @block.scalar
        def _(act):
            def split(b, k, n):
                act.wait_ge(w_in[k % RAW], (b * (KC // RAW) + k // RAW + 1) * 16)
                if k >= RING:
                    act.wait_ge(used, (KC - 1) * b + k - RING + 1)
                elif not (isinstance(b, int) and b == 0):
                    if k < RING - 1:
                        act.wait_ge(used, (KC - 1) * (b - 1) + KC + k - RING + 1)
                    else:
                        act.wait_ge(summed, RT * b)
                nc.scalar.activation(whi[:, k % RING, 0:n], raw[:, k % RAW, 0:n], ACT.Copy).then_inc(hi_done, 1)
                if side:
                    side.scalar(act, b, k)

            def step(b, n, after):
                chunks(split, b, n, after)
                if add:
                    return
                for r in range(0, RT, 2):
                    act.wait_ge(summed, RT * b + r + 1)
                    nc.scalar.activation(dest[:, r, at(b, n)], ps[r][:, 0:n], ACT.Copy).then_inc(out_act, 1)
            blocks(act, step)

        @block.vector
        def _(dve):
            def split(b, k, n):
                dve.wait_ge(hi_done, KC * b + k + 1)
                nc.vector.tensor_tensor(wlo[:, k % RING, 0:n], raw[:, k % RAW, 0:n], f32(whi[:, k % RING, 0:n]),
                                        ALU.subtract).then_inc(lo_done, 1)
                if side:
                    side.vector(dve, b, k, out_act, out_dve)

            def step(b, n, after):
                chunks(split, b, n, after)
                for r in range(0 if add else 1, RT, 1 if add else 2):
                    dve.wait_ge(summed, RT * b + r + 1)
                    to = dest[:, r, at(b, n)]
                    if add:
                        nc.vector.tensor_tensor(to, ps[r][:, 0:n], to, ALU.add).then_inc(out_dve, 1)
                    else:
                        nc.vector.tensor_copy(to, ps[r][:, 0:n]).then_inc(out_dve, 1)
                if side:
                    side.between(dve, b)
            blocks(dve, step)

        @block.tensor
        def _(pe):
            def step(b, n, after):
                for k in range(KC):
                    pe.wait_ge(lo_done, KC * b + k + 1)
                    hi, lo = whi[:, k % RING, 0:n], wlo[:, k % RING, 0:n]
                    for r in range(RT):
                        if k == 0 and not (isinstance(b, int) and b == 0):
                            if add:
                                pe.wait_ge(out_dve, RT * (b - 1) + r + 1)
                            else:
                                pe.wait_ge(out_dve if r % 2 else out_act, RT // 2 * (b - 1) + r // 2 + 1)
                        rows = slice(r * P, (r + 1) * P)
                        nc.tensor.matmul(ps[r][:, 0:n], Thi[:, k, rows], hi, start=(k == 0), stop=False)
                        nc.tensor.matmul(ps[r][:, 0:n], Thi[:, k, rows], lo, start=False, stop=False)
                        last = nc.tensor.matmul(ps[r][:, 0:n], Tlo[:, k, rows], hi, start=False, stop=(k == KC - 1))
                        if k == KC - 1:
                            last.then_inc(summed, 1)
                        elif r == RT - 1:
                            last.then_inc(used, 1)
            blocks(pe, step)


def mlp(nc, env, tag, weights):
    X, Thi, Tlo = env["X"], env["Thi"], env["Tlo"]
    NBLK = FC // 2
    HEAD, BODY = 3, 6
    with ExitStack() as ctx:
        def sem(n):
            return new_sem(nc, env, f"{tag}_{n}")

        mem = Mem(nc, Map.Z, Map.T)
        uhi = mem.take(f"{tag}_uhi", [P, 4, SEQ], F32R)
        ulo = mem.take(f"{tag}_ulo", [P, 4, SEQ], F32R)
        dhi = mem.take(f"{tag}_dhi", [P, 4, D], F32R)
        dlo = mem.take(f"{tag}_dlo", [P, 4, D], F32R)
        relu = mem.take(f"{tag}_relu", [P, 4, NB], F32)
        mem, raw, up_in, down_in = weights.mem, weights.raw, weights.up_in, weights.down_in
        phi = mem.take(f"{tag}_phi", [P, 2, D], F32R)
        plo = mem.take(f"{tag}_plo", [P, 2, D], F32R)
        psu = [ctx.enter_context(nc.psum_tensor(f"{tag}_psu{i}", [P, NB], F32)) for i in range(4)]
        psd = [ctx.enter_context(nc.psum_tensor(f"{tag}_psd{i}", [P, NB], F32)) for i in range(4)]
        up_hi, up_lo, down_hi, down_lo = map(sem, ("up_hi", "up_lo", "down_hi", "down_lo"))
        up_sum, relu_done, square, u_hi, u_lo, down_sum, added = map(
            sem, ("up_sum", "relu_done", "square", "u_hi", "u_lo", "down_sum", "added"))
        block = ctx.enter_context(nc.Block())

        def first(b, count=1):
            return isinstance(b, int) and b < count

        def blocks(eng, step):
            for b in range(HEAD):
                step(b, b % 2)
            with eng.Fori(0, BODY) as j:
                step(2 * j + HEAD, HEAD % 2)
                step(2 * j + HEAD + 1, (HEAD + 1) % 2)
            for b in range(HEAD + 2 * BODY, NBLK):
                step(b, b % 2)

        @block.sync
        def _(sp):
            def step(b, s):
                if not first(b):
                    weights.load_block(sp, b, lambda c: sp.wait_ge(up_lo, 2 * b - 1 + c),
                                       lambda c: sp.wait_ge(down_lo, 2 * b - 1 + c))
            blocks(sp, step)

        @block.scalar
        def _(act):
            def split_up(b, c):
                act.wait_ge(up_in[c], 16 * (b + 1))
                if not first(b):
                    act.wait_ge(up_sum, 4 * b - 2 + 2 * c)
                nc.scalar.activation(phi[:, c, :], raw[:, c, :], ACT.Copy).then_inc(up_hi, 1)

            def step(b, s):
                if first(b):
                    split_up(b, 0)
                    split_up(b, 1)
                for n in range(4):
                    c, half = divmod(n, 2)
                    act.wait_ge(up_sum, 4 * b + n + 1)
                    if not first(b):
                        act.wait_ge(u_lo, 4 * b + n - 3)
                    nc.scalar.activation(relu[:, n, :], psu[n][:, :], ACT.Relu).then_inc(relu_done, 1)
                    if half:
                        if not (isinstance(b, int) and b == NBLK - 1):
                            split_up(b + 1, c)
                    act.wait_ge(square, 4 * b + n + 1)
                    if n == 0 and not first(b, 2):
                        act.wait_ge(down_sum, 16 * (b - 1))
                    nc.scalar.activation(uhi[:, 2 * s + c, half * NB:(half + 1) * NB], relu[:, n, :],
                                         ACT.Copy).then_inc(u_hi, 1)
                for c in range(2):
                    act.wait_ge(down_in[c], 16 * (b + 1))
                    nc.scalar.activation(dhi[:, 2 * s + c, :], raw[:, 2 + c, :], ACT.Copy).then_inc(down_hi, 1)
            blocks(act, step)

        @block.vector
        def _(dve):
            def split_up(b, c):
                dve.wait_ge(up_hi, 2 * b + c + 1)
                nc.vector.tensor_tensor(plo[:, c, :], raw[:, c, :], f32(phi[:, c, :]), ALU.subtract).then_inc(up_lo, 1)

            def add_down(b, first_group, count):
                for n in range(first_group, first_group + count):
                    r, half = divmod(n, 2)
                    dve.wait_ge(down_sum, 16 * b + n + 1)
                    to = X[:, r, half * NB:(half + 1) * NB]
                    nc.vector.tensor_tensor(to, psd[n % 4][:, :], to, ALU.add).then_inc(added, 1)

            def step(b, s):
                if first(b):
                    split_up(b, 0)
                    split_up(b, 1)
                for n in range(4):
                    c, half = divmod(n, 2)
                    dve.wait_ge(relu_done, 4 * b + n + 1)
                    nc.vector.tensor_tensor(relu[:, n, :], relu[:, n, :], relu[:, n, :], ALU.mult).then_inc(square, 1)
                    dve.wait_ge(u_hi, 4 * b + n + 1)
                    part = slice(half * NB, (half + 1) * NB)
                    nc.vector.tensor_tensor(ulo[:, 2 * s + c, part], relu[:, n, :], f32(uhi[:, 2 * s + c, part]),
                                            ALU.subtract).then_inc(u_lo, 1)
                    if half and not (isinstance(b, int) and b == NBLK - 1):
                        split_up(b + 1, c)
                for c in range(2):
                    dve.wait_ge(down_hi, 2 * b + c + 1)
                    nc.vector.tensor_tensor(dlo[:, 2 * s + c, :], raw[:, 2 + c, :], f32(dhi[:, 2 * s + c, :]),
                                            ALU.subtract).then_inc(down_lo, 1)
                if not first(b):
                    add_down(b - 1, 0, 16)
            blocks(dve, step)
            add_down(NBLK - 1, 0, 16)

        @block.tensor
        def _(pe):
            def up(b, s):
                for c in range(2):
                    pe.wait_ge(up_lo, 2 * b + c + 1)
                    for half in range(2):
                        n = 2 * c + half
                        if not first(b):
                            pe.wait_ge(relu_done, 4 * b + n - 3)
                        cols = slice(half * NB, (half + 1) * NB)
                        for k in range(KC):
                            hi, lo = phi[:, c, k * P:(k + 1) * P], plo[:, c, k * P:(k + 1) * P]
                            nc.tensor.matmul(psu[n][:, :], hi, Thi[:, k, cols], start=(k == 0), stop=False)
                            nc.tensor.matmul(psu[n][:, :], hi, Tlo[:, k, cols], start=False, stop=False)
                            last = nc.tensor.matmul(psu[n][:, :], lo, Thi[:, k, cols], start=False, stop=(k == KC - 1))
                        last.then_inc(up_sum, 1)

            def down(b, s):
                pe.wait_ge(u_lo, 4 * b + 4)
                pe.wait_ge(down_lo, 2 * b + 2)
                for n in range(16):
                    r, half = divmod(n, 2)
                    if not (first(b) and n < 4):
                        pe.wait_ge(added, 16 * b + n - 3)
                    rows, cols = slice(r * P, (r + 1) * P), slice(half * NB, (half + 1) * NB)
                    for c in range(2):
                        q = 2 * s + c
                        nc.tensor.matmul(psd[n % 4][:, :], uhi[:, q, rows], dhi[:, q, cols], start=(c == 0), stop=False)
                        nc.tensor.matmul(psd[n % 4][:, :], uhi[:, q, rows], dlo[:, q, cols], start=False, stop=False)
                        last = nc.tensor.matmul(psd[n % 4][:, :], ulo[:, q, rows], dhi[:, q, cols], start=False, stop=(c == 1))
                    last.then_inc(down_sum, 1)

            def step(b, s):
                up(b, s)
                if not first(b):
                    down(b - 1, 1 - s)
            blocks(pe, step)
            down(NBLK - 1, (NBLK - 1) % 2)


def final_norm(nc, env, g_dram, out):
    X = env["X"]
    with ExitStack() as ctx:
        def sem(n):
            return new_sem(nc, env, f"final_{n}")

        mem = Mem(nc, Map.Z, Map.W)
        y = mem.take("final_y", [P, RT, D], F32)
        g = mem.take("final_g", [P, D], F32)
        ss = mem.take("final_ss", [P, RT], F32)
        st = mem.take("final_st", [P, 3, RT], F32)
        sums = [sem(f"sums{h}") for h in range(2)]
        g_in, var, root, rstd, y_done, y_out = map(sem, ("g_in", "var", "root", "rstd", "y_done", "y_out"))
        block = ctx.enter_context(nc.Block())

        @block.sync
        def _(sp):
            sp.dma_start(g[:, :], g_dram.rearrange("(a d) -> a d", a=1).broadcast_to([P, D])).then_inc(g_in, 16)
            for r in range(RT):
                sp.wait_ge(y_done, r + 1)
                sp.dma_start(out[r * P:(r + 1) * P, :], y[:, r, :]).then_inc(y_out, 16)
            sp.wait_ge(y_out, 16 * RT)

        @block.scalar
        def _(act):
            for r in range(0, RT, 2):
                nc.scalar.activation(y[:, r, :], X[:, r, :], ACT.Square, accum_out=ss[:, r:r + 1]).then_inc(sums[r // 4], 1)
                if r % 4 == 2:
                    part = slice(r - 2, r + 2)
                    act.wait_ge(var, r // 4 + 1)
                    nc.scalar.activation(st[:, 1, part], st[:, 0, part], ACT.Sqrt).then_inc(root, 1)

        @block.vector
        def _(dve):
            for half in range(2):
                part = slice(4 * half, 4 * half + 4)
                for r in range(4 * half + 1, 4 * half + 4, 2):
                    nc.vector.tensor_tensor_reduce(y[:, r, :], X[:, r, :], X[:, r, :], 1.0, 0.0, ALU.mult,
                                                   ALU.add, ss[:, r:r + 1]).then_inc(sums[half], 1)
                dve.wait_ge(sums[half], 4)
                nc.vector.tensor_scalar(st[:, 0, part], ss[:, part], 1.0 / D, EPS, ALU.mult, ALU.add).then_inc(var, 1)
                dve.wait_ge(root, half + 1)
                inverse_root(nc, dve, st[:, :, part], rstd, 5 * half)
                dve.wait_ge(g_in, 16)
                for r in range(4 * half, 4 * half + 4):
                    nc.vector.scalar_tensor_tensor(y[:, r, :], X[:, r, :], st[:, 2, r:r + 1], g[:, :], ALU.mult,
                                                   ALU.mult).then_inc(y_done, 1)


def spread(ap, shape):
    return ap.broadcast_to(shape)


def rotary_tables(nc, env, positions):
    cos, sin = env["cos"], env["sin"]
    freq = [float(np.float32(THETA ** (-2.0 * i / ROT))) for i in range(NF)]
    two_pi = 2.0 * np.pi
    c1 = 6.28125
    c2 = round((two_pi - c1) * 2 ** 17) / 2.0 ** 17
    c3 = float(np.float32(two_pi - c1 - c2))
    to_int = 1.5 * 2 ** 23
    lim = float(np.nextafter(np.float32(np.pi), np.float32(0)))
    with ExitStack() as ctx:
        mem = Mem(nc, Map.W, Map.SMALL)
        pos_i = mem.take("rot_pos_i", [P, RT], I32)
        pos = mem.take("rot_pos", [P, RT], F32)
        ang, mult, r, arg = (mem.take(f"rot_{n}", [P, RT, NF], F32) for n in ("ang", "mult", "r", "arg"))
        pos_in, made, r_done, arg_done, tables = (new_sem(nc, env, f"rot_{n}") for n in (
            "pos_in", "made", "r_done", "arg_done", "tables"))
        block = ctx.enter_context(nc.Block())

        @block.sync
        def _(sp):
            sp.dma_start(pos_i[:, :], positions.rearrange("(r p) -> p r", p=P),
                         allow_slow_non_contiguous=True).then_inc(pos_in, 16)

        @block.vector
        def _(dve):
            dve.wait_ge(pos_in, 16)
            nc.vector.tensor_copy(pos[:, :], pos_i[:, :]).then_inc(made, 1)
            dve.wait_ge(made, 1)
            for f in range(NF):
                nc.vector.tensor_scalar(ang[:, :, f], pos[:, :], freq[f], None, ALU.mult).then_inc(made, 1)
            dve.wait_ge(made, 1 + NF)
            nc.vector.tensor_scalar(mult[:, :, :], ang[:, :, :], 1.0 / two_pi, to_int, ALU.mult, ALU.add).then_inc(made, 1)
            dve.wait_ge(made, 2 + NF)
            nc.vector.tensor_scalar(mult[:, :, :], mult[:, :, :], to_int, None, ALU.subtract).then_inc(made, 1)
            for n, c in enumerate((c1, c2, c3)):
                dve.wait_ge(made, 3 + NF + n)
                nc.vector.scalar_tensor_tensor(r[:, :, :], mult[:, :, :], -c, (r if n else ang)[:, :, :], ALU.mult,
                                               ALU.add).then_inc(made, 1)
            dve.wait_ge(made, 6 + NF)
            nc.vector.tensor_scalar(r[:, :, :], r[:, :, :], lim, -lim, ALU.min, ALU.max).then_inc(r_done, 1)
            dve.wait_ge(r_done, 1)
            nc.vector.scalar_tensor_tensor(arg[:, :, :], r[:, :, :], -1.0, r[:, :, :], ALU.mult, ALU.min).then_inc(made, 1)
            dve.wait_ge(made, 7 + NF)
            nc.vector.tensor_scalar(arg[:, :, :], arg[:, :, :], float(np.pi / 2), None, ALU.add).then_inc(arg_done, 1)

        @block.scalar
        def _(act):
            act.wait_ge(r_done, 1)
            nc.scalar.activation(sin[:, :, :], r[:, :, :], ACT.Sin).then_inc(tables, 1)
            act.wait_ge(arg_done, 1)
            nc.scalar.activation(cos[:, :, :], arg[:, :, :], ACT.Sin).then_inc(tables, 1)


def rotate(nc, eng, env, z, col, heads, tmp, done, base, tiles=range(RT)):
    if base:
        eng.wait_ge(done, base)
    parts = []
    for n, r in enumerate(tiles):
        v = z[:, r, col:col + heads * HD].rearrange("p (h d) -> p h d", d=HD)
        t1, t2 = v[:, :, 0:NF], v[:, :, NF:ROT]
        c = spread(env["cos"][:, r, :].unsqueeze(1), [P, heads, NF])
        s = spread(env["sin"][:, r, :].unsqueeze(1), [P, heads, NF])
        q = [tmp[:, 4 * n + j, 0:heads * NF].rearrange("p (h f) -> p h f", f=NF) for j in range(4)]
        for j, (a, b) in enumerate(((t1, c), (t2, s), (t2, c), (t1, s))):
            eng.tensor_tensor(q[j], a, b, ALU.mult).then_inc(done, 1)
        parts.append((t1, t2, q))
    for n, (t1, t2, q) in enumerate(parts):
        if n == 0:
            eng.wait_ge(done, base + 4 * len(parts))
        eng.tensor_tensor(t1, q[0], q[1], ALU.subtract).then_inc(done, 1)
        eng.tensor_tensor(t2, q[2], q[3], ALU.add).then_inc(done, 1)


class MlstmPrelude:

    def __init__(self, nc, env, t, mem):
        self.nc, self.Z, self.ident, self.t = nc, env["Z"], env["ident"], t
        H = B_HEADS
        self.xT = mem.take("ml_xT", [P, 4, CONV - 1 + SEQ], F32)
        self.qk = mem.take("ml_qk", [P, 4, SEQ], F32)
        self.fr, self.ir, self.br, self.mk, self.mk2 = (
            mem.take(f"ml_{n}", [H, SEQ], F32) for n in ("fr", "ir", "br", "mk", "mk2"))
        self.cw = mem.take("ml_cw", [P, CONV, 4], F32)
        self.cb = mem.take("ml_cb", [P, 4], F32)
        self.bi = mem.take("ml_bi", [H, 2], F32)
        (self.par_in, self.padded, self.mark, self.g_turned, self.gates_in, self.x_turned, self.xT_done, self.conved,
         self.ga, self.ge, self.gl, self.gd, self.silu_s, self.silu_m, self.gate_s) = (new_sem(nc, env, f"mlp_{n}") for n in (
             "par_in", "padded", "mark", "g_turned", "gates_in", "x_turned", "xT_done", "conved", "ga", "ge", "gl", "gd", "silu_s", "silu_m",
             "gate_s"))

    def load(self, sp):
        t = self.t
        sp.dma_start(self.cw[:, :, :], t["even_conv_w"][0].rearrange("t (c p) -> p t c", p=P),
                     allow_slow_non_contiguous=True).then_inc(self.par_in, 16)
        sp.dma_start(self.cb[:, :], t["even_conv_b"][0].rearrange("(c p) -> p c", p=P),
                     allow_slow_non_contiguous=True).then_inc(self.par_in, 16)
        sp.dma_start(self.bi[:, 0:1], t["even_bias_f"][0].rearrange("(h o) -> h o", o=1)).then_inc(self.par_in, 16)
        sp.dma_start(self.bi[:, 1:2], t["even_bias_i"][0].rearrange("(h o) -> h o", o=1)).then_inc(self.par_in, 16)

    def pool(self, pool):
        nc = self.nc
        nc.gpsimd.memset(self.xT[:, :, 0:CONV - 1], 0.0).then_inc(self.padded, 1)
        nc.gpsimd.memset(self.mk[:, :], 1.0).then_inc(self.mark, 1)
        pool.wait_ge(self.mark, 1)
        nc.gpsimd.memset(self.mk[:, 0:SEQ:P], 0.0).then_inc(self.mark, 1)


    def tensor(self, pe, banks):
        nc = self.nc
        for n, col in enumerate((EBF, EBI)):
            for r in range(RT):
                last = nc.tensor.transpose(banks[2 * n + r // 4][0:B_HEADS, (r % 4) * P:(r % 4 + 1) * P],
                                           self.Z[:, r, col:col + B_HEADS], self.ident[:, :])
                if r % 4 == 3:
                    last.then_inc(self.g_turned, 1)
        for n in range(8):
            c, half = divmod(n, 2)
            if n >= 4:
                pe.wait_ge(self.gates_in, n - 3)
            for r in range(4):
                last = nc.tensor.transpose(banks[(4 + n) % 8][:, r * P:(r + 1) * P],
                                           self.Z[:, 4 * half + r, EBQK + c * P:EBQK + (c + 1) * P], self.ident[:, :])
            last.then_inc(self.x_turned, 1)
        pe.wait_ge(self.xT_done, 8)

    def scalar(self, act, banks):
        nc = self.nc
        act.wait_ge(self.par_in, 64)
        for n, row in enumerate((self.fr, self.ir)):
            for half in range(2):
                act.wait_ge(self.g_turned, 2 * n + half + 1)
                nc.scalar.activation(row[:, half * NB:(half + 1) * NB], banks[2 * n + half][0:B_HEADS, :], ACT.Identity,
                                     bias=self.bi[:, n:n + 1]).then_inc(self.gates_in, 1)
        for n in range(8):
            c, half = divmod(n, 2)
            act.wait_ge(self.x_turned, n + 1)
            nc.scalar.activation(self.xT[:, c, CONV - 1 + half * NB:CONV - 1 + (half + 1) * NB], banks[(4 + n) % 8],
                                 ACT.Copy).then_inc(self.xT_done, 1)

    def scalar_gates(self, act):
        nc = self.nc
        act.wait_ge(self.ga, 1)
        nc.scalar.activation(self.mk2[:, :], self.br[:, :], ACT.Exp, scale=-1.0).then_inc(self.ge, 1)
        act.wait_ge(self.ge, 1)
        nc.scalar.activation(self.mk2[:, :], self.mk2[:, :], ACT.Ln, bias=1.0).then_inc(self.gl, 1)

    def scalar_sigmoids(self, act):
        nc = self.nc
        for c in range(4):
            act.wait_ge(self.conved, CONV * (c + 1))
            nc.scalar.activation(self.xT[:, c, CONV - 1:], self.qk[:, c, :], ACT.Sigmoid).then_inc(self.silu_s, 1)
        for r in range(RT):
            o = self.Z[:, r, EBO:EBO + NB]
            nc.scalar.activation(o, o, ACT.Sigmoid).then_inc(self.gate_s, 1)

    def vector_abs(self, dve):
        dve.wait_ge(self.gates_in, 2)
        self.nc.vector.scalar_tensor_tensor(self.br[:, :], self.fr[:, :], -1.0, self.fr[:, :], ALU.mult,
                                            ALU.max).then_inc(self.ga, 1)

    def vector(self, dve, i):
        nc = self.nc
        fr, ir, br, mk, mk2, gd = self.fr, self.ir, self.br, self.mk, self.mk2, self.gd
        if i < 4:
            if i == 0:
                dve.wait_ge(self.padded, 1)
                dve.wait_ge(self.par_in, 64)
            dve.wait_ge(self.xT_done, 2 * i + 2)
            nc.vector.tensor_scalar(self.qk[:, i, :], self.xT[:, i, CONV - 1:], self.cw[:, CONV - 1, i:i + 1],
                                    self.cb[:, i:i + 1], ALU.mult, ALU.add).then_inc(self.conved, 1)
            for tap in range(CONV - 1):
                dve.wait_ge(self.conved, CONV * i + 1 + tap)
                nc.vector.scalar_tensor_tensor(self.qk[:, i, :], self.xT[:, i, tap:tap + SEQ], self.cw[:, tap, i:i + 1],
                                               self.qk[:, i, :], ALU.mult, ALU.add).then_inc(self.conved, 1)
        if i == 4:
            dve.wait_ge(self.gl, 1)
            nc.vector.scalar_tensor_tensor(fr[:, :], fr[:, :], 0.0, mk2[:, :], ALU.min, ALU.subtract).then_inc(gd, 1)
            dve.wait_ge(gd, 1)
            dve.wait_ge(self.mark, 2)
            nc.vector.tensor_tensor_scan(br[:, :], mk[:, :], fr[:, :], 0.0, ALU.mult, ALU.add).then_inc(gd, 1)
        if i == 5:
            dve.wait_ge(gd, 2)
            dve.wait_ge(self.gates_in, 4)
            nc.vector.tensor_tensor(ir[:, :], ir[:, :], br[:, :], ALU.subtract).then_inc(gd, 1)
            nc.vector.memset(mk[:, :], 0.0).then_inc(gd, 1)
        if i == 6:
            dve.wait_ge(gd, 4)
            nc.vector.tensor_copy(mk[:, P:SEQ:P], br[:, P - 1:SEQ - 1:P]).then_inc(gd, 1)
            dve.wait_ge(gd, 5)
            nc.vector.tensor_tensor_scan(fr[:, :], mk[:, :], ir[:, :], 0.0, ALU.add, ALU.max).then_inc(gd, 1)
        if i in (6, 7):
            for c in (0, 1) if i == 6 else (2, 3):
                dve.wait_ge(self.silu_s, c + 1)
                nc.vector.tensor_tensor(self.qk[:, c, :], self.qk[:, c, :], self.xT[:, c, CONV - 1:],
                                        ALU.mult).then_inc(self.silu_m, 1)


def window_attention(nc, env, sinks, prelude, mem):
    Z, ident = env["Z"], env["ident"]
    KW = CHUNK + SEQ
    with ExitStack() as ctx:
        def sem(n):
            return new_sem(nc, env, f"wa_{n}")

        tmp = mem.take("wa_tmp", [P, 4, RT, (A_HEADS + A_KV) * NF], F32)
        kT = mem.take("wa_kT", [P, A_KV, KW], F32)
        vs = mem.take("wa_vs", [P, RT, P], F32)
        qT = mem.take("wa_qT", [P, 2, 4, P], F32)
        prob = mem.take("wa_prob", [P, 2, 2, 4, P], F32)
        probT = mem.take("wa_probT", [P, 2, 8, P], F32)
        sink = mem.take("wa_sink", [P, A_HEADS], F32)
        mx = mem.take("wa_mx", [P, RT, 2, 4], F32)
        esink = mem.take("wa_esink", [P, RT, 2, 4], F32)
        den = mem.take("wa_den", [P, RT, 2, 4], F32)
        ps_s = [ctx.enter_context(nc.psum_tensor(f"wa_ps_s{i}", [P, 4, P], F32)) for i in range(2)]
        ps_t = [ctx.enter_context(nc.psum_tensor(f"wa_ps_t{i}", [P, 4, P], F32)) for i in range(2)]
        ps_q = [ctx.enter_context(nc.psum_tensor(f"wa_ps_q{i}", [P, 4, P], F32)) for i in range(2)]
        ps_o = [ctx.enter_context(nc.psum_tensor(f"wa_ps_o{i}", [P, 8, HD], F32)) for i in range(2)]
        banks = [t[:, :, :].rearrange("p a b -> p (a b)") for t in ps_s + ps_q + ps_t + ps_o]
        (sink_in, rotated, vs_zero, vs_in, k_zero, k_turned, kT_done, q_turned, qT_done, scored, masked, maxed,
         shifted, expd, sunk, summed, inverted, p_turned, pT_done, mixed, written) = map(sem, (
             "sink_in", "rotated", "vs_zero", "vs_in", "k_zero", "k_turned", "kT_done", "q_turned", "qT_done",
             "scored", "masked", "maxed", "shifted", "expd", "sunk", "summed", "inverted", "p_turned", "pT_done",
             "mixed", "written"))
        block = ctx.enter_context(nc.Block())

        @block.sync
        def _(sp):
            prelude.load(sp)
            sp.dma_start(sink[:, :], spread(sinks.rearrange("(a d) -> a d", a=1), [P, A_HEADS])).then_inc(sink_in, 16)
            sp.dma_start(vs[CHUNK:P, :, :], Z[0:CHUNK, :, EV:EV + P]).then_inc(vs_in, 16)
            sp.dma_start(vs[0:CHUNK, 1:RT, :], Z[CHUNK:P, 0:RT - 1, EV:EV + P]).then_inc(vs_in, 16)

        @block.gpsimd
        def _(pool):
            prelude.pool(pool)
            nc.gpsimd.memset(vs[0:CHUNK, 0, :], 0.0).then_inc(vs_zero, 1)
            nc.gpsimd.memset(kT[:, :, 0:CHUNK], 0.0).then_inc(k_zero, 1)

        @block.vector
        def _(dve):
            rotate_all(nc, nc.vector, env, Z, EQ, A_HEADS + A_KV, lambda j: tmp[:, j, :, :], rotated, 0)
            prelude.vector_abs(dve)
            dve.wait_ge(sink_in, 16)

            def finish(i):
                dve.wait_ge(mixed, i + 1)
                dve.wait_ge(inverted, 2 * i + 2)
                rinv = spread(den[:, i, :, :].rearrange("p a c -> p c a").unsqueeze(3), [P, 4, 2, HD])
                nc.vector.tensor_tensor(Z[:, i, 0:NB].rearrange("p (c a d) -> p c a d", c=4, a=2),
                                        ps_o[i % 2][:, :, :].rearrange("p (c a) d -> p c a d", a=2), rinv,
                                        ALU.mult).then_inc(written, 1)

            for i in range(RT):
                dve.wait_ge(scored, i + 1)
                if i == 0:
                    for a in range(2):
                        nc.vector.memset(ps_s[a][0:CHUNK, :, 0:CHUNK], -1e30).then_inc(masked, 1)
                    dve.wait_ge(masked, 2)
                for a in range(2):
                    nc.vector.tensor_reduce(mx[:, i, a, :], ps_s[a][:, :, :], AX.X, ALU.max).then_inc(maxed, 1)
                dve.wait_ge(maxed, 3 * i + 2)
                nc.vector.tensor_tensor(mx[:, i, :, :], mx[:, i, :, :], sink[:, :].rearrange("p (c a) -> p a c", a=2),
                                        ALU.max).then_inc(maxed, 1)
                dve.wait_ge(maxed, 3 * i + 3)
                if i >= 2:
                    dve.wait_ge(p_turned, 2 * i - 2)
                for a in range(2):
                    nc.vector.tensor_tensor(prob[:, i % 2, a, :, :], ps_s[a][:, :, :],
                                            spread(mx[:, i, a, :].unsqueeze(2), [P, 4, P]), ALU.subtract).then_inc(shifted, 1)
                nc.vector.tensor_tensor(esink[:, i, :, :], sink[:, :].rearrange("p (c a) -> p a c", a=2), mx[:, i, :, :],
                                        ALU.subtract).then_inc(shifted, 1)
                prelude.vector(dve, i)
                if i >= 1:
                    finish(i - 1)
                dve.wait_ge(expd, 2 * i + 2)
                for a in range(2):
                    nc.vector.tensor_reduce(den[:, i, a, :], prob[:, i % 2, a, :, :], AX.X, ALU.add).then_inc(summed, 1)
                dve.wait_ge(summed, 2 * i + 2)
                dve.wait_ge(sunk, i + 1)
                nc.vector.tensor_tensor(den[:, i, :, :], den[:, i, :, :], esink[:, i, :, :], ALU.add).then_inc(inverted, 1)
                dve.wait_ge(inverted, 2 * i + 1)
                nc.vector.reciprocal(den[:, i, :, :], den[:, i, :, :]).then_inc(inverted, 1)
            finish(RT - 1)

        @block.scalar
        def _(act):
            prelude.scalar(act, banks)
            for g in range(A_KV):
                for half in range(2):
                    act.wait_ge(k_turned, 2 * g + half + 1)
                    nc.scalar.activation(kT[:, g, CHUNK + half * NB:CHUNK + (half + 1) * NB], ps_t[half][:, :, :],
                                         ACT.Copy).then_inc(kT_done, 1)
            def queries(i):
                act.wait_ge(q_turned, i + 1)
                if i >= 2:
                    act.wait_ge(scored, i - 1)
                nc.scalar.activation(qT[:, i % 2, :, :], ps_q[i % 2][:, :, :], ACT.Copy, scale=HD ** -0.5).then_inc(qT_done, 1)

            queries(0)
            queries(1)
            for i in range(RT):
                for a in range(2):
                    act.wait_ge(shifted, 3 * i + 1 + a)
                    nc.scalar.activation(prob[:, i % 2, a, :, :], prob[:, i % 2, a, :, :], ACT.Exp).then_inc(expd, 1)
                act.wait_ge(shifted, 3 * i + 3)
                nc.scalar.activation(esink[:, i, :, :], esink[:, i, :, :], ACT.Exp).then_inc(sunk, 1)
                if i == 1:
                    prelude.scalar_gates(act)
                if i == 5:
                    prelude.scalar_sigmoids(act)
                if i + 2 < RT:
                    queries(i + 2)
                if i >= 2:
                    act.wait_ge(mixed, i - 1)
                for a in range(2):
                    act.wait_ge(p_turned, 2 * i + a + 1)
                    nc.scalar.activation(probT[:, i % 2, 4 * a:4 * a + 4, :], ps_t[a][:, :, :], ACT.Copy).then_inc(pT_done, 1)

        @block.tensor
        def _(pe):
            prelude.tensor(pe, banks)
            pe.wait_ge(rotated, 6)
            for g in range(A_KV):
                for half in range(2):
                    if g:
                        pe.wait_ge(kT_done, half + 1)
                    for r in range(4):
                        last = turn_twice(nc, ps_t[half][:, r, :], Z[:, 4 * half + r, EK + g * HD:EK + (g + 1) * HD], ident)
                    last.then_inc(k_turned, 1)

            def queries(i):
                if i >= 2:
                    pe.wait_ge(qT_done, i - 1)
                for c in range(4):
                    last = nc.tensor.transpose(ps_q[i % 2][:, c, :], Z[:, i, c * P:(c + 1) * P], ident[:, :])
                last.then_inc(q_turned, 1)

            def scores(i):
                pe.wait_ge(qT_done, i + 1)
                if i:
                    pe.wait_ge(shifted, 3 * i - 1)
                for c in range(4):
                    for a in range(2):
                        g = (2 * c + a) // 4
                        rows = slice(a * CHUNK, (a + 1) * CHUNK)
                        for u in range(2):
                            at = i * P + u * CHUNK
                            last = nc.tensor.matmul(ps_s[a][u * CHUNK:(u + 1) * CHUNK, c, :],
                                                    qT[rows, i % 2, c, u * CHUNK:(u + 1) * CHUNK],
                                                    kT[rows, g, at:at + P], start=True, stop=True)
                last.then_inc(scored, 1)

            def turn(i):
                for a in range(2):
                    pe.wait_ge(expd, 2 * i + a + 1)
                    if i:
                        pe.wait_ge(pT_done, 2 * i - 1 + a)
                    for c in range(4):
                        last = nc.tensor.transpose(ps_t[a][:, c, :], prob[:, i % 2, a, c, :], ident[:, :])
                    last.then_inc(p_turned, 1)

            def mix(i):
                pe.wait_ge(pT_done, 2 * i + 2)
                if i >= 2:
                    pe.wait_ge(written, i - 1)
                for u in range(2):
                    for a in range(2):
                        for c in range(4):
                            h = 2 * c + a
                            g = h // 4
                            v = Z[:, i, EV + g * HD:EV + (g + 1) * HD] if u else vs[:, i, g * HD:(g + 1) * HD]
                            last = nc.tensor.matmul(ps_o[i % 2][u * CHUNK:(u + 1) * CHUNK, h, :],
                                                    probT[:, i % 2, 4 * a + c, u * CHUNK:(u + 1) * CHUNK], v,
                                                    start=True, stop=True)
                last.then_inc(mixed, 1)

            queries(0)
            queries(1)
            pe.wait_ge(kT_done, 4)
            pe.wait_ge(k_zero, 1)
            pe.wait_ge(vs_zero, 1)
            pe.wait_ge(vs_in, 32)
            for i in range(RT):
                scores(i)
                if i + 2 < RT:
                    queries(i + 2)
                if i:
                    mix(i - 1)
                turn(i)
            mix(RT - 1)


def mlstm(nc, env, prelude, mem):
    Z, ident = env["Z"], env["ident"]
    H = B_HEADS
    with ExitStack() as ctx:
        def sem(n):
            return new_sem(nc, env, f"ml_{n}")

        qk, fr, ir, br = prelude.qk, prelude.fr, prelude.ir, prelude.br
        va = mem.take("ml_va", [P, RT, H, B_DV + 1], F32)
        E = mem.take("ml_E", [P, 2, H, P], F32)
        Wt = mem.take("ml_W", [P, 2, H, P], F32)
        dg = mem.take("ml_dg", [P, H, P], F32)
        late = mem.take("ml_late", [P, P], F32)
        sel = mem.take("ml_sel", [H, H, P], F32)
        last_row = mem.take("ml_last_row", [P, P], F32)
        nat = mem.take("ml_nat", [P, 3, RT, H], F32)
        total = mem.take("ml_total", [P, RT, H], F32)
        G = mem.take("ml_G", [P, RT, RT, H], F32)
        emn = mem.take("ml_emn", [P, RT, H], F32)
        den = mem.take("ml_den", [P, RT, H], F32)
        ps_s = [ctx.enter_context(nc.psum_tensor(f"ml_ps_s{i}", [P, 2, NB], F32)) for i in range(2)]
        ps_n = ctx.enter_context(nc.psum_tensor("ml_ps_n", [P, 2, NB], F32))
        ps_a = ctx.enter_context(nc.psum_tensor("ml_ps_a", [P, H, P], F32))
        ps_x = ctx.enter_context(nc.psum_tensor("ml_ps_x", [P, NB], F32))
        (consts, back, back_done, tot_mm, tot_done, G_done, emn_sum, emn_done, va_done, a_bc,
         dg_done, e_done, s_done, w_done, mixed, den_abs, den_max, den_inv, written) = map(sem, (
             "consts", "back", "back_done", "tot_mm", "tot_done", "G_done", "emn_sum",
             "emn_done", "va_done", "a_bc", "dg_done", "e_done", "s_done", "w_done", "mixed", "den_abs", "den_max",
             "den_inv", "written"))
        block = ctx.enter_context(nc.Block())
        pairs = [(i, j) for i in range(RT) for j in range(i + 1)]

        @block.gpsimd
        def _(pool):
            nc.gpsimd.memset(sel[:, :, :], 0.0).then_inc(consts, 1)
            nc.gpsimd.memset(last_row[:, :], 0.0).then_inc(consts, 1)
            nc.gpsimd.memset(late[:, :], 0.0).then_inc(consts, 1)
            pool.wait_ge(consts, 3)
            nc.gpsimd.affine_select(out=sel[:, :, :], in_=sel[:, :, :], compare_op=ALU.not_equal, fill=1.0, base=0,
                                    pattern=[[-1, H], [0, P]], channel_multiplier=1).then_inc(consts, 1)
            nc.gpsimd.affine_select(out=last_row[:, :], in_=last_row[:, :], compare_op=ALU.not_equal, fill=1.0,
                                    base=1 - P, pattern=[[0, P]], channel_multiplier=1).then_inc(consts, 1)
            nc.gpsimd.affine_select(out=late[:, :], in_=late[:, :], compare_op=ALU.is_ge, fill=1e30, base=0,
                                    pattern=[[1, P]], channel_multiplier=-1).then_inc(consts, 1)
            nc.gpsimd.memset(va[:, :, :, B_DV:B_DV + 1], 1.0).then_inc(va_done, 1)
            for r in range(RT):
                nc.gpsimd.tensor_copy(va[:, r, :, 0:B_DV],
                                      Z[:, r, EBV:EBV + H * B_DV].rearrange("p (h d) -> p h d", h=H)).then_inc(va_done, 1)

        @block.scalar
        def _(act):
            act.wait_ge(back, 1)
            nc.scalar.activation(nat[:, :, :, :], ps_x[:, 0:3 * RT * H].rearrange("p (a r h) -> p a r h", a=3, r=RT),
                                 ACT.Copy).then_inc(back_done, 1)
            act.wait_ge(emn_sum, 1)
            nc.scalar.activation(emn[:, :, :], emn[:, :, :], ACT.Exp, scale=-1.0).then_inc(emn_done, 1)
            act.wait_ge(G_done, 2 * RT - 1)
            for n, (i, j) in enumerate(pairs):
                if j == 0:
                    act.wait_ge(dg_done, i + 1)
                if n >= 2:
                    act.wait_ge(w_done, n - 1)
                for a in range(2):
                    for c in range(2):
                        h = 2 * c + a
                        src = dg[:, h, :] if j == i else ps_a[:, h, :]
                        nc.scalar.activation(E[:, n % 2, 2 * a + c, :], src, ACT.Exp, scale=-1.0,
                                             bias=G[:, i, j, h:h + 1]).then_inc(e_done, 1)

        @block.vector
        def _(dve):
            dve.wait_ge(back_done, 1)
            nc.vector.tensor_tensor(emn[:, :, :], nat[:, 1, :, :], nat[:, 2, :, :], ALU.add).then_inc(emn_sum, 1)
            dve.wait_ge(tot_mm, 1)
            nc.vector.tensor_copy(total[:, :, :], ps_x[:, P:P + RT * H].rearrange("p (r h) -> p r h", h=H)).then_inc(tot_done, 1)
            dve.wait_ge(tot_done, 1)
            for i in range(RT):
                if i:
                    dve.wait_ge(G_done, 2 * i - 1)
                    nc.vector.tensor_tensor(G[:, i, 0:i, :], G[:, i - 1, 0:i, :],
                                            spread(total[:, i - 1, :].unsqueeze(1), [P, i, H]), ALU.add).then_inc(G_done, 1)
                nc.vector.tensor_copy(G[:, i, i, :], nat[:, 0, i, :]).then_inc(G_done, 1)
            dve.wait_ge(consts, 6)

            def diagonal(i):
                dve.wait_ge(a_bc, i + 1)
                if i:
                    dve.wait_ge(e_done, 4 * pairs.index((i - 1, i - 1)) + 4)
                nc.vector.tensor_tensor(dg[:, :, :], ps_a[:, :, :], spread(late[:, :].unsqueeze(1), [P, H, P]),
                                        ALU.add).then_inc(dg_done, 1)

            def finish(i):
                dve.wait_ge(mixed, pairs.index((i, i)) + 1)
                num = ps_n[:, :, 0:2 * (B_DV + 1)].rearrange("p a (c d) -> p a c d", d=B_DV + 1)
                d = den[:, i, :].rearrange("p (a c) -> p a c", a=2)
                dve.wait_ge(emn_done, 1)
                nc.vector.scalar_tensor_tensor(d, num[:, :, :, B_DV], -1.0, emn[:, i, :].rearrange("p (c a) -> p a c", a=2),
                                               ALU.mult, ALU.max).then_inc(den_abs, 1)
                dve.wait_ge(den_abs, i + 1)
                nc.vector.tensor_tensor(d, num[:, :, :, B_DV], d, ALU.max).then_inc(den_max, 1)
                dve.wait_ge(den_max, i + 1)
                nc.vector.reciprocal(den[:, i, :], den[:, i, :]).then_inc(den_inv, 1)
                dve.wait_ge(den_inv, i + 1)
                for a in range(2):
                    for c in range(2):
                        h = 2 * c + a
                        o = Z[:, i, EBO + h * B_DV:EBO + (h + 1) * B_DV]
                        nc.vector.scalar_tensor_tensor(o, num[:, a, c, 0:B_DV], den[:, i, 2 * a + c:2 * a + c + 1], o,
                                                       ALU.mult, ALU.mult).then_inc(written, 1)

            for n, (i, j) in enumerate(pairs):
                if j == 0:
                    diagonal(i)
                dve.wait_ge(s_done, n + 1)
                dve.wait_ge(e_done, 4 * n + 4)
                if n >= 2:
                    dve.wait_ge(mixed, n - 1)
                nc.vector.scalar_tensor_tensor(
                    Wt[:, n % 2, :, :], ps_s[n % 2][:, :, 0:2 * P], B_DK ** -0.5,
                    E[:, n % 2, :, :].rearrange("p (a c) t -> p a (c t)", a=2), ALU.mult, ALU.mult).then_inc(w_done, 1)
                if j == 0 and i:
                    finish(i - 1)
            finish(RT - 1)

        @block.tensor
        def _(pe):
            for n, row in enumerate((ir, br, fr)):
                for r in range(RT):
                    last = nc.tensor.transpose(ps_x[:, (n * RT + r) * H:(n * RT + r + 1) * H], row[:, r * P:(r + 1) * P],
                                               ident[0:H, 0:H])
            last.then_inc(back, 1)
            pe.wait_ge(back_done, 1)
            pe.wait_ge(consts, 6)
            nc.tensor.matmul(ps_x[:, P:P + RT * H], last_row[:, :], nat[:, 1, :, :], start=True, stop=True).then_inc(tot_mm, 1)

            def broadcast(i):
                if i:
                    pe.wait_ge(dg_done, i)
                if i > 1:
                    pe.wait_ge(e_done, 4 * pairs.index((i - 1, i - 1)))
                for h in range(H):
                    last = nc.tensor.matmul(ps_a[:, h, :], sel[:, h, :], fr[:, i * P:(i + 1) * P], start=True, stop=True)
                last.then_inc(a_bc, 1)

            def scores(n):
                i, j = pairs[n]
                if n >= 2:
                    pe.wait_ge(w_done, n - 1)
                for c in range(2):
                    for a in range(2):
                        part = slice(a * B_DK, (a + 1) * B_DK)
                        last = nc.tensor.matmul(ps_s[n % 2][:, a, c * P:(c + 1) * P],
                                                qk[part, 2 + c, j * P:(j + 1) * P], qk[part, c, i * P:(i + 1) * P],
                                                start=True, stop=True)
                last.then_inc(s_done, 1)

            def mix(n):
                i, j = pairs[n]
                pe.wait_ge(w_done, n + 1)
                pe.wait_ge(va_done, 2 + j)
                for a in range(2):
                    if j == 0 and i:
                        pe.wait_ge(written, 4 * (i - 1) + 2 * a + 2)
                    for c in range(2):
                        h = 2 * c + a
                        last = nc.tensor.matmul(ps_n[:, a, c * (B_DV + 1):(c + 1) * (B_DV + 1)],
                                                Wt[:, n % 2, 2 * a + c, :], va[:, j, h, :], start=(j == 0 and c == 0),
                                                stop=(j == i and c == 1), skip_group_check=True)
                last.then_inc(mixed, 1)

            for n, (i, j) in enumerate(pairs):
                if j == 0:
                    broadcast(i)
                scores(n)
                if n:
                    mix(n - 1)
            mix(len(pairs) - 1)


def rotate_all(nc, eng, env, z, col, heads, tmp, done, base):
    v = z[:, :, col:col + heads * HD].rearrange("p r (h d) -> p r h d", d=HD)
    t1, t2 = v[:, :, :, 0:NF], v[:, :, :, NF:ROT]
    c = spread(env["cos"][:, :, :].unsqueeze(2), [P, RT, heads, NF])
    s = spread(env["sin"][:, :, :].unsqueeze(2), [P, RT, heads, NF])
    q = [tmp(j).rearrange("p r (h f) -> p r h f", f=NF) for j in range(4)]
    for j, (a, b) in enumerate(((t1, c), (t2, s), (t2, c), (t1, s))):
        eng.tensor_tensor(q[j], a, b, ALU.mult).then_inc(done, 1)
    eng.wait_ge(done, base + 4)
    eng.tensor_tensor(t1, q[0], q[1], ALU.subtract).then_inc(done, 1)
    eng.tensor_tensor(t2, q[2], q[3], ALU.add).then_inc(done, 1)


INDEX_COLS = ODD_IN - OIQ
ORDER = (0, 7, 2, 3, 1, 6, 5, 4)
GROUPS = ((7, 2, 3), (6, 5, 4))


def key_buffers(nc, env):
    low = Mem(nc, Map.Z + RT * ODD_IN * 4, Map.T)
    high = Mem(nc, Map.W + 24 * KB, Map.SMALL)
    return [{i: (low if i < 5 else high).take(f"{n}{i}", [P, (i + 1) * P], dt) for i in range(EASY, RT)}
            for n, dt in (("hi", I16), ("lo", U16))]


class Selection:

    def __init__(self, nc, env, tag, tiles, hi, lo, mem, junk, pace=0):
        self.nc, self.tiles, self.hi, self.lo, self.junk, self.pace = nc, tiles, hi, lo, junk, pace
        n = len(tiles)
        self.cand, self.count, self.up, self.T, self.TL, self.need = (
            mem.take(f"{tag}_{x}", [P, n], F32) for x in ("cand", "count", "up", "T", "TL", "need"))
        self.step, self.counted, self.masks = (new_sem(nc, env, f"{tag}_{x}") for x in ("step", "counted", "masks"))
        self.work = self.steps()
        self.found = 2 * 16 * (n + 1) + 2 * n
        self.total = self.found + 4 * n
        self.done = 0

    def bisect(self, keys, first, result, n, c):
        nc, m = self.nc, len(self.tiles)
        nc.vector.memset(self.cand[:, :], first).then_inc(self.step, 1)
        n += 1
        bit = 2 ** 15
        while bit:
            self.dve.wait_ge(self.step, n)
            for x, i in enumerate(self.tiles):
                nc.vector.tensor_scalar(self.junk[x][:, 0:(i + 1) * P].bitcast(U16), keys[i][:, :], self.cand[:, x:x + 1],
                                        None, ALU.is_ge, ALU.add, accum_out=self.count[:, x:x + 1]).then_inc(self.counted, 1)
                yield
            c += m
            self.dve.wait_ge(self.counted, c)
            nc.vector.tensor_scalar(self.up[:, :], self.count[:, :], float(TOPK), 0.5, ALU.is_ge,
                                    ALU.subtract).then_inc(self.step, 1)
            n += 1
            self.dve.wait_ge(self.step, n)
            if bit > 1:
                nc.vector.scalar_tensor_tensor(self.cand[:, :], self.up[:, :], float(bit), self.cand[:, :], ALU.mult,
                                               ALU.add).then_inc(self.step, 1)
            else:
                nc.vector.scalar_tensor_tensor(result[:, :], self.up[:, :], -0.5, self.cand[:, :], ALU.add,
                                               ALU.add).then_inc(self.step, 1)
            n += 1
            yield
            bit //= 2

    def steps(self):
        nc, m = self.nc, len(self.tiles)
        yield from self.bisect(self.hi, 0.0, self.T, 0, 0)
        n, c = 33, 16 * m
        self.dve.wait_ge(self.step, n)
        for x, i in enumerate(self.tiles):
            hi, lo, above = self.hi[i][:, :], self.lo[i][:, :], self.junk[x][:, 0:(i + 1) * P].bitcast(U16)
            nc.vector.tensor_scalar(above, hi, self.T[:, x:x + 1], 65535.0, ALU.is_gt, ALU.mult).then_inc(self.step, 1)
            nc.vector.scalar_tensor_tensor(lo, hi, self.T[:, x:x + 1], lo, ALU.is_equal, ALU.mult).then_inc(self.step, 1)
            n += 2
            yield
            self.dve.wait_ge(self.step, n)
            nc.vector.tensor_tensor(lo, lo, above, ALU.max).then_inc(self.step, 1)
            n += 1
            yield
        yield from self.bisect(self.lo, 2.0 ** 15, self.TL, n, c)
        n += 33
        self.dve.wait_ge(self.step, n)
        for x, i in enumerate(self.tiles):
            wide = (i + 1) * P
            hi, lo, mask = self.hi[i][:, :], self.lo[i][:, :], self.hi[i][:, :].bitcast(BF16)
            level, not_above, place = (b[:, 0:wide].bitcast(dt) for b, dt in zip(self.junk, (BF16, BF16, I16)))
            T, TL, need = self.T[:, x:x + 1], self.TL[:, x:x + 1], self.need[:, x:x + 1]
            nc.vector.tensor_scalar(level, hi, T, None, ALU.is_equal).then_inc(self.step, 1)
            nc.vector.tensor_scalar(not_above, hi, T, OFF, ALU.is_le, ALU.mult).then_inc(self.step, 1)
            n += 2
            yield
            self.dve.wait_ge(self.step, n)
            nc.vector.scalar_tensor_tensor(level, lo, TL, level, ALU.is_equal, ALU.mult).then_inc(self.step, 1)
            nc.vector.scalar_tensor_tensor(not_above, lo, TL, not_above, ALU.is_le, ALU.mult).then_inc(self.step, 1)
            n += 2
            yield
            self.dve.wait_ge(self.step, n)
            nc.vector.tensor_scalar(lo, not_above, OFF / 2, None, ALU.is_lt, ALU.add, accum_out=need).then_inc(self.step, 1)
            nc.vector.tensor_tensor_scan(place, level, level, 0.0, ALU.add, ALU.max).then_inc(self.step, 1)
            n += 2
            yield
            self.dve.wait_ge(self.step, n)
            nc.vector.tensor_scalar(need, need, float(TOPK - wide), None, ALU.add).then_inc(self.step, 1)
            n += 1
            self.dve.wait_ge(self.step, n)
            nc.vector.scalar_tensor_tensor(level, place, need, level, ALU.is_le, ALU.mult).then_inc(self.step, 1)
            n += 1
            self.dve.wait_ge(self.step, n)
            nc.vector.scalar_tensor_tensor(mask, level, 0.0, not_above, ALU.is_equal, ALU.mult).then_inc(self.masks, 1)
            self.dve.wait_ge(self.masks, x + 1)
            yield

    def advance(self, dve, upto):
        self.dve = dve
        while self.done < min(upto, self.total):
            next(self.work, None)
            self.done += 1

    def load(self, sp):
        pass

    def scalar(self, act, b, k):
        pass

    def vector(self, dve, b, k, out_act, out_dve):
        if k < 3:
            return
        last = b == 1 and k == KC - 1
        self.advance(dve, self.found if last else min(self.done + self.pace, self.found))

    def between(self, dve, b):
        if b == 0:
            self.advance(dve, self.done + 2 * self.pace)


def turn_twice(nc, out, src, ident):
    nc.tensor.transpose(out[0:HD, :], src, ident[:, :])
    return nc.tensor.matmul(out[HD:P, :], src, ident[:, :], start=True, stop=True)


class IndexPrelude:

    def __init__(self, nc, env, g_dram):
        self.nc, self.env, self.g_dram = nc, env, g_dram
        small = Mem(nc, Map.SMALL + 2 * KB, nc.sbuf_usable_end - BASE)
        self.g = small.take("ixp_g", [P, HD], F32)
        self.ss = small.take("ixp_ss", [P, RT], F32)
        self.st = small.take("ixp_st", [P, 3, RT], F32)
        self.g_in, self.squared, self.sums, self.var, self.root, self.rstd, self.normed, self.irot, self.krot = (
            new_sem(nc, env, f"ixp_{n}") for n in ("g_in", "squared", "sums", "var", "root", "rstd", "normed", "irot", "krot"))

    def load(self, sp):
        sp.dma_start(self.g[:, :], spread(self.g_dram.rearrange("(a d) -> a d", a=1), [P, HD])).then_inc(self.g_in, 16)

    def between(self, dve, b):
        pass

    def scalar(self, act, b, k):
        if b == 2 and k == 5:
            act.wait_ge(self.var, 1)
            self.nc.scalar.activation(self.st[:, 1, :], self.st[:, 0, :], ACT.Sqrt).then_inc(self.root, 1)

    def vector(self, dve, b, k, out_act, out_dve):
        nc, Z = self.nc, self.env["Z"]
        ik = Z[:, :, OIK:OIK + HD]
        if (b, k) == (2, 3):
            dve.wait_ge(out_act, RT)
            dve.wait_ge(out_dve, RT)
            sq = Z[:, :, 4 * HD:5 * HD]
            nc.vector.tensor_tensor(sq, ik, ik, ALU.mult).then_inc(self.squared, 1)
            dve.wait_ge(self.squared, 1)
            nc.vector.tensor_reduce(self.ss[:, :], sq, AX.X, ALU.add).then_inc(self.sums, 1)
            dve.wait_ge(self.sums, 1)
            nc.vector.tensor_scalar(self.st[:, 0, :], self.ss[:, :], 1.0 / HD, EPS, ALU.mult, ALU.add).then_inc(self.var, 1)
        if (b, k) == (2, 4):
            rotate_all(nc, nc.vector, self.env, Z, OIQ, IH, lambda j: Z[:, :, j * HD:(j + 1) * HD], self.irot, 0)
        if (b, k) == (2, 6):
            dve.wait_ge(self.root, 1)
            inverse_root(nc, dve, self.st, self.rstd, 0)
            nc.vector.tensor_tensor(ik, ik, spread(self.st[:, 2, :].unsqueeze(2), [P, RT, HD]), ALU.mult).then_inc(self.normed, 1)
            dve.wait_ge(self.normed, 1)
            dve.wait_ge(self.g_in, 16)
            nc.vector.tensor_tensor(ik, ik, spread(self.g[:, :].unsqueeze(1), [P, RT, HD]), ALU.mult).then_inc(self.normed, 1)
            nc.vector.tensor_scalar(Z[:, :, OIW:OIW + IH], Z[:, :, OIW:OIW + IH], float(np.float32(IH ** -0.5)), None,
                                    ALU.mult).then_inc(self.normed, 1)
        if (b, k) == (2, 7):
            dve.wait_ge(self.normed, 3)
            rotate_all(nc, nc.vector, self.env, Z, OIK, 1,
                       lambda j: Z[:, :, 5 * HD + j * NF:5 * HD + (j + 1) * NF], self.krot, 0)


def indexer(nc, env, hi_keys, lo_keys):
    Z, ident = env["Z"], env["ident"]
    tiles = list(range(RT - 1, EASY - 1, -1))
    place = {i: x for x, i in enumerate(tiles)}
    with ExitStack() as ctx:
        def sem(n):
            return new_sem(nc, env, f"ix_{n}")

        mem = Mem(nc, Map.W, Map.W + 24 * KB)
        ikhi = mem.take("ix_ikhi", [P, SEQ], F32R)
        iklo = mem.take("ix_iklo", [P, SEQ], F32R)
        iqT = [mem.take("ix_iqT0", [P, IH, P], F32R)]
        iqT += [mem.take("ix_iqT1", [P, IH, P], F32R)]
        rel = mem.take("ix_rel", [P, 2, SEQ], F32)
        score = {i: Z[:, i, 0:(i + 1) * P] for i in tiles}
        flips = Z[:, 0, 0:SEQ].bitcast(I32)
        ktmp = Z[:, 1, 0:SEQ].rearrange("p (j r f) -> p j r f", j=4, r=RT)
        ps_x = [ctx.enter_context(nc.psum_tensor(f"ix_ps_x{i}", [P, 4, P], F32)) for i in range(2)]
        ps = [ctx.enter_context(nc.psum_tensor(f"ix_ps{i}", [P, SEQ], F32)) for i in range(3)]
        krot, turned, hi_done, lo_done, full, relu_done, acc_done, barred, flip, sorted_, upper, lower = map(sem, (
            "krot", "turned", "hi_done", "lo_done", "full", "relu_done", "acc_done", "barred", "flip",
            "sorted", "upper", "lower"))
        ik = Z[:, :, OIK:OIK + HD]
        turns = [("k", h) for h in range(2)] + [(i, h) for i in tiles for h in range(2)]
        units = [(i, head) for i in tiles for head in range(IH)]
        block = ctx.enter_context(nc.Block())

        def halves(i):
            return score[i].bitcast(I16).rearrange("p (n two) -> p n two", two=2)

        @block.gpsimd
        def _(pool):
            def keep_upper(i):
                pool.wait_ge(sorted_, place[i] + 1)
                nc.gpsimd.tensor_copy(hi_keys[i][:, :], halves(i)[:, :, 1]).then_inc(upper, 1)

            rotate_all(nc, nc.gpsimd, env, Z, OK_, C_KV, lambda j: ktmp[:, j, :, :], krot, 0)
            for i in tiles:
                keep_upper(i)

        @block.tensor
        def _(pe):
            def turn(m):
                i, h = turns[m]
                if m >= 2:
                    pe.wait_ge(lo_done, m - 1)
                for r in range(4):
                    src = ik[:, 4 * h + r, :] if i == "k" else Z[:, i, OIQ + (4 * h + r) * HD:OIQ + (4 * h + r + 1) * HD]
                    last = turn_twice(nc, ps_x[m % 2][:, r, :], src, ident)
                last.then_inc(turned, 1)

            for m in range(4):
                turn(m)
            for n, (i, head) in enumerate(units):
                if head % 4 == 0:
                    pe.wait_ge(lo_done, 3 + 2 * place[i] + head // 4)
                if n >= 3:
                    pe.wait_ge(relu_done, n - 2)
                for part in range(0, (i + 1) * P, NB):
                    k = slice(part, min((i + 1) * P, part + NB))
                    nc.tensor.matmul(ps[n % 3][:, k], iqT[i % 2][:, head, :], ikhi[:, k], start=True, stop=False)
                    last = nc.tensor.matmul(ps[n % 3][:, k], iqT[i % 2][:, head, :], iklo[:, k], start=False, stop=True)
                last.then_inc(full, 1)
                if head in (1, 5) and i > EASY:
                    turn(4 + 2 * place[i] + head // 4)

        @block.scalar
        def _(act):
            def hi(m):
                i, h = turns[m]
                act.wait_ge(turned, m + 1)
                if i == "k":
                    nc.scalar.activation(ikhi[:, h * NB:(h + 1) * NB], ps_x[m % 2][:, :, :].rearrange("p a b -> p (a b)"),
                                         ACT.Copy).then_inc(hi_done, 1)
                else:
                    if place[i] >= 2:
                        act.wait_ge(full, (place[i] - 1) * IH)
                    nc.scalar.activation(iqT[i % 2][:, 4 * h:4 * h + 4, :], ps_x[m % 2][:, :, :], ACT.Copy,
                                         scale=HD ** -0.5).then_inc(hi_done, 1)

            for m in range(4):
                hi(m)
            for n, (i, head) in enumerate(units):
                wide = (i + 1) * P
                act.wait_ge(full, n + 1)
                if n >= 2:
                    act.wait_ge(acc_done, n - 1)
                nc.scalar.activation(rel[:, n % 2, 0:wide], ps[n % 3][:, 0:wide], ACT.Relu).then_inc(relu_done, 1)
                if head in (1, 5) and i > EASY:
                    hi(4 + 2 * place[i] + head // 4)

        @block.vector
        def _(dve):
            def lo(m):
                i, h = turns[m]
                dve.wait_ge(hi_done, m + 1)
                if i == "k":
                    part = slice(h * NB, (h + 1) * NB)
                    nc.vector.tensor_tensor(iklo[:, part], ps_x[m % 2][:, :, :].rearrange("p a b -> p (a b)"),
                                            f32(ikhi[:, part]), ALU.subtract).then_inc(lo_done, 1)
                else:
                    to = iqT[i % 2][HD:P, 4 * h:4 * h + 4, :].rearrange("p a b -> p (a b)")
                    nc.vector.scalar_tensor_tensor(to, ps_x[m % 2][HD:P, :, :].rearrange("p a b -> p (a b)"), HD ** -0.5,
                                                   f32(to), ALU.mult, ALU.subtract).then_inc(lo_done, 1)

            for m in range(4):
                lo(m)
            for n, (i, head) in enumerate(units):
                to, r = score[i], rel[:, n % 2, 0:(i + 1) * P]
                w = Z[:, i, OIW + head:OIW + head + 1]
                dve.wait_ge(relu_done, n + 1)
                if head == 0:
                    nc.vector.tensor_scalar(to, r, w, 0.0, ALU.mult, ALU.add).then_inc(acc_done, 1)
                else:
                    dve.wait_ge(acc_done, n)
                    nc.vector.scalar_tensor_tensor(to, r, w, to, ALU.mult, ALU.add).then_inc(acc_done, 1)
                if head in (1, 5) and i > EASY:
                    lo(4 + 2 * place[i] + head // 4)
                if head == IH - 1:
                    dve.wait_ge(acc_done, n + 1)
                    nc.vector.memset(score[i][0:CHUNK, i * P + CHUNK:(i + 1) * P], BARRED).then_inc(barred, 1)
                    dve.wait_ge(barred, place[i] + 1)
                    s, flips_i = score[i].bitcast(I32), flips[:, 0:(i + 1) * P]
                    nc.vector.tensor_scalar(flips_i, s, 31, 1, ALU.arith_shift_right,
                                            ALU.logical_shift_right).then_inc(flip, 1)
                    dve.wait_ge(flip, place[i] + 1)
                    nc.vector.tensor_tensor(s, s, flips_i, ALU.bitwise_xor).then_inc(sorted_, 1)
                    dve.wait_ge(sorted_, place[i] + 1)
                    nc.vector.tensor_copy(lo_keys[i][:, :].bitcast(I16), halves(i)[:, :, 0]).then_inc(lower, 1)


def sparse_attention(nc, env, hi_keys, lo_keys, first, small):
    Z, ident = env["Z"], env["ident"]
    H = C_HEADS
    with ExitStack() as ctx:
        def sem(n):
            return new_sem(nc, env, f"sa_{n}")

        mem = Mem(nc, Map.T, Map.W + 24 * KB)
        kThi = mem.take("sa_kThi", [P, C_KV, SEQ], F32R)
        kTlo = mem.take("sa_kTlo", [P, C_KV, SEQ], F32R)
        easy = mem.take("sa_easy", [P, EASY, EASY * P], BF16)
        junk = [mem.take(f"sa_junk{x}", [P, SEQ], BF16) for x in range(3)]
        first.junk = junk
        second = Selection(nc, env, "sel1", GROUPS[1], hi_keys, lo_keys, small, junk)
        qfull = mem.take("sa_qfull", [P, 2, 4, P], F32)
        qT = mem.take("sa_qT", [P, 2, 4, P], F32R)
        prob = mem.take("sa_prob", [P, 3, SEQ], F32)
        probT = mem.take("sa_probT", [P, 2, RT, P], F32)
        twice = mem.take("sa_twice", [P, 2, 4, 2, HD], F32)
        rtmp = mem.take("sa_rtmp", [P, 2 * 4, H * NF], F32)
        nmax = mem.take("sa_nmax", [P, RT, H], F32)
        rsum = mem.take("sa_rsum", [P, RT, H], F32)
        ps_s = [ctx.enter_context(nc.psum_tensor(f"sa_ps_s{i}", [P, SEQ], F32)) for i in range(2)]
        ps_t = [ctx.enter_context(nc.psum_tensor(f"sa_ps_t{i}", [P, 4, P], F32)) for i in range(2)]
        ps_o = ctx.enter_context(nc.psum_tensor("sa_ps_o", [P, 8, HD], F32))
        ps_x = ctx.enter_context(nc.psum_tensor("sa_ps_x", [P, 4, P], F32))
        (k_turned, khi_done, klo_done, rotated, doubled, x_full, x_hi, x_free, q_lo, zeroed, mask_done,
         scored, max_done, exp_done, t_done, pT_done, mixed, inv_done, out_done) = map(sem, (
             "k_turned", "khi_done", "klo_done", "rotated", "doubled", "x_full", "x_hi", "x_free", "q_lo",
             "zeroed", "mask_done", "scored", "max_done", "exp_done", "t_done", "pT_done", "mixed", "inv_done",
             "out_done"))
        steps = [(i, h) for i in ORDER for h in range(H)]
        groups = [(i, g) for i in ORDER for g in range(H // 4)]
        kunits = [(k, h) for k in range(C_KV) for h in range(2)]
        kbanks = [ps_t[0][:, :, :], ps_t[1][:, :, :], ps_s[0][:, 0:NB].rearrange("p (a b) -> p a b", b=P),
                  ps_s[1][:, 0:NB].rearrange("p (a b) -> p a b", b=P)]
        turns = [(n, b) for n, (i, h) in enumerate(steps) for b in range(i // 4 + 1)]
        turns_at = {nb: m for m, nb in enumerate(turns)}
        block = ctx.enter_context(nc.Block())

        def parts(i):
            return (i * P + P + NB - 1) // NB

        def mask(i, keys):
            return easy[:, i, keys] if i < EASY else hi_keys[i][:, keys].bitcast(BF16)

        def last_turn(n):
            return turns_at[(n, steps[n][0] // 4)]

        def group_beside(n):
            return n // 4 + 1 if n % 4 == 1 and n // 4 + 1 < len(groups) else None

        @block.tensor
        def _(pe):
            def turn_queries(m):
                if m:
                    pe.wait_ge(x_free, m)
                pe.wait_ge(doubled, 2 * m + 2)
                for u in range(4):
                    last = nc.tensor.transpose(ps_x[:, u, :], twice[:, m % 2, u, :, :], ident[:, :])
                last.then_inc(x_full, 1)

            def logits(n):
                i, h = steps[n]
                if h % 4 == 0:
                    pe.wait_ge(q_lo, n // 4 + 1)
                if n >= 2:
                    pe.wait_ge(max_done, n - 1)
                for part in range(parts(i)):
                    keys = slice(part * NB, min((i + 1) * P, (part + 1) * NB))
                    bank = ps_s[n % 2][:, keys]
                    q = qT[:, n // 4 % 2, h % 4, :]
                    nc.tensor.matmul(bank, q, kThi[:, h // 4, keys], start=True, stop=False)
                    last = nc.tensor.matmul(bank, q, kTlo[:, h // 4, keys], start=False, stop=True)
                last.then_inc(scored, 1)

            def turn(n):
                i, h = steps[n]
                pe.wait_ge(exp_done, n + 1)
                for b in range(i // 4 + 1):
                    m = turns_at[(n, b)]
                    if m >= 2:
                        pe.wait_ge(pT_done, m - 1)
                    for j in range(4 * b, min(i + 1, 4 * b + 4)):
                        last = nc.tensor.transpose(ps_t[m % 2][:, j - 4 * b, :], prob[:, n % 3, j * P:(j + 1) * P], ident[:, :])
                    last.then_inc(t_done, 1)

            def mix(n):
                i, h = steps[n]
                pe.wait_ge(pT_done, last_turn(n) + 1)
                if n:
                    pe.wait_ge(out_done, n)
                for j in range(i + 1):
                    last = nc.tensor.matmul(ps_o[:, h % 8, :], probT[:, n % 2, j, :],
                                            Z[:, j, OV + h // 4 * HD:OV + (h // 4 + 1) * HD], start=(j == 0), stop=(j == i))
                last.then_inc(mixed, 1)

            for m, (k, half) in enumerate(kunits):
                if m >= 4:
                    pe.wait_ge(klo_done, m - 3)
                for r in range(4):
                    last = turn_twice(nc, kbanks[m % 4][:, r, :], Z[:, 4 * half + r, OK_ + k * HD:OK_ + (k + 1) * HD], ident)
                last.then_inc(k_turned, 1)
            turn_queries(0)
            pe.wait_ge(klo_done, len(kunits))
            for n in range(len(steps) + 3):
                if n < len(steps):
                    logits(n)
                if 0 <= n - 2 < len(steps):
                    turn(n - 2)
                if group_beside(n):
                    turn_queries(group_beside(n))
                if n - 3 >= 0:
                    mix(n - 3)

        @block.scalar
        def _(act):
            def empty(m):
                act.wait_ge(x_full, m + 1)
                if m >= 2:
                    act.wait_ge(q_lo, m - 1)
                    act.wait_ge(scored, 4 * (m - 1))
                nc.scalar.activation(qfull[:, m % 2, :, :], ps_x[:, :, :], ACT.Copy, scale=HD ** -0.5).then_inc(x_hi, 1)
                nc.scalar.activation(qT[:, m % 2, :, :], ps_x[:, :, :], ACT.Copy, scale=HD ** -0.5).then_inc(x_free, 1)

            def softmax(n):
                i, h = steps[n]
                act.wait_ge(max_done, n + 1)
                nc.scalar.activation(prob[:, n % 3, 0:(i + 1) * P], prob[:, n % 3, 0:(i + 1) * P], ACT.Exp, scale=-1.0,
                                     bias=nmax[:, i, h:h + 1], accum_out=rsum[:, i, h:h + 1]).then_inc(exp_done, 1)

            def keep_turned(n):
                i, h = steps[n]
                if n >= 2:
                    act.wait_ge(mixed, n - 1)
                for b in range(i // 4 + 1):
                    m = turns_at[(n, b)]
                    act.wait_ge(t_done, m + 1)
                    count = min(i + 1 - 4 * b, 4)
                    nc.scalar.activation(probT[:, n % 2, 4 * b:4 * b + count, :], ps_t[m % 2][:, 0:count, :],
                                         ACT.Copy).then_inc(pT_done, 1)

            def write(n):
                i, h = steps[n]
                act.wait_ge(mixed, n + 1)
                act.wait_ge(inv_done, n + 1)
                nc.scalar.activation(Z[:, i, OQ + h * HD:OQ + (h + 1) * HD], ps_o[:, h % 8, :], ACT.Copy,
                                     scale=rsum[:, i, h:h + 1]).then_inc(out_done, 1)

            for m, (k, half) in enumerate(kunits):
                act.wait_ge(k_turned, m + 1)
                nc.scalar.activation(kThi[:, k, half * NB:(half + 1) * NB].rearrange("p (a b) -> p a b", b=P), kbanks[m % 4],
                                     ACT.Copy).then_inc(khi_done, 1)
            empty(0)
            for n in range(len(steps) + 3):
                if 0 <= n - 2 < len(steps):
                    keep_turned(n - 2)
                if n < len(steps):
                    softmax(n)
                if group_beside(n):
                    empty(group_beside(n))
                if n - 3 >= 0:
                    write(n - 3)

        @block.gpsimd
        def _(pool):
            def double(m):
                i, g = groups[m]
                if m >= 2:
                    pool.wait_ge(x_full, m - 1)
                    pool.wait_ge(q_lo, m - 1)
                if g == 0:
                    rotate_queries(i)
                    pool.wait_ge(rotated, 6 * (ORDER.index(i) + 1))
                for c in range(2):
                    nc.gpsimd.tensor_copy(twice[:, m % 2, :, c, :], Z[:, i, OQ + 4 * g * HD:OQ + 4 * (g + 1) * HD]
                                          .rearrange("p (h d) -> p h d", d=HD)).then_inc(doubled, 1)

            def rotate_queries(i):
                rotate(nc, nc.gpsimd, env, Z, OQ, H,
                       rtmp[:, 4 * (ORDER.index(i) % 2):4 * (ORDER.index(i) % 2) + 4, :],
                       rotated, 6 * ORDER.index(i), [i])

            double(0)
            for m in range(len(groups)):
                if m + 1 < len(groups):
                    double(m + 1)
                pool.wait_ge(doubled, min(2 * m + 4, 2 * len(groups)))
                pool.wait_ge(x_hi, m + 1)
                pool.wait_ge(x_free, m + 1)
                to = qT[HD:P, m % 2, :, :]
                nc.gpsimd.tensor_tensor(to, qfull[HD:P, m % 2, :, :], f32(to), ALU.subtract).then_inc(q_lo, 1)

        @block.vector
        def _(dve):
            for i in range(EASY):
                nc.vector.memset(easy[:, i, :], 0.0).then_inc(zeroed, 1)
            dve.wait_ge(zeroed, EASY)
            for i in range(EASY):
                nc.vector.memset(easy[0:CHUNK, i, i * P + CHUNK:(i + 1) * P], OFF).then_inc(mask_done, 1)
            for m, (k, half) in enumerate(kunits):
                dve.wait_ge(khi_done, m + 1)
                part = slice(half * NB, (half + 1) * NB)
                nc.vector.tensor_tensor(kTlo[:, k, part].rearrange("p (a b) -> p a b", b=P), kbanks[m % 4],
                                        f32(kThi[:, k, part]).rearrange("p (a b) -> p a b", b=P), ALU.subtract).then_inc(klo_done, 1)
            plan = [(first, H - 2), (second, ORDER.index(GROUPS[1][0]) * H - 4)]
            weights = [i + 2 for i, _ in steps]
            was = first.done

            def select(n, part):
                start = 0
                for selection, end in plan:
                    if n >= start:
                        done = sum(weights[start:min(n, end)]) + (weights[n] * part / 2 if n < end else 0)
                        share = done / sum(weights[start:end])
                        base = was if selection is first else 0
                        selection.advance(dve, base + int(np.ceil(share * (selection.total - base))))
                    start = end

            for n in range(len(steps) + 1):
                if n < len(steps):
                    i, h = steps[n]
                    keys = slice(0, (i + 1) * P)
                    if n == 0:
                        dve.wait_ge(mask_done, EASY)
                    for group, part in zip(GROUPS, (first, second)):
                        if h == 0 and i in group:
                            dve.wait_ge(part.masks, group.index(i) + 1)
                    dve.wait_ge(scored, n + 1)
                    if n >= 3:
                        dve.wait_ge(t_done, last_turn(n - 3) + 1)
                    nc.vector.tensor_tensor_reduce(prob[:, n % 3, keys], ps_s[n % 2][:, keys], mask(i, keys), -1.0, 3e38,
                                                   ALU.add, ALU.min, nmax[:, i, h:h + 1]).then_inc(max_done, 1)
                if n < len(steps):
                    select(n, 1)
                if n >= 1:
                    i2, h2 = steps[n - 1]
                    dve.wait_ge(exp_done, n)
                    nc.vector.reciprocal(rsum[:, i2, h2:h2 + 1], rsum[:, i2, h2:h2 + 1]).then_inc(inv_done, 1)
                if n < len(steps):
                    select(n, 2)


def program(nc, t):
    mem = Mem(nc, Map.X, Map.Z)
    env = {"X": mem.take("X", [P, RT, D], F32), "sems": []}
    mem = Mem(nc, Map.Z, Map.T)
    env["Z"] = mem.take("Z", [P, RT, ZW], F32)
    mem = Mem(nc, Map.T, Map.W)
    env["Thi"] = mem.take("Thi", [P, KC, SEQ], F32R)
    env["Tlo"] = mem.take("Tlo", [P, KC, SEQ], F32R)
    mem = Mem(nc, Map.SMALL, nc.sbuf_usable_end - BASE)
    env["ident"] = mem.take("ident", [P, P], F32)
    env["cos"] = mem.take("cos", [P, RT, NF], F32)
    env["sin"] = mem.take("sin", [P, RT, NF], F32)
    constants(nc, env)
    ahead = ProjectWeights(nc, env, "in0", t["even_w_in"][0])
    norm_transpose(nc, env, "n0", t["norm_mix"][0], ahead, load_x=t["x"][0])
    project(nc, env, "in0", t["even_w_in"][0], EVEN_IN, env["Z"], ahead=ahead)
    rotary_tables(nc, env, t["positions"][0])
    mem = Mem(nc, Map.T, Map.SMALL)
    prelude = MlstmPrelude(nc, env, t, mem)
    after = mem.at - BASE
    window_attention(nc, env, t["even_sinks"][0], prelude, mem)
    mlstm(nc, env, prelude, Mem(nc, after, Map.SMALL))
    Z = env["Z"]
    ahead = ProjectWeights(nc, env, "out0", t["even_w_out"][0])
    norm_transpose(nc, env, "y0", None, ahead, src=lambda r, k: Z[:, r, k * P:(k + 1) * P] if k < 4
                   else Z[:, r, EBO + (k - 4) * P:EBO + (k - 3) * P])
    project(nc, env, "out0", t["even_w_out"][0], D, env["X"], add=True, ahead=ahead)
    ahead = MlpWeights(nc, env, "mlp0", t["w_up"][0], t["w_down"][0])
    norm_transpose(nc, env, "n1", t["norm_mlp"][0], ahead)
    mlp(nc, env, "mlp0", ahead)
    reset_semaphores(nc, env)
    cols = [(OIQ, INDEX_COLS // 2), (OIQ + INDEX_COLS // 2, INDEX_COLS // 2), (OK_, NB)]
    ahead = ProjectWeights(nc, env, "in1", t["odd_w_in"][0], cols[0][1], cols[0][0])
    norm_transpose(nc, env, "n2", t["norm_mix"][1], ahead)
    hi_keys, lo_keys = key_buffers(nc, env)
    Z = env["Z"] = Mem(nc, Map.Z, Map.T).take("Z_odd", [P, RT, ODD_IN], F32)
    project(nc, env, "in1", t["odd_w_in"][0], ODD_IN, Z, cols=cols, side=IndexPrelude(nc, env, t["odd_idx_k_norm"][0]),
            ahead=ahead)
    indexer(nc, env, hi_keys, lo_keys)
    small = Mem(nc, Map.SMALL + 3 * KB, nc.sbuf_usable_end - BASE)
    junk = [Z[:, r, NB:2 * NB].bitcast(BF16) for r in (1, 3, 5)]
    first = Selection(nc, env, "sel0", GROUPS[0], hi_keys, lo_keys, small, junk, pace=12)
    project(nc, env, "inq", t["odd_w_in"][0], ODD_IN, Z, cols=[(0, NB), (NB, NB)], side=first)
    sparse_attention(nc, env, hi_keys, lo_keys, first, small)
    ahead = ProjectWeights(nc, env, "out1", t["odd_w_out"][0])
    norm_transpose(nc, env, "y1", None, ahead, src=lambda r, k: Z[:, r, k * P:(k + 1) * P])
    project(nc, env, "out1", t["odd_w_out"][0], D, env["X"], add=True, ahead=ahead)
    ahead = MlpWeights(nc, env, "mlp1", t["w_up"][1], t["w_down"][1])
    norm_transpose(nc, env, "n3", t["norm_mlp"][1], ahead)
    mlp(nc, env, "mlp1", ahead)
    final_norm(nc, env, t["final_norm"], t["out"][0])


INPUTS = ["x", "positions", "norm_mix", "even_w_in", "even_sinks", "even_conv_w", "even_conv_b", "even_bias_i",
          "even_bias_f", "even_w_out", "odd_w_in", "odd_idx_k_norm", "odd_w_out", "norm_mlp", "w_up", "w_down",
          "final_norm"]


def kernel(**inputs):
    import numpy as _np
    import concourse.bacc as _bacc
    from concourse import mybir as _mybir
    from concourse.bass_utils import run_bass_kernel_spmd as _run

    nc = _bacc.Bacc("TRN2", target_bir_lowering=False, num_devices=1)
    arrays, t = {}, {}
    for name in INPUTS:
        a = _np.ascontiguousarray(inputs[name])
        arrays[f"in_{name}"] = a
        t[name] = nc.dram_tensor(f"in_{name}", a.shape, _mybir.dt.from_np(a.dtype), kind="ExternalInput").ap()
    t["out"] = nc.dram_tensor("out_y", (1, SEQ, D), _mybir.dt.float32, kind="ExternalOutput").ap()
    program(nc, t)
    r = _run(nc, [arrays], core_ids=[0])
    return r.results[0]["out_y"]
```
